# Optimizing a Trainium2 kernel written in Bass

```python
import math
import jax, jax.numpy as jnp
from jax import lax
import numpy as np

D_MODEL = 1024
BATCH = 1
SEQ = 1024
DEPTH = 2
DEC_BATCH = 8
DEC_SEQ = 8
PAST_LEN = 2048
PAGE_SIZE = 128

N_A_LAYERS = DEPTH // 2
N_B_LAYERS = DEPTH - N_A_LAYERS
A_HEADS = 8
A_DQK = D_MODEL // 16
A_DV = D_MODEL // A_HEADS
A_CHUNK = 64
A_F_BIAS_LO = 3.0
A_F_BIAS_HI = 6.0
B_HEADS = 8
B_D_NOPE = 128
B_D_ROPE = 64
B_D_V = 128
B_KV_RANK = D_MODEL // 4
B_Q_RANK = D_MODEL // 2
Q_BLOCK = 128
ROPE_THETA = 10000.0
ATTN_SCALE = (B_D_NOPE + B_D_ROPE) ** -0.5
N_EXPERTS = 16
N_GROUPS = 4
EXPERTS_PER_GROUP = N_EXPERTS // N_GROUPS
TOP_K = 2
D_EXPERT = D_MODEL // 2
MOE_BLOCK = 128
ALPHA = (2 * DEPTH) ** 0.25
BETA = (8 * DEPTH) ** -0.25
EPS = 1e-6

kernel_name = 'yoco_mlstm_mla_grouped_moe_decoder_step'

f32 = jnp.float32

def _layer_norm(x, g, b):
    x32 = x.astype(f32)
    mu = x32.mean(-1, keepdims=True)
    var = jnp.square(x32 - mu).mean(-1, keepdims=True)
    return ((x32 - mu) * lax.rsqrt(var + EPS) * g.astype(f32) + b.astype(f32)).astype(x.dtype)

def _rms_norm(x, g):
    x32 = x.astype(f32)
    return (x32 * lax.rsqrt(jnp.square(x32).mean(-1, keepdims=True) + EPS) * g.astype(f32)).astype(x.dtype)

def _rope(x, pos):
    half = x.shape[-1] // 2
    inv = jnp.power(ROPE_THETA, -jnp.arange(half, dtype=f32) / half)
    ang = pos.astype(f32)[:, None] * inv[None, :]
    cos = jnp.cos(ang)[None, :, None, :]
    sin = jnp.sin(ang)[None, :, None, :]
    x32 = x.astype(f32)
    x1, x2 = x32[..., :half], x32[..., half:]
    return jnp.concatenate([x1 * cos - x2 * sin, x1 * sin + x2 * cos], axis=-1).astype(x.dtype)

def _mlstm_chunkwise(q, k, v, log_i, log_f, C0, n0, m0, chunk):
    B, T = q.shape[:2]
    nc = T // chunk

    def blocks(a):
        a = a.astype(f32).reshape((B, nc, chunk) + a.shape[2:])
        return jnp.moveaxis(a, 1, 0)

    causal = jnp.tril(jnp.ones((chunk, chunk), bool))

    def step(carry, xs):
        C, n, m = carry
        qc, kc, vc, li, lf = xs
        b = jnp.cumsum(lf, axis=1)
        d = b[:, :, None, :] - b[:, None, :, :] + li[:, None, :, :]
        d = jnp.where(causal[None, :, :, None], d, -jnp.inf)
        a = b + m[:, None, :]
        m_t = jnp.maximum(a, d.max(axis=2))
        s = jnp.einsum('bthk,bshk->btsh', qc, kc) * jnp.exp(d - m_t[:, :, None, :])
        inter = jnp.exp(a - m_t)
        num = jnp.einsum('btsh,bshv->bthv', s, vc) + inter[..., None] * jnp.einsum('bthk,bhkv->bthv', qc, C)
        den = s.sum(axis=2) + inter * jnp.einsum('bthk,bhk->bth', qc, n)
        h = num / jnp.maximum(jnp.abs(den), jnp.exp(-m_t))[..., None]
        b_end = b[:, -1]
        g = b_end[:, None, :] - b + li
        m_new = jnp.maximum(b_end + m, g.max(axis=1))
        w = jnp.exp(g - m_new[:, None, :])
        decay = jnp.exp(b_end + m - m_new)
        C_new = decay[..., None, None] * C + jnp.einsum('bsh,bshk,bshv->bhkv', w, kc, vc)
        n_new = decay[..., None] * n + jnp.einsum('bsh,bshk->bhk', w, kc)
        return (C_new, n_new, m_new), h

    carry0 = (C0.astype(f32), n0.astype(f32), m0.astype(f32))
    xs = (blocks(q), blocks(k), blocks(v), blocks(log_i), blocks(log_f))
    (C, n, m), h = lax.scan(step, carry0, xs)
    h = jnp.moveaxis(h, 0, 1).reshape((B, T) + h.shape[3:])
    return h, C, n, m

def _mlstm_mixer(h, w_in, b_gates, norm_g, w_out, C0, n0, m0):
    B, T, _ = h.shape
    hqk, hv = A_HEADS * A_DQK, A_HEADS * A_DV
    q, k, v, o, gates = jnp.split(h @ w_in, [hqk, 2 * hqk, 2 * hqk + hv, 2 * hqk + 2 * hv], axis=-1)
    q = q.reshape(B, T, A_HEADS, A_DQK)
    k = k.reshape(B, T, A_HEADS, A_DQK) * (A_DQK ** -0.5)
    v = v.reshape(B, T, A_HEADS, A_DV)
    gates = gates.astype(f32) + b_gates.astype(f32)
    log_i = gates[..., :A_HEADS]
    log_f = jax.nn.log_sigmoid(gates[..., A_HEADS:])
    chunk = A_CHUNK if T % A_CHUNK == 0 else T
    hh, C, n, m = _mlstm_chunkwise(q, k, v, log_i, log_f, C0, n0, m0, chunk)
    mu = hh.mean(-1, keepdims=True)
    var = jnp.square(hh - mu).mean(-1, keepdims=True)
    hn = ((hh - mu) * lax.rsqrt(var + EPS)).reshape(B, T, hv) * norm_g.astype(f32)
    y = (hn.astype(h.dtype) * jax.nn.sigmoid(o)) @ w_out
    return y, C.astype(C0.dtype), n.astype(n0.dtype), m.astype(m0.dtype)

def _shared_kv(x_mid, pos, w_kv_a, kv_norm_g):
    kva = x_mid @ w_kv_a
    lat = _rms_norm(kva[..., :B_KV_RANK], kv_norm_g)
    kr = _rope(kva[..., B_KV_RANK:][:, :, None, :], pos)[:, :, 0, :]
    return lat, kr

def _attend_block(ql, qr, qp, kv_lat, kv_rope, k_pos):
    s = jnp.einsum('bthc,bsc->bhts', ql, kv_lat) + jnp.einsum('bthr,bsr->bhts', qr, kv_rope)
    s = s.astype(f32) * ATTN_SCALE
    s = jnp.where((k_pos[None, :] <= qp[:, None])[None, None], s, -jnp.inf)
    p = jax.nn.softmax(s, axis=-1)
    return jnp.einsum('bhts,bsc->bthc', p.astype(kv_lat.dtype), kv_lat)

def _attend(q_lat, q_rope, q_pos, kv_lat, kv_rope, k_pos):
    B, T = q_lat.shape[:2]
    if T % Q_BLOCK != 0:
        return _attend_block(q_lat, q_rope, q_pos, kv_lat, kv_rope, k_pos)
    nb = T // Q_BLOCK

    def split(a):
        return jnp.moveaxis(a.reshape((B, nb, Q_BLOCK) + a.shape[2:]), 1, 0)

    out = lax.map(lambda blk: _attend_block(blk[0], blk[1], blk[2], kv_lat, kv_rope, k_pos),
                  (split(q_lat), split(q_rope), q_pos.reshape(nb, Q_BLOCK)))
    return jnp.moveaxis(out, 0, 1).reshape((B, T) + out.shape[3:])

def _mla_mixer(h, pos, w_dq, q_norm_g, w_uq, w_o, w_uk, w_uv, kv_lat, kv_rope, k_pos):
    B, T, _ = h.shape
    cq = _rms_norm(h @ w_dq, q_norm_g)
    q = (cq @ w_uq).reshape(B, T, B_HEADS, B_D_NOPE + B_D_ROPE)
    q_nope, q_rope = q[..., :B_D_NOPE], _rope(q[..., B_D_NOPE:], pos)
    q_lat = jnp.einsum('bthn,chn->bthc', q_nope, w_uk)
    o_lat = _attend(q_lat, q_rope, pos, kv_lat, kv_rope, k_pos)
    o = jnp.einsum('bthc,chv->bthv', o_lat, w_uv).reshape(B, T, B_HEADS * B_D_V)
    return o @ w_o

def _moe(h, router_w, router_b, w_gate, w_up, w_down):
    B, T, D = h.shape
    N = B * T
    xf = h.reshape(N, D)
    scores = jax.nn.sigmoid((xf @ router_w).astype(f32))
    sel = (scores + router_b.astype(f32)).reshape(N, N_GROUPS, EXPERTS_PER_GROUP)
    group_score = lax.top_k(sel, 2)[0].sum(-1)
    grp = jnp.argmax(group_score, axis=-1)
    in_group = jnp.take_along_axis(sel, grp[:, None, None], axis=1)[:, 0]
    _, local = lax.top_k(in_group, TOP_K)
    expert = grp[:, None] * EXPERTS_PER_GROUP + local
    wts = jnp.take_along_axis(scores, expert, axis=1)
    wts = wts / wts.sum(-1, keepdims=True)
    NK = N * TOP_K
    flat_e = expert.reshape(NK)
    flat_t = jnp.repeat(jnp.arange(N, dtype=jnp.int32), TOP_K)
    flat_w = wts.reshape(NK)
    order = jnp.argsort(flat_e)
    se, st, sw = flat_e[order], flat_t[order], flat_w[order]
    counts = jnp.bincount(flat_e, length=N_EXPERTS)
    starts = jnp.cumsum(counts) - counts
    padded = (counts + MOE_BLOCK - 1) // MOE_BLOCK * MOE_BLOCK
    pends = jnp.cumsum(padded)
    pstarts = pends - padded
    dest = pstarts[se] + jnp.arange(NK) - starts[se]
    n_blocks = -(-NK // MOE_BLOCK) + N_EXPERTS
    P = n_blocks * MOE_BLOCK
    tok_pad = jnp.full((P,), N, jnp.int32).at[dest].set(st)
    w_pad = jnp.zeros((P,), f32).at[dest].set(sw)
    block_e = jnp.minimum(jnp.searchsorted(pends, jnp.arange(n_blocks) * MOE_BLOCK, side='right'), N_EXPERTS - 1)
    x_pad = jnp.concatenate([xf, jnp.zeros((1, D), xf.dtype)], axis=0)[tok_pad].reshape(n_blocks, MOE_BLOCK, D)

    def expert_block(args):
        xb, e = args
        hid = jax.nn.silu(xb @ w_gate[e]) * (xb @ w_up[e])
        return hid @ w_down[e]

    yb = lax.map(expert_block, (x_pad, block_e)).reshape(P, D)
    out = jnp.zeros((N + 1, D), yb.dtype).at[tok_pad].add(yb * w_pad[:, None].astype(yb.dtype))
    return out[:N].reshape(B, T, D).astype(h.dtype)

def setup_inputs(seed: int = 0) -> dict:
    key = jax.random.key(seed)
    ks = iter(jax.random.split(key, 48))

    def nrm(shape, scale):
        return jax.random.normal(next(ks), shape, f32) * scale

    n_pages = PAST_LEN // PAGE_SIZE
    n_pool = (DEC_BATCH * n_pages * 5) // 4
    page_table = jax.random.permutation(next(ks), n_pool)[:DEC_BATCH * n_pages].reshape(DEC_BATCH, n_pages).astype(jnp.int32)
    hqk, hv = A_HEADS * A_DQK, A_HEADS * A_DV
    a_in = 2 * hqk + 2 * hv + 2 * A_HEADS
    b_i = nrm((N_A_LAYERS, A_HEADS), 0.1)
    b_f = jnp.linspace(A_F_BIAS_LO, A_F_BIAS_HI, A_HEADS)[None, :] + nrm((N_A_LAYERS, A_HEADS), 0.1)
    return {
        'x_prompt': nrm((BATCH, SEQ, D_MODEL), 1.0),
        'x_sample': nrm((DEC_BATCH, DEC_SEQ, D_MODEL), 1.0),
        'cache_latent': nrm((n_pool, PAGE_SIZE, B_KV_RANK), 1.0),
        'cache_krope': nrm((n_pool, PAGE_SIZE, B_D_ROPE), 1.0),
        'page_table': page_table,
        'state_C': nrm((N_A_LAYERS, DEC_BATCH, A_HEADS, A_DQK, A_DV), 0.3),
        'state_n': nrm((N_A_LAYERS, DEC_BATCH, A_HEADS, A_DQK), 0.3),
        'state_m': nrm((N_A_LAYERS, DEC_BATCH, A_HEADS), 1.0),
        'c_prompt': nrm((BATCH, D_MODEL), 1.0),
        'c_sample': nrm((DEC_BATCH, D_MODEL), 1.0),
        'ada_w': nrm((DEPTH, D_MODEL, 6 * D_MODEL), 0.5 * D_MODEL ** -0.5),
        'ada_b': nrm((DEPTH, 6 * D_MODEL), 0.02),
        'ln_g': 1.0 + nrm((DEPTH, 2, D_MODEL), 0.02),
        'ln_b': nrm((DEPTH, 2, D_MODEL), 0.02),
        'a_w_in': nrm((N_A_LAYERS, D_MODEL, a_in), D_MODEL ** -0.5),
        'a_b_gates': jnp.concatenate([b_i, b_f], axis=-1),
        'a_norm_g': 1.0 + nrm((N_A_LAYERS, hv), 0.02),
        'a_w_out': nrm((N_A_LAYERS, hv, D_MODEL), BETA * hv ** -0.5),
        'b_w_kv_a': nrm((D_MODEL, B_KV_RANK + B_D_ROPE), D_MODEL ** -0.5),
        'b_kv_norm_g': 1.0 + nrm((B_KV_RANK,), 0.02),
        'b_w_uk': nrm((B_KV_RANK, B_HEADS, B_D_NOPE), B_KV_RANK ** -0.5),
        'b_w_uv': nrm((B_KV_RANK, B_HEADS, B_D_V), B_KV_RANK ** -0.5),
        'b_w_dq': nrm((N_B_LAYERS, D_MODEL, B_Q_RANK), D_MODEL ** -0.5),
        'b_q_norm_g': 1.0 + nrm((N_B_LAYERS, B_Q_RANK), 0.02),
        'b_w_uq': nrm((N_B_LAYERS, B_Q_RANK, B_HEADS * (B_D_NOPE + B_D_ROPE)), B_Q_RANK ** -0.5),
        'b_w_o': nrm((N_B_LAYERS, B_HEADS * B_D_V, D_MODEL), BETA * (B_HEADS * B_D_V) ** -0.5),
        'router_w': nrm((D_MODEL, N_EXPERTS), D_MODEL ** -0.5),
        'router_b': nrm((N_EXPERTS,), 0.01),
        'e_w_gate': nrm((DEPTH, N_EXPERTS, D_MODEL, D_EXPERT), D_MODEL ** -0.5),
        'e_w_up': nrm((DEPTH, N_EXPERTS, D_MODEL, D_EXPERT), D_MODEL ** -0.5),
        'e_w_down': nrm((DEPTH, N_EXPERTS, D_EXPERT, D_MODEL), BETA * D_EXPERT ** -0.5),
    }

def reference(x_prompt, x_sample, cache_latent, cache_krope, page_table, state_C, state_n, state_m,
              c_prompt, c_sample, ada_w, ada_b, ln_g, ln_b, a_w_in, a_b_gates, a_norm_g, a_w_out,
              b_w_kv_a, b_kv_norm_g, b_w_uk, b_w_uv, b_w_dq, b_q_norm_g, b_w_uq, b_w_o,
              router_w, router_b, e_w_gate, e_w_up, e_w_down):

    def trunk(x, c, pos, C0, n0, m0, past_lat, past_kr, past_pos):
        mods = jnp.einsum('bd,lde->lbe', jax.nn.silu(c), ada_w) + ada_b[:, None, :]
        new_C, new_n, new_m = [], [], []
        kv_lat = kv_rope = k_pos = lat_rows = rope_rows = None
        for l in range(DEPTH):
            shift1, scale1, gate1, shift2, scale2, gate2 = jnp.split(mods[l][:, None, :], 6, axis=-1)
            h = x * (1 + scale1) + shift1
            if l < N_A_LAYERS:
                y, Cl, nl, ml = _mlstm_mixer(h, a_w_in[l], a_b_gates[l], a_norm_g[l], a_w_out[l], C0[l], n0[l], m0[l])
                new_C.append(Cl)
                new_n.append(nl)
                new_m.append(ml)
            else:
                j = l - N_A_LAYERS
                y = _mla_mixer(h, pos, b_w_dq[j], b_q_norm_g[j], b_w_uq[j], b_w_o[j], b_w_uk, b_w_uv,
                               kv_lat, kv_rope, k_pos)
            x = _layer_norm(ALPHA * x + gate1 * y, ln_g[l, 0], ln_b[l, 0])
            h = x * (1 + scale2) + shift2
            y = _moe(h, router_w, router_b, e_w_gate[l], e_w_up[l], e_w_down[l])
            x = _layer_norm(ALPHA * x + gate2 * y, ln_g[l, 1], ln_b[l, 1])
            if l == N_A_LAYERS - 1:
                lat_rows, rope_rows = _shared_kv(x, pos, b_w_kv_a, b_kv_norm_g)
                kv_lat = jnp.concatenate([past_lat, lat_rows], axis=1)
                kv_rope = jnp.concatenate([past_kr, rope_rows], axis=1)
                k_pos = jnp.concatenate([past_pos, pos])
        return x, jnp.stack(new_C), jnp.stack(new_n), jnp.stack(new_m), lat_rows, rope_rows

    Bp, Tp = x_prompt.shape[:2]
    dt = x_prompt.dtype
    y_prompt, C_p, n_p, m_p, lat_p, krope_p = trunk(
        x_prompt, c_prompt, jnp.arange(Tp, dtype=jnp.int32),
        jnp.zeros((N_A_LAYERS, Bp, A_HEADS, A_DQK, A_DV), dt),
        jnp.zeros((N_A_LAYERS, Bp, A_HEADS, A_DQK), dt),
        jnp.zeros((N_A_LAYERS, Bp, A_HEADS), dt),
        jnp.zeros((Bp, 0, B_KV_RANK), dt), jnp.zeros((Bp, 0, B_D_ROPE), dt), jnp.zeros((0,), jnp.int32))

    Bs, Ts = x_sample.shape[:2]
    n_pages = page_table.shape[1]
    past_len = n_pages * PAGE_SIZE
    past_lat = cache_latent[page_table].reshape(Bs, past_len, B_KV_RANK)
    past_kr = cache_krope[page_table].reshape(Bs, past_len, B_D_ROPE)
    y_sample, C_s, n_s, m_s, lat_s, krope_s = trunk(
        x_sample, c_sample, past_len + jnp.arange(Ts, dtype=jnp.int32),
        state_C, state_n, state_m, past_lat, past_kr, jnp.arange(past_len, dtype=jnp.int32))

    return (y_prompt, y_sample, C_p, n_p, m_p, lat_p, krope_p, C_s, n_s, m_s, lat_s, krope_s)


_drawn_inputs = setup_inputs


def setup_inputs(seed=0):
    import zlib

    import numpy as np

    out = dict(_drawn_inputs(seed))
    spreads = {}
    factors = {'cache_latent': 8.0,
     'cache_krope': 8.0,
     'a_norm_g': 8.0,
     'b_kv_norm_g': 2.906,
     'b_w_uk': 4.861,
     'b_w_uv': 3.419,
     'b_w_dq': 4.26,
     'b_q_norm_g': 8.0,
     'b_w_uq': 4.364,
     'b_w_o': 3.431,
     'router_b': 2.967}
    for name, (base, spread) in spreads.items():
        noise = np.random.default_rng([zlib.crc32(name.encode()), seed]).standard_normal(out[name].shape)
        drawn = base * np.exp(spread * noise) if base else spread * noise
        out[name] = __import__('jax').numpy.asarray(drawn.astype(out[name].dtype))
    for name, factor in factors.items():
        out[name] = (out[name] * factor).astype(out[name].dtype)
    return out
```

```python
from contextlib import ExitStack

import numpy as np

import concourse.bass as bass
from concourse import mybir

F32 = mybir.dt.float32
I32 = mybir.dt.int32
ALU = mybir.AluOpType
ACT = mybir.ActivationFunctionType
AX = mybir.AxisListType.X

P = 128
D = 1024
KD = D // P
HALF = 512
SEQ = 1024
BATCHES, STEPS = 8, 8
NSAMP = BATCHES * STEPS
N = SEQ + NSAMP
PT = SEQ // P
TILES = PT + 1
H = 8
DK = 64
DV = 128
AUG = DV + 1
PAIRS = H // 2
A_IN = 3072
GATES = 2 * H
KVR, ROPE, QR = 256, 64, 512
NOPE = 128
PAST, PAGE = 2048, 128
PAGES = PAST // PAGE
CTX = PAST + STEPS
KVW = 2 * PAGE + PAGE + KVR
E, GROUPS, PER = 16, 4, 4
FE = 512
FT = FE // P
SLOTS = (2 * N + E * (P - 1)) // P
ALPHA = 4.0 ** 0.25
EPS = 1e-6
SCALE = float(NOPE + ROPE) ** -0.5
NEG = -1.0e30
SHIFT1, SCALE1, GATE1, SHIFT2, SCALE2, GATE2 = range(6)


class Shared:
    pass


def rows_of(t):
    return NSAMP if t is TILES - 1 else P


def load_mods(eng, g, dst, layer, which, sample, sem):
    at = (layer * 6 + which) * D
    if not sample:
        eng.dma_start(dst[:, :], g.mods[0:1, at:at + D].broadcast_to([P, D])).then_inc(sem, 16)
    else:
        for b in range(BATCHES):
            src = g.mods[1 + b:2 + b, at:at + D].broadcast_to([STEPS, D])
            eng.dma_start(dst[b * STEPS:(b + 1) * STEPS, :], src).then_inc(sem, 16)


def stage_ada(nc, g):
    CH = 2 * 6 * D // HALF
    RING = 3
    with nc.cleanup_on_exit(), ExitStack() as ctx:
        def sb(n, s, d=F32):
            return ctx.enter_context(nc.sbuf_tensor(n, s, d))

        def sem(n):
            return nc.alloc_semaphore(f"ada_{n}")

        w = sb("ada_w_ring", [P, RING, KD * HALF])
        bias = sb("ada_bias_ring", [9, RING, HALF])
        out = sb("ada_out", [9, RING, HALF])
        c = sb("ada_c", [P, KD * 9])
        ex = sb("ada_exp", [P, KD * 9])
        sc = sb("ada_silu", [P, KD * 9])
        ps = ctx.enter_context(nc.psum_tensor("ada_ps", [P, RING, HALF], F32))
        s_c, s_exp, s_silu = sem("c_loaded"), sem("c_exp"), sem("silu_ready")
        s_w = [sem(f"w_loaded{i}") for i in range(RING)]
        s_mm, s_ev = sem("chunk_summed"), sem("chunk_out")
        s_st = [sem(f"mods_stored{i}") for i in range(RING)]
        block = ctx.enter_context(nc.Block())

        @block.sync
        def _(sp):
            sp.dma_start(c[:], g.cT).then_inc(s_c, 16)
            with sp.Fori(0, CH // RING) as i:
                for r in range(RING):
                    j = i * RING + r
                    sp.wait_ge(s_mm, j + 1)
                    sp.dma_start(w[:, r, :], g.ada_w[bass.ds(j, 1)].rearrange("o p n -> (o p) n")).then_inc(s_w[r], 16)
                    sp.wait_ge(s_ev, j + 1)
                    sp.dma_start(bias[:, r, :], g.ada_b[bass.ds(j, 1)].broadcast_to([9, HALF])).then_inc(s_w[r], 16)

        @block.scalar
        def _(act):
            for k in range(KD):
                act.dma_start(g.w_in[:, k, :], g.a_w_in[k * P:(k + 1) * P, :]).then_inc(g.s_w_in, 16)
            act.dma_start(g.x[:, 0:PT, :], g.x_prompt.rearrange("(t p) d -> p t d", p=P)).then_inc(g.s_x, 16)
            act.dma_start(g.x[0:NSAMP, PT, :], g.x_sample).then_inc(g.s_x, 16)
            act.wait_ge(s_c, 16)
            nc.scalar.activation(ex[:], c[:], ACT.Exp, scale=-1.0).then_inc(s_exp, 1)
            with act.Fori(0, CH // RING) as i:
                for r in range(RING):
                    j = i * RING + r
                    act.wait_ge(s_ev, j + 1 + RING)
                    act.dma_start(g.mods[:, bass.ds(j * HALF, HALF)], out[:, r, :]).then_inc(s_st[r], 16)
            for r in range(RING):
                act.wait_ge(s_st[r], 16 * (CH // RING) + 16)

        @block.vector
        def _(v):
            v.wait_ge(s_exp, 1)
            nc.vector.tensor_scalar(ex[:], ex[:], 1.0, None, ALU.add)
            v.drain()
            nc.vector.reciprocal(ex[:], ex[:])
            v.drain()
            nc.vector.tensor_tensor(sc[:], c[:], ex[:], ALU.mult).then_inc(s_silu, 1)
            v.sem_inc(s_ev, RING)
            for r in range(RING):
                v.sem_inc(s_st[r], 16)
            with v.Fori(0, CH // RING) as i:
                for r in range(RING):
                    j = i * RING + r
                    v.wait_ge(s_mm, j + 1 + RING)
                    v.wait_ge(s_w[r], 32 * i + 32)
                    v.wait_ge(s_st[r], 16 * i + 16)
                    nc.vector.tensor_tensor(out[:, r, :], ps[0:9, r, :], bias[:, r, :], ALU.add).then_inc(s_ev, 1)

        @block.tensor
        def _(pe):
            pe.sem_inc(s_mm, RING)
            pe.wait_ge(s_silu, 1)
            with pe.Fori(0, CH // RING) as i:
                for r in range(RING):
                    j = i * RING + r
                    pe.wait_ge(s_w[r], 32 * i + 32)
                    pe.wait_ge(s_ev, j + 1)
                    for k in range(KD):
                        mm = nc.tensor.matmul(ps[0:9, r, :], sc[:, k * 9:(k + 1) * 9],
                                              w[:, r, k * HALF:(k + 1) * HALF], start=(k == 0), stop=(k == KD - 1))
                    mm.then_inc(s_mm, 1)


def stage_in_proj(nc, g):
    OUTS = A_IN // HALF
    with nc.cleanup_on_exit(), ExitStack() as ctx:
        def sb(n, s, d=F32):
            return ctx.enter_context(nc.sbuf_tensor(n, s, d))

        def sem(n):
            return nc.alloc_semaphore(f"in_{n}")

        shift = sb("in_shift", [P, D])
        scale = sb("in_scale", [P, D])
        h = sb("in_h", [P, D])
        hT = sb("in_hT", [P, 2, KD, P])
        out = sb("in_out", [P, 2, A_IN])
        psT = ctx.enter_context(nc.psum_tensor("in_psT", [P, KD, P], F32))
        ps = ctx.enter_context(nc.psum_tensor("in_ps", [P, OUTS, HALF], F32))
        s_mods, s_modfree = sem("mods_loaded"), sem("mods_used")
        s_h, s_T, s_hT, s_mm, s_ev = sem("h_ready"), sem("h_turned"), sem("hT_ready"), sem("chunk_summed"), sem("chunk_out")
        s_st = [sem("qkvo_stored0"), sem("qkvo_stored1")]
        block = ctx.enter_context(nc.Block())

        @block.sync
        def _(sp):
            load_mods(sp, g, shift, 0, SHIFT1, False, s_mods)
            load_mods(sp, g, scale, 0, SCALE1, False, s_mods)

            def store(t, par, i, n):
                for c in range(2):
                    sp.wait_ge(s_ev, 7 * t + 3 * c + 3 + 7)
                    sp.dma_start(g.qkvo[bass.ds(t * P, n), c * 1536:(c + 1) * 1536],
                                 out[0:n, par, c * 1536:(c + 1) * 1536]).then_inc(s_st[par], 16)

            with sp.Fori(0, PT // 2) as i:
                for par in range(2):
                    store(i * 2 + par, par, i, P)
            sp.wait_ge(s_modfree, PT)
            load_mods(sp, g, shift, 0, SHIFT1, True, s_mods)
            load_mods(sp, g, scale, 0, SCALE1, True, s_mods)
            store(PT, 0, PT // 2, NSAMP)
            sp.wait_ge(s_st[0], 32 * (PT // 2 + 1) + 32)
            sp.wait_ge(s_st[1], 32 * (PT // 2) + 32)

        @block.vector
        def _(v):
            nc.vector.memset(g.gates[:], 0.0)
            v.wait_ge(g.s_x, 32)

            def tile(t, n, mods):
                v.wait_ge(s_mods, mods)
                v.wait_ge(s_T, t + 1)
                x = g.x[0:n, bass.ds(t, 1), :].rearrange("p o d -> p (o d)")
                nc.vector.scalar_tensor_tensor(out=h[0:n, :], in0=scale[0:n, :], scalar=1.0, in1=x,
                                               op0=ALU.add, op1=ALU.mult)
                v.drain()
                nc.vector.tensor_tensor(h[0:n, :], h[0:n, :], shift[0:n, :], ALU.add)
                v.drain()
                v.sem_inc(s_h, 1)
                v.sem_inc(s_modfree, 1)

            with v.Fori(0, PT) as t:
                tile(t, P, 32)
            tile(PT, NSAMP, 32 + 2 * 16 * BATCHES)

        @block.tensor
        def _(pe):
            pe.sem_inc(s_T, 1)
            pe.wait_ge(g.s_w_in, 16 * KD)

            def tile(t, par, n):
                pe.wait_ge(s_h, t + 1)
                pe.wait_ge(s_hT, t + 1)
                for k in range(KD):
                    mm = nc.tensor.transpose(psT[:, k, 0:n], h[0:n, k * P:(k + 1) * P], g.ident[0:n, 0:n])
                mm.then_inc(s_T, 1)
                pe.wait_ge(s_hT, t + 2)
                for c in range(OUTS):
                    if c == 0:
                        pe.wait_ge(s_ev, 7 * t + 7)
                    else:
                        pe.wait_ge(s_ev, 7 * t + c + 1)
                    for k in range(KD):
                        mm = nc.tensor.matmul(ps[0:n, c, :], hT[:, par, k, 0:n], g.w_in[:, k, c * HALF:(c + 1) * HALF],
                                              start=(k == 0), stop=(k == KD - 1))
                    mm.then_inc(s_mm, 1)
                pe.wait_ge(s_ev, 7 * t + 1 + 7)
                for k in range(KD):
                    mm = nc.tensor.matmul(ps[0:n, 0, 0:GATES], hT[:, par, k, 0:n], g.w_in[:, k, A_IN:A_IN + GATES],
                                          start=(k == 0), stop=(k == KD - 1))
                mm.then_inc(s_mm, 1)

            with pe.Fori(0, PT // 2) as i:
                for par in range(2):
                    tile(i * 2 + par, par, P)
            tile(PT, 0, NSAMP)

        @block.scalar
        def _(act):
            act.sem_inc(s_hT, 1)
            act.sem_inc(s_ev, 7)
            act.sem_inc(s_st[0], 32)
            act.sem_inc(s_st[1], 32)

            def turn(t, par, n):
                act.wait_ge(s_T, t + 2)
                for z in range(2):
                    cp = nc.scalar.copy(hT[:, par, z * 4:z * 4 + 4, 0:n], psT[:, z * 4:z * 4 + 4, 0:n])
                act.drain()
                act.sem_inc(s_hT, 1)

            def tile(t, par, i, n):
                turn(t, par, n)
                act.wait_ge(s_st[par], 32 * i + 32)
                for c in range(OUTS):
                    act.wait_ge(s_mm, 7 * t + c + 1)
                    nc.scalar.copy(out[0:n, par, c * HALF:(c + 1) * HALF], ps[0:n, c, :]).then_inc(s_ev, 1)
                act.wait_ge(s_mm, 7 * t + 7)
                nc.scalar.copy(g.gates[0:n, bass.ds(t, 1), :].rearrange("p o d -> p (o d)"),
                               ps[0:n, 0, 0:GATES]).then_inc(s_ev, 1)

            with act.Fori(0, PT // 2) as i:
                for par in range(2):
                    tile(i * 2 + par, par, i, P)
            tile(PT, 0, PT // 2, NSAMP)


def stage_gates(nc, g):
    with nc.cleanup_on_exit(), ExitStack() as ctx:
        def sb(n, s, d=F32):
            return ctx.enter_context(nc.sbuf_tensor(n, s, d))

        def sem(n):
            return nc.alloc_semaphore(f"g_{n}")

        bg = sb("g_bias", [P, GATES])
        mn = sb("g_min", [P, TILES, H])
        ab = sb("g_abs", [P, TILES, H])
        lf = sb("g_logf", [P, TILES, H])
        btok = sb("g_btok", [P, TILES, H])
        bh = sb("g_bh", [H, N])
        uh = sb("g_uh", [H, N])
        ca = sb("g_ca", [H, N])
        cb = sb("g_cb", [H, N])
        e3 = sb("g_e3", [H, 3, N])
        mend = sb("g_mend", [H, 2 * BATCHES])
        bend = sb("g_bend", [H, 2 * BATCHES])
        dec = sb("g_dec", [H, 2 * BATCHES])
        decd = sb("g_decd", [H, H, 2 * BATCHES])
        mprev = sb("g_mprev", [H, 2 * BATCHES])
        mout = sb("g_mout", [H, 1 + BATCHES])
        psb = ctx.enter_context(nc.psum_tensor("g_psb", [P, HALF], F32))
        psh = ctx.enter_context(nc.psum_tensor("g_psh", [P, 6, HALF], F32))
        s_ld, s_ab, s_e, s_ln, s_lf, s_b, s_u, s_t = (sem(x) for x in (
            "loaded", "abs_ready", "exp_ready", "ln_ready", "logf_ready", "b_summed", "u_ready", "turned_in"))
        s_args, s_exps, s_dd, s_back, s_st, s_gates = (sem(x) for x in (
            "exp_args", "exps_ready", "decay_diag", "turned_back", "m_stored", "gates_out"))
        block = ctx.enter_context(nc.Block())
        CP, CS = P, STEPS
        NC = PT + BATCHES

        def chunks(a):
            return (a[:, 0:SEQ].rearrange("h (c t) -> h c t", t=CP), a[:, SEQ:N].rearrange("h (c t) -> h c t", t=CS))

        @block.sync
        def _(sp):
            sp.dma_start(bg[:], g.a_b_gates.broadcast_to([P, GATES])).then_inc(s_ld, 16)
            sp.dma_start(mprev[:, PT:NC], g.state_mT).then_inc(s_ld, 16)
            sp.wait_ge(s_args, 1)
            sp.dma_start(g.m_out, mout[:]).then_inc(s_st, 16)
            sp.wait_ge(s_st, 16)

        @block.vector
        def _(v):
            V = nc.vector
            v.wait_ge(s_ld, 32)
            V.tensor_tensor(g.gates[:], g.gates[:], bg[:].unsqueeze(1).broadcast_to([P, TILES, GATES]), ALU.add)
            v.drain()
            xf = g.gates[:, :, H:GATES]
            V.tensor_scalar(mn[:], xf, 0.0, None, ALU.min)
            V.tensor_scalar(ab[:], xf, 0.0, None, ALU.max)
            v.drain()
            V.tensor_tensor(ab[:], mn[:], ab[:], ALU.subtract)
            v.drain()
            v.sem_inc(s_ab, 1)
            v.wait_ge(s_e, 1)
            V.tensor_scalar(ab[:], ab[:], 1.0, None, ALU.add)
            v.drain()
            v.sem_inc(s_ab, 1)
            v.wait_ge(s_ln, 1)
            V.tensor_tensor(lf[:], mn[:], ab[:], ALU.subtract)
            v.drain()
            v.sem_inc(s_lf, 1)
            v.wait_ge(s_b, 1)
            V.tensor_copy(btok[:, 0:PT, :], psb[:, 0:PT * H].rearrange("p (t h) -> p t h", h=H))
            V.memset(btok[:, PT, :], 0.0)
            v.drain()
            V.tensor_copy(btok[0:NSAMP, PT, :], psb[0:NSAMP, 128:128 + H])
            v.drain()
            V.tensor_tensor(g.u[:], g.gates[:, :, 0:H], btok[:], ALU.subtract)
            v.drain()
            v.sem_inc(s_u, 1)
            v.wait_ge(s_t, 1)
            V.tensor_copy(uh[:, 0:SEQ], psh[0:H, 0:2, :])
            V.tensor_copy(uh[:, SEQ:N], psh[0:H, 4, 0:NSAMP])
            V.tensor_copy(bh[:, 0:SEQ], psh[0:H, 2:4, :])
            V.tensor_copy(bh[:, SEQ:N], psh[0:H, 4, NSAMP:2 * NSAMP])
            v.drain()
            V.tensor_copy(ca[:], uh[:])
            v.drain()
            src, dst = ca, cb
            k = 1
            while k < CP:
                for part, n in zip(range(2), (CP, CS)):
                    s, d = chunks(src)[part], chunks(dst)[part]
                    if k < n:
                        V.tensor_tensor(d[:, :, k:n], s[:, :, k:n], s[:, :, 0:n - k], ALU.max)
                        V.tensor_copy(d[:, :, 0:k], s[:, :, 0:k])
                    else:
                        V.tensor_copy(d, s)
                v.drain()
                src, dst = dst, src
                k *= 2
            cm, tmp = src, dst
            for part, (lo, n) in enumerate(((0, CP), (PT, CS))):
                V.tensor_copy(mend[:, lo:lo + PT], chunks(cm)[part][:, :, n - 1])
                V.tensor_copy(bend[:, lo:lo + PT], chunks(bh)[part][:, :, n - 1])
            V.memset(mprev[:, 0:1], 0.0)
            v.drain()
            for c in range(PT):
                V.tensor_tensor(mend[:, c:c + 1], mend[:, c:c + 1], mprev[:, c:c + 1], ALU.max)
                v.drain()
                nxt = mprev[:, c + 1:c + 2] if c + 1 < PT else mout[:, 0:1]
                V.tensor_tensor(nxt, mend[:, c:c + 1], bend[:, c:c + 1], ALU.add)
                v.drain()
            V.tensor_tensor(mend[:, PT:NC], mend[:, PT:NC], mprev[:, PT:NC], ALU.max)
            v.drain()
            V.tensor_tensor(mout[:, 1:1 + BATCHES], mend[:, PT:NC], bend[:, PT:NC], ALU.add)
            for part, (lo, n) in enumerate(((0, CP), (PT, CS))):
                mp = mprev[:, lo:lo + PT].unsqueeze(2).broadcast_to([H, PT, n])
                me = mend[:, lo:lo + PT].unsqueeze(2).broadcast_to([H, PT, n])
                M = chunks(g.M)[part]
                V.tensor_tensor(M, chunks(cm)[part], mp, ALU.max)
                v.drain()
                V.tensor_tensor(chunks(e3[:, 0, :])[part], mp, M, ALU.subtract)
                V.tensor_tensor(chunks(tmp)[part], chunks(bh)[part], M, ALU.add)
                V.tensor_tensor(chunks(e3[:, 2, :])[part], chunks(uh)[part], me, ALU.subtract)
            v.drain()
            V.tensor_scalar(e3[:, 1, :], tmp[:], -1.0, None, ALU.mult)
            V.tensor_tensor(dec[:], mprev[:], mend[:], ALU.subtract)
            v.drain()
            v.sem_inc(s_args, 1)
            v.wait_ge(s_exps, 1)
            V.tensor_tensor(decd[:], g.ident[0:H, 0:H].unsqueeze(2).broadcast_to([H, H, NC]),
                            dec[:].unsqueeze(1).broadcast_to([H, H, NC]), ALU.mult)
            v.drain()
            v.sem_inc(s_dd, 1)
            v.wait_ge(s_back, 1)
            V.memset(g.factors[:], 0.0)
            v.drain()
            for x in range(3):
                V.tensor_copy(g.factors[:, x, 0:PT, :], psh[:, x, 0:PT * H].rearrange("p (t h) -> p t h", h=H))
                V.tensor_copy(g.factors[0:NSAMP, x, PT, :], psh[0:NSAMP, x, PT * H:TILES * H])
            V.tensor_copy(g.decay[:], psh[:, 3, 0:H * NC].rearrange("p (h c) -> p h c", h=H))

        @block.scalar
        def _(act):
            act.wait_ge(s_ab, 1)
            nc.scalar.activation(ab[:], ab[:], ACT.Exp)
            act.drain()
            act.sem_inc(s_e, 1)
            act.wait_ge(s_ab, 2)
            nc.scalar.activation(ab[:], ab[:], ACT.Ln)
            act.drain()
            act.sem_inc(s_ln, 1)
            act.wait_ge(s_args, 1)
            nc.scalar.activation(e3[:], e3[:], ACT.Exp)
            nc.scalar.activation(dec[:], dec[:], ACT.Exp)
            act.drain()
            act.sem_inc(s_exps, 1)

        @block.tensor
        def _(pe):
            T = nc.tensor
            pe.wait_ge(s_lf, 1)
            T.matmul(psb[:, 0:PT * H], g.tri[:, 0, :], lf[:, 0:PT, :], start=True, stop=True)
            T.matmul(psb[0:NSAMP, 128:128 + H], g.tri[0:NSAMP, 1, 0:NSAMP], lf[0:NSAMP, PT, :],
                     start=True, stop=True)
            pe.drain()
            pe.sem_inc(s_b, 1)
            pe.wait_ge(s_u, 1)
            for bank, src in ((0, g.u), (2, btok)):
                for t in range(PT):
                    T.transpose(psh[0:H, bank + t // 4, (t % 4) * P:(t % 4 + 1) * P], src[:, t, :], g.ident[:])
                o = 0 if bank == 0 else NSAMP
                T.transpose(psh[0:H, 4, o:o + NSAMP], src[0:NSAMP, PT, :], g.ident[0:NSAMP, 0:NSAMP])
            pe.drain()
            pe.sem_inc(s_t, 1)
            pe.wait_ge(s_dd, 1)
            for x in range(3):
                for t in range(TILES):
                    n = rows_of(t)
                    T.transpose(psh[0:n, x, t * H:(t + 1) * H], e3[:, x, t * P:t * P + n], g.ident[0:H, 0:H])
            T.matmul(psh[:, 3, 0:H * NC], g.ones[0:H, :], decd[:], start=True, stop=True)
            pe.drain()
            pe.sem_inc(s_back, 1)


def stage_mlstm(nc, g):
    with nc.cleanup_on_exit(), ExitStack() as ctx:
        def sb(n, s, d=F32):
            return ctx.enter_context(nc.sbuf_tensor(n, s, d))

        def sem(n):
            return nc.alloc_semaphore(f"m_{n}")

        qkvo = sb("m_qkvo", [P, 2, A_IN])
        qT = sb("m_qT", [P, PAIRS, P])
        kT = sb("m_kT", [P, PAIRS, P])
        Md = sb("m_Md", [H, H, P])
        mask4 = sb("m_mask4", [P, 4, P])
        ex = sb("m_ex", [P, H, P])
        va = sb("m_va", [P, H, AUG])
        kw = sb("m_kw", [P, H, DK])
        kwb = sb("m_kwb", [NSAMP, BATCHES, H * DK])
        qb = sb("m_qb", [P, BATCHES, PAIRS, NSAMP])
        C = sb("m_C", [P, PAIRS, AUG])
        Cs = sb("m_Cs", [P, BATCHES, PAIRS, AUG])
        hh = sb("m_hh", [P, H, AUG])
        sg = sb("m_sg", [P, D])
        y = sb("m_y", [P, D])
        ng = sb("m_ng", [P, D])
        dn = sb("m_dn", [P, 2, H])
        st = sb("m_st", [P, H, 6])
        mv = sb("m_mv", [P, H, 2])
        rs = sb("m_rs", [P, H])
        bmT = sb("m_bmT", [P, BATCHES, NSAMP])
        ps = ctx.enter_context(nc.psum_tensor("m_ps", [P, 8, HALF], F32))
        TS, AA, NN, QQ = 0, 2, 4, 6
        s_ld = [sem("qkvo_loaded0"), sem("qkvo_loaded1")]
        s_c, s_T, s_qk, s_Md, s_A, s_E, s_S, s_P, s_va = (sem(x) for x in (
            "side_loaded", "qk_turned", "qkT_ready", "M_diag", "exponents", "exp_ready", "scores", "weighted", "values_ready"))
        s_N, s_comb, s_kw, s_U, s_C, s_free, s_var, s_sd, s_osig, s_y, s_yT, s_out, s_mask, s_qb, s_st = (sem(x) for x in (
            "heads_summed", "heads_combined", "k_weighted", "state_added", "state_ready", "chunk_done", "variance",
            "deviation", "o_exp", "y_ready", "y_turned", "y_out", "mask_ready", "q_by_batch", "states_stored"))
        block = ctx.enter_context(nc.Block())

        @block.sync
        def _(sp):
            sp.dma_start(ng[:], g.a_norm_g.broadcast_to([P, D])).then_inc(s_c, 16)
            sp.dma_start(Cs[:], g.state).then_inc(s_c, 16)
            sp.dma_start(bmT[:], g.const["bmaskT"]).then_inc(s_c, 16)
            with sp.Fori(0, PT // 2) as i:
                for par in range(2):
                    t = i * 2 + par
                    sp.wait_ge(s_free, t + 1)
                    sp.dma_start(qkvo[:, par, :], g.qkvo[bass.ds(t * P, P), :]).then_inc(s_ld[par], 16)
            sp.wait_ge(s_free, PT + 1)
            sp.dma_start(qkvo[0:NSAMP, 0, :], g.qkvo[SEQ:N, :]).then_inc(s_ld[0], 16)
            sp.wait_ge(s_C, PT)
            sp.dma_start(g.C_p, C[:]).then_inc(s_st, 16)
            sp.wait_ge(s_C, PT + BATCHES)
            sp.dma_start(g.C_s, Cs[:]).then_inc(s_st, 16)
            sp.wait_ge(s_st, 32)

        def half(h):
            return slice(DK * (h % 2), DK * (h % 2) + DK)

        @block.tensor
        def _(pe):
            T = nc.tensor

            def chunk(t, par, i, n, sample):
                pe.wait_ge(s_ld[par], 16 * i + 16)
                pe.wait_ge(s_out, t + 1)
                for z in range(2):
                    for p in range(PAIRS):
                        mm = T.transpose(ps[:, TS + z, p * P:p * P + n],
                                         qkvo[0:n, par, z * 512 + p * P:z * 512 + (p + 1) * P], g.ident[0:n, 0:n])
                mm.then_inc(s_T, 1)
                pe.wait_ge(s_Md, t + 1)
                pe.wait_ge(s_mask, 2 if sample else 1)
                for a in range(2):
                    T.matmul(ps[0:n, AA + a, 0:4 * n], g.ident[0:n, 0:n], mask4[0:n, :, 0:n], start=True, stop=False)
                    mm = T.matmul(ps[0:n, AA + a, 0:4 * n], g.ones[0:H, 0:n], Md[:, a * 4:a * 4 + 4, 0:n],
                                  start=False, stop=True)
                mm.then_inc(s_A, 1)
                pe.wait_ge(s_qk, t + 1)
                for h in range(H):
                    mm = T.matmul(ps[0:n, TS + h % 2, (h // 2) * n:(h // 2 + 1) * n], kT[half(h), h // 2, 0:n],
                                  qT[half(h), h // 2, 0:n], start=True, stop=True, skip_group_check=True)
                pe.drain()
                pe.sem_inc(s_S, 1)
                pe.wait_ge(s_va, t + 1)
                if sample:
                    pe.wait_ge(s_qb, 1)
                for a in range(2):
                    pe.wait_ge(s_P, 2 * t + 2)
                    pe.wait_ge(s_comb, 2 * t + a + 1)
                    for h in range(4 * a, 4 * a + 4):
                        b, o = h % 2, (h // 2 % 2) * AUG
                        T.matmul(ps[0:n, NN + b, o:o + AUG], ex[0:n, h, 0:n], va[0:n, h, :],
                                 start=True, stop=True, skip_group_check=True)
                        if not sample:
                            mm = T.matmul(ps[0:n, QQ + b, o:o + AUG], qT[half(h), h // 2, 0:n], C[half(h), h // 2, :],
                                          start=True, stop=True, skip_group_check=True)
                        else:
                            for z in range(BATCHES):
                                mm = T.matmul(ps[0:n, QQ + b, o:o + AUG], qb[half(h), z, h // 2, :],
                                              Cs[half(h), z, h // 2, :], start=(z == 0), stop=(z == BATCHES - 1),
                                              skip_group_check=True)
                    pe.drain()
                    pe.sem_inc(s_N, 1)
                pe.wait_ge(s_kw, t + 1)
                if not sample:
                    for p in range(PAIRS):
                        mm = T.matmul(ps[:, (TS if p < 2 else AA) + p % 2, 0:2 * AUG],
                                      kw[:, 2 * p:2 * p + 2, :], va[:, 2 * p:2 * p + 2, :], start=True, stop=True)
                    mm.then_inc(s_U, 1)
                else:
                    for z in range(BATCHES):
                        if z >= 1:
                            pe.wait_ge(s_C, PT + z)
                        for p in range(PAIRS):
                            mm = T.matmul(ps[:, (TS if p < 2 else AA) + p % 2, 0:2 * AUG],
                                          kwb[:, z, p * P:(p + 1) * P], va[0:n, 2 * p:2 * p + 2, :],
                                          start=True, stop=True)
                        mm.then_inc(s_U, 1)
                pe.wait_ge(s_y, t + 2)
                pe.wait_ge(s_comb, 2 * t + 3)
                for k in range(KD):
                    mm = T.transpose(ps[:, NN + k // 4, (k % 4) * P:(k % 4) * P + n], y[0:n, k * P:(k + 1) * P],
                                     g.ident[0:n, 0:n])
                mm.then_inc(s_yT, 1)

            with pe.Fori(0, PT // 2) as i:
                for par in range(2):
                    chunk(i * 2 + par, par, i, P, False)
            chunk(PT, 0, PT // 2, NSAMP, True)

        @block.scalar
        def _(act):
            S = nc.scalar
            act.sem_inc(s_out, 1)

            def chunk(t, par, n):
                act.wait_ge(s_T, t + 1)
                S.copy(qT[:, :, 0:n], ps[:, TS, :].rearrange("p (a s) -> p a s", a=PAIRS)[:, :, 0:n])
                S.mul(kT[:, :, 0:n], ps[:, TS + 1, :].rearrange("p (a s) -> p a s", a=PAIRS)[:, :, 0:n], DK ** -0.5)
                act.drain()
                act.sem_inc(s_qk, 1)
                act.wait_ge(s_A, t + 1)
                act.wait_ge(s_N, 2 * t + 2)
                act.wait_ge(s_y, t + 1)
                for h in range(H):
                    a = ps[0:n, AA + h // 4, (h % 4) * n:(h % 4 + 1) * n]
                    S.activation(ex[0:n, h, 0:n], a, ACT.Exp,
                                 bias=g.u[0:n, bass.ds(t, 1), h:h + 1].rearrange("p o h -> p (o h)"))
                S.activation(sg[0:n, :], qkvo[0:n, par, 2 * D:3 * D], ACT.Exp, scale=-1.0)
                act.drain()
                act.sem_inc(s_E, 1)
                act.wait_ge(s_var, t + 1)
                S.activation(rs[0:n, :], rs[0:n, :], ACT.Sqrt)
                act.drain()
                act.sem_inc(s_sd, 1)
                act.wait_ge(s_yT, t + 1)
                for z in range(2):
                    S.copy(g.mixT[:, z * 4:z * 4 + 4, bass.ds(t * P, n)],
                           ps[:, NN + z, :].rearrange("p (k s) -> p k s", k=4)[:, :, 0:n])
                act.drain()
                act.sem_inc(s_out, 1)

            with act.Fori(0, PT // 2) as i:
                for par in range(2):
                    chunk(i * 2 + par, par, P)
            chunk(PT, 0, NSAMP)

        @block.vector
        def _(v):
            V = nc.vector
            v.sem_inc(s_free, 2)
            v.sem_inc(s_comb, 1)
            v.sem_inc(s_y, 1)
            V.memset(va[:, :, DV:AUG], 1.0)
            V.memset(C[:], 0.0)
            V.tensor_copy(mask4[:], g.lmask[:, 0, :].unsqueeze(1).broadcast_to([P, 4, P]))
            v.drain()
            v.sem_inc(s_mask, 1)
            v.sem_inc(s_N, 2)
            v.wait_ge(s_c, 48)

            def chunk(t, par, i, n, sample):
                M = g.M[:, bass.ds(t * P, n)]
                V.scalar_tensor_tensor(out=Md[:, :, 0:n], in0=M.unsqueeze(1).broadcast_to([H, H, n]), scalar=-1.0,
                                       in1=g.ident[0:H, 0:H].unsqueeze(2).broadcast_to([H, H, n]),
                                       op0=ALU.mult, op1=ALU.mult)
                v.drain()
                v.sem_inc(s_Md, 1)
                v.wait_ge(s_ld[par], 16 * i + 16)
                L = qkvo[0:n, par, :]
                f = g.factors[0:n, :, bass.ds(t, 1), :].rearrange("p x o h -> p x (o h)")
                V.tensor_copy(va[0:n, :, 0:DV], L[:, D:2 * D].rearrange("p (h v) -> p h v", h=H))
                V.scalar_tensor_tensor(out=kw[0:n, :, :], in0=L[:, 512:D].rearrange("p (h k) -> p h k", h=H),
                                       scalar=DK ** -0.5, in1=f[:, 2, :].unsqueeze(2).broadcast_to([n, H, DK]),
                                       op0=ALU.mult, op1=ALU.mult)
                v.drain()
                v.sem_inc(s_va, 1)
                if sample:
                    v.wait_ge(s_qk, t + 1)
                    for z in range(BATCHES):
                        V.tensor_scalar(kwb[:, z, :], kw[0:n, :, :].rearrange("p h k -> p (h k)"),
                                        g.bmask[0:n, z:z + 1], None, ALU.mult)
                        V.tensor_tensor(qb[:, z, :, :], qT[:, :, 0:n],
                                        bmT[:, z, :].unsqueeze(1).broadcast_to([P, PAIRS, n]), ALU.mult)
                    v.drain()
                    v.sem_inc(s_qb, 1)
                v.sem_inc(s_kw, 1)
                v.wait_ge(s_E, t + 1)
                v.wait_ge(s_S, t + 1)
                for a in range(2):
                    V.tensor_tensor(ex[0:n, a:H:2, 0:n], ex[0:n, a:H:2, 0:n],
                                    ps[0:n, TS + a, 0:4 * n].rearrange("p (h s) -> p h s", h=4), ALU.mult)
                    v.drain()
                    v.sem_inc(s_P, 1)
                V.tensor_scalar(sg[0:n, :], sg[0:n, :], 1.0, None, ALU.add)
                v.drain()
                V.reciprocal(sg[0:n, :], sg[0:n, :])
                v.drain()
                V.tensor_tensor(sg[0:n, :], sg[0:n, :], ng[0:n, :], ALU.mult)
                for a in range(2):
                    v.wait_ge(s_N, 2 * t + a + 3)
                    for b in range(2):
                        hs = slice(4 * a + b, 4 * a + 4, 2)
                        two = ps[0:n, QQ + b, 0:2 * AUG].rearrange("p (h v) -> p h v", h=2)
                        V.tensor_tensor(hh[0:n, hs, :], two,
                                        f[:, 0, hs].unsqueeze(2).broadcast_to([n, 2, AUG]), ALU.mult)
                        v.drain()
                        V.tensor_tensor(hh[0:n, hs, :], hh[0:n, hs, :],
                                        ps[0:n, NN + b, 0:2 * AUG].rearrange("p (h v) -> p h v", h=2), ALU.add)
                    v.drain()
                    v.sem_inc(s_comb, 1)
                if not sample:
                    v.wait_ge(s_U, t + 1)
                    for h in range(H):
                        U = ps[half(h), (TS if h < 4 else AA) + (h // 2) % 2, (h % 2) * AUG:(h % 2 + 1) * AUG]
                        V.scalar_tensor_tensor(out=C[half(h), h // 2, :], in0=C[half(h), h // 2, :],
                                               scalar=g.decay[half(h), h, bass.ds(t, 1)], in1=U,
                                               op0=ALU.mult, op1=ALU.add)
                    v.drain()
                    v.sem_inc(s_C, 1)
                else:
                    for z in range(BATCHES):
                        v.wait_ge(s_U, PT + z + 1)
                        for h in range(H):
                            U = ps[half(h), (TS if h < 4 else AA) + (h // 2) % 2, (h % 2) * AUG:(h % 2 + 1) * AUG]
                            V.scalar_tensor_tensor(out=Cs[half(h), z, h // 2, :], in0=Cs[half(h), z, h // 2, :],
                                                   scalar=g.decay[half(h), h, PT + z:PT + z + 1], in1=U,
                                                   op0=ALU.mult, op1=ALU.add)
                        v.drain()
                        v.sem_inc(s_C, 1)
                den = hh[0:n, :, DV]
                V.tensor_scalar(dn[0:n, 0, :], den, -1.0, None, ALU.mult)
                v.drain()
                V.tensor_tensor(dn[0:n, 0, :], dn[0:n, 0, :], den, ALU.max)
                v.drain()
                V.tensor_tensor(dn[0:n, 0, :], dn[0:n, 0, :], f[:, 1, :], ALU.max)
                v.drain()
                V.reciprocal(dn[0:n, 1, :], dn[0:n, 0, :])
                v.drain()
                yh = y[0:n, :].rearrange("p (h v) -> p h v", h=H)
                V.tensor_tensor(yh, hh[0:n, :, 0:DV], dn[0:n, 1, :].unsqueeze(2).broadcast_to([n, H, DV]), ALU.mult)
                v.drain()
                for h in range(H):
                    V.bn_stats(st[0:n, h, :], yh[:, h, :])
                v.drain()
                for h in range(H):
                    V.bn_aggr(mv[0:n, h, :], st[0:n, h, :])
                v.drain()
                V.tensor_scalar(rs[0:n, :], mv[0:n, :, 1], EPS, None, ALU.add)
                V.tensor_tensor(yh, yh, mv[0:n, :, 0].unsqueeze(2).broadcast_to([n, H, DV]), ALU.subtract)
                v.drain()
                v.sem_inc(s_var, 1)
                V.tensor_tensor(y[0:n, :], y[0:n, :], sg[0:n, :], ALU.mult)
                v.wait_ge(s_sd, t + 1)
                V.reciprocal(rs[0:n, :], rs[0:n, :])
                v.drain()
                V.tensor_tensor(yh, yh, rs[0:n, :].unsqueeze(2).broadcast_to([n, H, DV]), ALU.mult)
                v.drain()
                v.sem_inc(s_y, 1)
                v.sem_inc(s_free, 1)
                v.wait_ge(s_yT, t + 1)

            with v.Fori(0, PT // 2) as i:
                for par in range(2):
                    chunk(i * 2 + par, par, i, P, False)
            V.tensor_copy(mask4[:, :, 0:NSAMP], g.lmask[:, 1, 0:NSAMP].unsqueeze(1).broadcast_to([P, 4, NSAMP]))
            v.drain()
            v.sem_inc(s_mask, 1)
            chunk(PT, 0, PT // 2, NSAMP, True)


def norm_steps(nc, v, w, n, ask, answer, have):
    V = nc.vector
    z = w.z[0:n, :]
    for a in range(2):
        V.bn_stats(w.stats[0:n, a, :], z[:, a * HALF:(a + 1) * HALF])
    v.drain()
    V.bn_aggr(w.mv[0:n, :], w.stats[0:n, :, :].rearrange("p a s -> p (a s)"))
    v.drain()
    V.tensor_scalar(w.sd[0:n, :], w.mv[0:n, 1:2], EPS, None, ALU.add)
    v.drain()
    v.sem_inc(ask, 1)
    v.wait_ge(answer, have)
    V.reciprocal(w.sd[0:n, :], w.sd[0:n, :])
    v.drain()
    V.tensor_scalar(z, z, w.mv[0:n, 0:1], w.sd[0:n, 0:1], ALU.subtract, ALU.mult)
    v.drain()
    V.tensor_tensor(z, z, w.g[0:n, :], ALU.mult)
    v.drain()


def stage_out_proj(nc, g, layer, weight):
    with nc.cleanup_on_exit(), ExitStack() as ctx:
        def sb(n, s, d=F32):
            return ctx.enter_context(nc.sbuf_tensor(f"o{layer}_{n}", s, d))

        def sem(n):
            return nc.alloc_semaphore(f"o{layer}_{n}")

        w = Shared()
        wt = sb("w", [P, KD, D])
        rw = sb("rw", [P, KD, E])
        mix = sb("mix", [P, 2, KD, P])
        w.z, w.stats, w.mv, w.sd = sb("z", [P, D]), sb("stats", [P, 2, 6]), sb("mv", [P, 2]), sb("sd", [P, 1])
        w.g, lb = sb("lg", [P, D]), sb("lb", [P, D])
        gate, scale, shift = sb("gate", [P, D]), sb("scale", [P, D]), sb("shift", [P, D])
        h2 = sb("h2", [P, 2, D])
        hT = sb("hT", [P, KD, P])
        ps = ctx.enter_context(nc.psum_tensor(f"o{layer}_ps", [P, 2, D], F32))
        psT = ctx.enter_context(nc.psum_tensor(f"o{layer}_psT", [P, KD, P], F32))
        psR = ctx.enter_context(nc.psum_tensor(f"o{layer}_psR", [P, HALF], F32))
        s_w, s_ld, s_mods, s_mix, s_Y, s_read, s_var, s_sd, s_h2, s_T, s_hT, s_R, s_done, s_z = (sem(x) for x in (
            "w_loaded", "side_loaded", "mods_loaded", "mix_staged", "y_summed", "y_read", "variance", "deviation",
            "h2_ready", "h2_turned", "h2T_ready", "logits_summed", "logits_out", "zero_row"))
        s_st = [sem("h2_stored0"), sem("h2_stored1")]
        block = ctx.enter_context(nc.Block())

        @block.sync
        def _(sp):
            sp.dma_start(wt[:], weight.rearrange("(k p) n -> p k n", p=P)).then_inc(s_w, 16)
            sp.dma_start(w.g[:], g.ln_g[2 * layer:2 * layer + 1, :].broadcast_to([P, D])).then_inc(s_ld, 16)
            sp.dma_start(lb[:], g.ln_b[2 * layer:2 * layer + 1, :].broadcast_to([P, D])).then_inc(s_ld, 16)
            sp.dma_start(rw[:], g.router_w.rearrange("(k p) e -> p k e", p=P)).then_inc(s_ld, 16)
            for which, dst in ((GATE1, gate), (SHIFT2, shift), (SCALE2, scale)):
                load_mods(sp, g, dst, layer, which, False, s_mods)

            def store(t, par, n):
                sp.wait_ge(s_h2, t + 2)
                sp.dma_start(g.h2[bass.ds(t * P, n), :], h2[0:n, par, :]).then_inc(s_st[par], 16)

            with sp.Fori(0, PT // 2) as i:
                for par in range(2):
                    store(i * 2 + par, par, P)
            for which, dst in ((GATE1, gate), (SHIFT2, shift), (SCALE2, scale)):
                load_mods(sp, g, dst, layer, which, True, s_mods)
            store(PT, 0, NSAMP)
            sp.wait_ge(s_z, 1)
            sp.wait_ge(s_st[1], 16 * (PT // 2) + 16)
            sp.dma_start(g.h2[N:N + 1, :], h2[0:1, 1, :]).then_inc(s_st[1], 16)
            sp.wait_ge(s_st[0], 16 * (PT // 2 + 1) + 16)
            sp.wait_ge(s_st[1], 16 * (PT // 2 + 1) + 16)

        @block.gpsimd
        def _(po):
            po.sem_inc(s_mix, 1)

            def stage(t, par, n):
                po.wait_ge(s_Y, t + 1)
                nc.gpsimd.tensor_copy(mix[:, par, :, 0:n], g.mixT[:, :, bass.ds(t * P, n)])
                po.drain()
                po.sem_inc(s_mix, 1)

            with po.Fori(0, PT // 2) as i:
                for par in range(2):
                    stage(i * 2 + par, par, P)
            stage(PT, 0, NSAMP)

        @block.tensor
        def _(pe):
            T = nc.tensor
            pe.sem_inc(s_Y, 2)
            pe.wait_ge(s_w, 16)
            pe.wait_ge(s_ld, 48)

            def route(t, n):
                pe.wait_ge(s_h2, t + 2)
                pe.wait_ge(s_hT, t + 1)
                for k in range(KD):
                    mm = T.transpose(psT[:, k, 0:n], hcur(t)[0:n, k * P:(k + 1) * P], g.ident[0:n, 0:n])
                mm.then_inc(s_T, 1)
                pe.wait_ge(s_hT, t + 2)
                pe.wait_ge(s_done, t + 1)
                for k in range(KD):
                    mm = T.matmul(psR[0:n, 0:E], hT[:, k, 0:n], rw[:, k, :], start=(k == 0), stop=(k == KD - 1))
                mm.then_inc(s_R, 1)

            def project(t, par, n):
                pe.wait_ge(s_mix, t + 2)
                pe.wait_ge(s_read, t + 1)
                for c in range(2):
                    for k in range(KD):
                        mm = T.matmul(ps[0:n, par, c * HALF:(c + 1) * HALF], mix[:, par, k, 0:n],
                                      wt[:, k, c * HALF:(c + 1) * HALF], start=(k == 0), stop=(k == KD - 1))
                mm.then_inc(s_Y, 1)

            slot = [0]

            def hcur(t):
                return h2[:, slot[0], :]

            project(0, 0, P)
            with pe.Fori(0, PT // 2 - 1) as i:
                for par in range(2):
                    t = i * 2 + par
                    project(t + 1, 1 - par, P)
                    slot[0] = par
                    route(t, P)
            project(PT - 1, 1, P)
            slot[0] = 0
            route(PT - 2, P)
            project(PT, 0, NSAMP)
            slot[0] = 1
            route(PT - 1, P)
            slot[0] = 0
            route(PT, NSAMP)

        @block.scalar
        def _(act):
            act.sem_inc(s_hT, 1)
            act.sem_inc(s_done, 1)

            def tile(t, n):
                act.wait_ge(s_var, t + 1)
                nc.scalar.activation(w.sd[0:n, :], w.sd[0:n, :], ACT.Sqrt)
                act.drain()
                act.sem_inc(s_sd, 1)
                act.wait_ge(s_T, t + 1)
                act.wait_ge(s_R, t + 1)
                for z in range(2):
                    nc.scalar.copy(hT[:, z * 4:z * 4 + 4, 0:n], psT[:, z * 4:z * 4 + 4, 0:n])
                act.drain()
                act.sem_inc(s_hT, 1)
                act.wait_ge(s_R, t + 2)
                nc.scalar.copy(g.logits[0:n, bass.ds(t, 1), :].rearrange("p o e -> p (o e)"), psR[0:n, 0:E])
                act.drain()
                act.sem_inc(s_done, 1)

            with act.Fori(0, PT) as t:
                tile(t, P)
            tile(PT, NSAMP)

        @block.vector
        def _(v):
            V = nc.vector
            v.sem_inc(s_read, 2)
            v.sem_inc(s_h2, 1)
            v.sem_inc(s_R, 1)
            v.sem_inc(s_st[0], 16)
            v.sem_inc(s_st[1], 16)
            V.memset(g.logits[:], 0.0)
            v.wait_ge(s_ld, 48)

            def tile(t, par, i, n, mods):
                x = g.x[0:n, bass.ds(t, 1), :].rearrange("p o d -> p (o d)")
                z = w.z[0:n, :]
                v.wait_ge(s_mods, mods)
                v.wait_ge(s_Y, t + 3)
                V.tensor_tensor(z, ps[0:n, par, :], gate[0:n, :], ALU.mult)
                v.drain()
                v.sem_inc(s_read, 1)
                V.scalar_tensor_tensor(out=z, in0=x, scalar=ALPHA, in1=z, op0=ALU.mult, op1=ALU.add)
                v.drain()
                norm_steps(nc, v, w, n, s_var, s_sd, t + 1)
                V.tensor_tensor(x, z, lb[0:n, :], ALU.add)
                v.drain()
                v.wait_ge(s_st[par], 16 * i + 16)
                o = h2[0:n, par, :]
                V.scalar_tensor_tensor(out=o, in0=scale[0:n, :], scalar=1.0, in1=x, op0=ALU.add, op1=ALU.mult)
                v.drain()
                V.tensor_tensor(o, o, shift[0:n, :], ALU.add)
                v.drain()
                v.sem_inc(s_h2, 1)

            with v.Fori(0, PT // 2) as i:
                for par in range(2):
                    tile(i * 2 + par, par, i, P, 48)
            tile(PT, 0, PT // 2, NSAMP, 48 + 3 * 16 * BATCHES)
            v.wait_ge(s_st[1], 16 * (PT // 2) + 16)
            v.wait_ge(s_R, PT + 1)
            V.memset(h2[0:1, 1, :], 0.0)
            v.drain()
            v.sem_inc(s_z, 1)


def stage_route(nc, g, layer):
    with nc.cleanup_on_exit(), ExitStack() as ctx:
        def sb(n, s, d=F32):
            return ctx.enter_context(nc.sbuf_tensor(f"r{layer}_{n}", s, d))

        def sem(n):
            return nc.alloc_semaphore(f"r{layer}_{n}")

        sh3 = [P, TILES, E]
        rb = sb("bias", [P, E])
        sc, sel, work = sb("scores", sh3), sb("sel", sh3), sb("work", sh3)
        oh = [sb("first", sh3), sb("second", sh3)]
        gs, gm, gi = sb("gs", [P, TILES, GROUPS]), sb("gm", [P, TILES, GROUPS]), sb("gi", [P, TILES, GROUPS])
        pr = sb("pairs", [P, TILES, GROUPS, 3])
        mx = sb("mx", [P, TILES])
        ws = sb("ws", [P, TILES])
        both = sb("both", sh3)
        tot = sb("tot", sh3)
        carry = sb("carry", [P, TILES + 1, E])
        place = sb("place", sh3)
        more = sb("more", [P, E, TILES])
        blocks, ends, tmp = sb("blocks", [P, E]), sb("ends", [P, 2, E]), sb("start", [P, E])
        destf = sb("destf", [P, 2, TILES])
        full = sb("full", [P, SLOTS, E])
        slotf = sb("slotf", [P, SLOTS])
        ids = sb("ids", [P, TILES], I32)
        ps = ctx.enter_context(nc.psum_tensor(f"r{layer}_ps", [P, 2, HALF], F32))
        s_ld, s_e, s_oh, s_cnt, s_dest, s_sc = (sem(x) for x in (
            "loaded", "exp_ready", "choices", "counted", "dest_ready", "scattered"))
        block = ctx.enter_context(nc.Block())

        @block.sync
        def _(sp):
            sp.dma_start(rb[:], g.router_b.broadcast_to([P, E])).then_inc(s_ld, 16)
            sp.dma_start(ids[:], g.const["token_ids"]).then_inc(s_ld, 16)
            sp.dma_start(g.slot_token, g.const["no_token"].rearrange("s (p o) -> (s p) o", o=1)).then_inc(s_ld, 16)

        @block.scalar
        def _(act):
            nc.scalar.activation(sc[:], g.logits[:], ACT.Exp, scale=-1.0)
            act.drain()
            act.sem_inc(s_e, 1)

        @block.tensor
        def _(pe):
            pe.wait_ge(s_oh, 1)
            b2 = both[:].rearrange("p t e -> p (t e)")
            nc.tensor.matmul(ps[:, 0, 0:TILES * E], g.tri[:, 2, :], b2, start=True, stop=True)
            nc.tensor.matmul(ps[:, 1, 0:TILES * E], g.ones[:], b2, start=True, stop=True)
            pe.drain()
            pe.sem_inc(s_cnt, 1)

        @block.gpsimd
        def _(po):
            po.wait_ge(s_ld, 48)
            po.wait_ge(s_dest, 1)
            n = 0
            for k in range(2):
                for t in range(TILES):
                    r = rows_of(t)
                    nc.gpsimd.indirect_dma_start(
                        g.slot_token, bass.IndirectOffsetOnAxis(g.dest[0:r, k, t:t + 1], axis=0),
                        ids[0:r, t:t + 1], None).then_inc(s_sc, 16)
                    n += 16
            po.wait_ge(s_sc, n)

        @block.vector
        def _(v):
            V = nc.vector

            def wide(a, n=E):
                return a.unsqueeze(2).broadcast_to([P, TILES, n])

            v.wait_ge(s_ld, 48)
            v.wait_ge(s_e, 1)
            V.tensor_scalar(sc[:], sc[:], 1.0, None, ALU.add)
            v.drain()
            V.reciprocal(sc[:], sc[:])
            v.drain()
            V.tensor_tensor(sel[:], sc[:], rb[:].unsqueeze(1).broadcast_to(sh3), ALU.add)
            v.drain()
            s4 = sel[:].rearrange("p t (g x) -> p t g x", g=GROUPS)
            V.tensor_tensor(pr[:], s4[:, :, :, 0:3], s4[:, :, :, 1:4], ALU.add)
            V.tensor_tensor(gs[:], s4[:, :, :, 0], s4[:, :, :, 3], ALU.add)
            v.drain()
            V.tensor_reduce(gm[:], pr[:], AX, ALU.max)
            v.drain()
            V.tensor_tensor(pr[:, :, :, 0:2], s4[:, :, :, 0:2], s4[:, :, :, 2:4], ALU.add)
            V.tensor_tensor(gs[:], gs[:], gm[:], ALU.max)
            v.drain()
            V.tensor_tensor(gs[:], gs[:], pr[:, :, :, 0], ALU.max)
            v.drain()
            V.tensor_tensor(gs[:], gs[:], pr[:, :, :, 1], ALU.max)
            v.drain()

            def first_largest(values, hot, n):
                down = g.count_down[:, E - n:E].unsqueeze(1).broadcast_to([P, TILES, n])
                V.tensor_reduce(mx[:], values, AX, ALU.max)
                v.drain()
                V.tensor_tensor(hot, values, wide(mx[:], n), ALU.is_equal)
                v.drain()
                V.tensor_tensor(hot, hot, down, ALU.mult)
                v.drain()
                V.tensor_reduce(mx[:], hot, AX, ALU.max)
                v.drain()
                V.tensor_tensor(hot, down, wide(mx[:], n), ALU.is_equal)
                v.drain()

            first_largest(gs[:], gi[:], GROUPS)
            V.tensor_scalar(gm[:], gi[:], -1.0, -NEG, ALU.add, ALU.mult)
            V.tensor_tensor(work[:].rearrange("p t (g x) -> p t g x", g=GROUPS), s4,
                            gi[:].unsqueeze(3).broadcast_to([P, TILES, GROUPS, PER]), ALU.mult)
            v.drain()
            V.tensor_tensor(work[:].rearrange("p t (g x) -> p t g x", g=GROUPS),
                            work[:].rearrange("p t (g x) -> p t g x", g=GROUPS),
                            gm[:].unsqueeze(3).broadcast_to([P, TILES, GROUPS, PER]), ALU.add)
            v.drain()
            first_largest(work[:], oh[0][:], E)
            V.scalar_tensor_tensor(out=work[:], in0=oh[0][:], scalar=4 * NEG, in1=work[:], op0=ALU.mult, op1=ALU.add)
            v.drain()
            first_largest(work[:], oh[1][:], E)
            for k in range(2):
                V.tensor_tensor(work[:], sc[:], oh[k][:], ALU.mult)
                v.drain()
                V.tensor_reduce(g.weight[:, k, :], work[:], AX, ALU.add)
                v.drain()
            V.tensor_tensor(ws[:], g.weight[:, 0, :], g.weight[:, 1, :], ALU.add)
            v.drain()
            V.reciprocal(ws[:], ws[:])
            V.tensor_tensor(both[:], oh[0][:], oh[1][:], ALU.add)
            v.drain()
            for k in range(2):
                V.tensor_tensor(g.weight[:, k, :], g.weight[:, k, :], ws[:], ALU.mult)
            V.memset(both[NSAMP:P, TILES - 1, :], 0.0)
            V.memset(carry[:, 0, :], 0.0)
            v.drain()
            v.sem_inc(s_oh, 1)
            v.wait_ge(s_cnt, 1)
            V.tensor_copy(tot[:].rearrange("p t e -> p (t e)"), ps[:, 1, 0:TILES * E])
            v.drain()
            for t in range(TILES):
                V.tensor_tensor(carry[:, t + 1, :], carry[:, t, :], tot[:, t, :], ALU.add)
                v.drain()
            V.tensor_tensor(more[:], carry[:, TILES, :].unsqueeze(2).broadcast_to([P, E, TILES]),
                            g.steps[:].unsqueeze(1).broadcast_to([P, E, TILES]), ALU.is_gt)
            v.drain()
            V.tensor_reduce(blocks[:], more[:], AX, ALU.add)
            v.drain()
            V.tensor_copy(ends[:, 0, :], blocks[:])
            v.drain()
            a, k = 0, 1
            while k < E:
                V.tensor_tensor(ends[:, 1 - a, k:E], ends[:, a, k:E], ends[:, a, 0:E - k], ALU.add)
                V.tensor_copy(ends[:, 1 - a, 0:k], ends[:, a, 0:k])
                v.drain()
                a, k = 1 - a, 2 * k
            V.tensor_tensor(tmp[:], ends[:, a, :], blocks[:], ALU.subtract)
            V.tensor_tensor(full[:], ends[:, a, :].unsqueeze(1).broadcast_to([P, SLOTS, E]),
                            g.count_up[:, 0:SLOTS].unsqueeze(2).broadcast_to([P, SLOTS, E]), ALU.is_le)
            v.drain()
            V.tensor_reduce(slotf[:], full[:], AX, ALU.add)
            V.tensor_scalar(tmp[:], tmp[:], float(P), None, ALU.mult)
            v.drain()
            V.tensor_scalar(slotf[:], slotf[:], float(E - 1), None, ALU.min)
            V.tensor_tensor(place[:], carry[:, 0:TILES, :], tmp[:].unsqueeze(1).broadcast_to(sh3), ALU.add)
            v.drain()
            V.tensor_copy(g.slot_expert[:], slotf[:])
            V.tensor_tensor(place[:], place[:], ps[:, 0, 0:TILES * E].rearrange("p (t e) -> p t e", e=E), ALU.add)
            v.drain()
            for k in range(2):
                V.tensor_tensor(work[:], place[:], oh[k][:], ALU.mult)
                v.drain()
                V.tensor_reduce(destf[:, k, :], work[:], AX, ALU.add)
                v.drain()
            V.tensor_copy(g.dest[:], destf[:])
            v.drain()
            v.sem_inc(s_dest, 1)


def stage_experts(nc, g, layer):
    with nc.cleanup_on_exit(), ExitStack() as ctx:
        def sb(n, s, d=F32):
            return ctx.enter_context(nc.sbuf_tensor(f"e{layer}_{n}", s, d))

        def sem(n):
            return nc.alloc_semaphore(f"e{layer}_{n}")

        wg, wu = sb("wg", [P, 2, KD, FE]), sb("wu", [P, 2, KD, FE])
        wd = sb("wd", [P, 2, FT, D])
        tok = sb("tok", [P, 2], I32)
        xg = sb("xg", [P, 2, D])
        xT = sb("xT", [P, 2, KD, P])
        sg, hid = sb("silu", [P, FE]), sb("hid", [P, FE])
        hT = sb("hT", [P, FT, P])
        y = sb("y", [P, D])
        psX = ctx.enter_context(nc.psum_tensor(f"e{layer}_psX", [P, KD, P], F32))
        psG = ctx.enter_context(nc.psum_tensor(f"e{layer}_psG", [P, 2, FE], F32))
        psH = ctx.enter_context(nc.psum_tensor(f"e{layer}_psH", [P, FT, P], F32))
        psY = ctx.enter_context(nc.psum_tensor(f"e{layer}_psY", [P, 2, HALF], F32))
        s_w, s_wd = [sem("wgu_loaded0"), sem("wgu_loaded1")], [sem("wd_loaded0"), sem("wd_loaded1")]
        s_tok, s_x = [sem("tokens_loaded0"), sem("tokens_loaded1")], [sem("rows_gathered0"), sem("rows_gathered1")]
        s_ask, s_xt, s_xT, s_gu, s_silu, s_hid, s_ht, s_hT, s_y, s_out, s_st = (sem(x) for x in (
            "tokens_known", "rows_turned", "xT_ready", "gate_up_summed", "silu_ready", "hidden_ready", "hidden_turned", "hT_ready",
            "down_summed", "y_out", "y_stored"))
        block = ctx.enter_context(nc.Block())

        def slots(eng, body):
            with eng.Fori(0, SLOTS // 2) as i:
                for par in range(2):
                    body(i * 2 + par, par, i)

        @block.sync
        def _(sp):
            def load(b, par, i):
                e = sp.value_load(g.slot_expert[0:1, bass.ds(b, 1)], min_val=0, max_val=E - 1) + layer * E
                sp.wait_ge(s_gu, b + 1)
                for w, src in ((wg, g.e_gate), (wu, g.e_up)):
                    sp.dma_start(w[:, par, :, :], src[bass.ds(e, 1)].rearrange("o (k p) f -> p (o k) f", p=P)
                                 ).then_inc(s_w[par], 16)
                sp.wait_ge(s_y, b + 1)
                sp.dma_start(wd[:, par, :, :], g.e_down[bass.ds(e, 1)].rearrange("o (k p) f -> p (o k) f", p=P)
                             ).then_inc(s_wd[par], 16)

            slots(sp, load)

        @block.gpsimd
        def _(po):
            def gather(b, par, i):
                po.wait_ge(s_xt, b + 1)
                po.dma_start(tok[:, par:par + 1], g.slot_token[bass.ds(b * P, P), :]).then_inc(s_tok[par], 16)
                po.wait_ge(s_tok[par], 16 * i + 16)
                po.sem_inc(s_ask, 1)
                nc.gpsimd.indirect_dma_start(xg[:, par, :], None, g.h2,
                                             bass.IndirectOffsetOnAxis(tok[:, par:par + 1], axis=0)
                                             ).then_inc(s_x[par], 16)

            slots(po, gather)

        @block.tensor
        def _(pe):
            T = nc.tensor
            pe.sem_inc(s_xt, 2)
            pe.sem_inc(s_gu, 2)
            pe.sem_inc(s_y, 2)

            def turn(b, par, i):
                pe.wait_ge(s_x[par], 16 * i + 16)
                pe.wait_ge(s_xT, b + 1)
                for k in range(KD):
                    mm = T.transpose(psX[:, k, :], xg[:, par, k * P:(k + 1) * P], g.ident[:])
                mm.then_inc(s_xt, 1)

            def hidden(b, par, i):
                pe.wait_ge(s_w[par], 32 * i + 32)
                pe.wait_ge(s_xT, b + 2)
                pe.wait_ge(s_hid, b + 1)
                for z, w in enumerate((wg, wu)):
                    for k in range(KD):
                        mm = T.matmul(psG[:, z, :], xT[:, par, k, :], w[:, par, k, :],
                                      start=(k == 0), stop=(k == KD - 1))
                mm.then_inc(s_gu, 1)

            def down(b, par, i):
                pe.wait_ge(s_hid, b + 2)
                for f in range(FT):
                    mm = T.transpose(psH[:, f, :], hid[:, f * P:(f + 1) * P], g.ident[:])
                mm.then_inc(s_ht, 1)
                pe.wait_ge(s_wd[par], 16 * i + 16)
                pe.wait_ge(s_hT, b + 1)
                pe.wait_ge(s_out, b + 1)
                for c in range(2):
                    for f in range(FT):
                        mm = T.matmul(psY[:, c, :], hT[:, f, :], wd[:, par, f, c * HALF:(c + 1) * HALF],
                                      start=(f == 0), stop=(f == FT - 1))
                mm.then_inc(s_y, 1)

            def slot(b, par, i, more=True):
                hidden(b, par, i)
                if more:
                    turn(b + 1, 1 - par, i + par)
                down(b, par, i)

            turn(0, 0, 0)
            with pe.Fori(0, SLOTS // 2 - 1) as i:
                slot(i * 2, 0, i)
                slot(i * 2 + 1, 1, i)
            slot(SLOTS - 2, 0, SLOTS // 2 - 1)
            slot(SLOTS - 1, 1, SLOTS // 2 - 1, more=False)

        @block.scalar
        def _(act):
            S = nc.scalar
            act.sem_inc(s_xT, 1)

            def copy_x(b, par):
                act.wait_ge(s_xt, b + 3)
                act.wait_ge(s_gu, b + 1)
                for z in range(2):
                    S.copy(xT[:, par, z * 4:z * 4 + 4, :], psX[:, z * 4:z * 4 + 4, :])
                act.drain()
                act.sem_inc(s_xT, 1)

            def silu(b):
                act.wait_ge(s_gu, b + 3)
                act.wait_ge(s_hid, b + 1)
                S.activation(sg[:], psG[:, 0, :], ACT.Silu).then_inc(s_silu, 1)

            def store(b):
                act.wait_ge(s_out, b + 2)
                act.dma_start(g.yrows[bass.ds(b * P, P), :], y[:]).then_inc(s_st, 16)

            def slot(b, par, more=True):
                silu(b)
                if more:
                    copy_x(b + 1, 1 - par)
                store(b)

            copy_x(0, 0)
            with act.Fori(0, SLOTS // 2 - 1) as i:
                slot(i * 2, 0)
                slot(i * 2 + 1, 1)
            slot(SLOTS - 2, 0)
            slot(SLOTS - 1, 1, more=False)

        @block.vector
        def _(v):
            V = nc.vector
            v.sem_inc(s_hid, 1)
            v.sem_inc(s_out, 1)

            def step(b, par, i):
                v.wait_ge(s_silu, b + 1)
                V.tensor_tensor(hid[:], sg[:], psG[:, 1, :], ALU.mult).then_inc(s_hid, 1)
                v.wait_ge(s_ht, b + 1)
                V.tensor_copy(hT[:], psH[:]).then_inc(s_hT, 1)
                v.wait_ge(s_y, b + 3)
                v.wait_ge(s_st, 16 * b + 16)
                V.tensor_copy(y[:], psY[:].rearrange("p a c -> p (a c)")).then_inc(s_out, 1)

            v.sem_inc(s_st, 16)
            slots(v, step)
            v.wait_ge(s_st, 16 * SLOTS + 16)


def stage_combine(nc, g, layer, last):
    with nc.cleanup_on_exit(), ExitStack() as ctx:
        def sb(n, s, d=F32):
            return ctx.enter_context(nc.sbuf_tensor(f"c{layer}_{n}", s, d))

        def sem(n):
            return nc.alloc_semaphore(f"c{layer}_{n}")

        w = Shared()
        w.z, w.stats, w.mv, w.sd = sb("z", [P, D]), sb("stats", [P, 2, 6]), sb("mv", [P, 2]), sb("sd", [P, 1])
        w.g, lb, gate = sb("lg", [P, D]), sb("lb", [P, D]), sb("gate", [P, 2, D])
        ya, yb = sb("ya", [P, 2, D]), sb("yb", [P, 2, D])
        s_ld, s_mods, s_var, s_sd, s_used, s_x, s_st = (sem(x) for x in (
            "side_loaded", "mods_loaded", "variance", "deviation", "rows_used", "x_ready", "y_stored"))
        s_g = [sem("rows_gathered0"), sem("rows_gathered1")]
        block = ctx.enter_context(nc.Block())

        @block.sync
        def _(sp):
            r = 2 * layer + 1
            sp.dma_start(w.g[:], g.ln_g[r:r + 1, :].broadcast_to([P, D])).then_inc(s_ld, 16)
            sp.dma_start(lb[:], g.ln_b[r:r + 1, :].broadcast_to([P, D])).then_inc(s_ld, 16)
            load_mods(sp, g, gate[:, 0, :], layer, GATE2, False, s_mods)
            load_mods(sp, g, gate[:, 1, :], layer, GATE2, True, s_mods)
            if last:
                with sp.Fori(0, PT) as t:
                    sp.wait_ge(s_x, t + 1)
                    sp.dma_start(g.y_prompt[bass.ds(t * P, P), :],
                                 g.x[:, bass.ds(t, 1), :].rearrange("p o d -> p (o d)")).then_inc(s_st, 16)
                sp.wait_ge(s_x, TILES)
                sp.dma_start(g.y_sample, g.x[0:NSAMP, PT, :]).then_inc(s_st, 16)
                sp.wait_ge(s_st, 16 * TILES)

        @block.gpsimd
        def _(po):
            for t in range(TILES):
                n, par = rows_of(t), t % 2
                if t >= 2:
                    po.wait_ge(s_used, t - 1)
                for k, y in enumerate((ya, yb)):
                    nc.gpsimd.indirect_dma_start(y[0:n, par, :], None, g.yrows,
                                                 bass.IndirectOffsetOnAxis(g.dest[0:n, k, t:t + 1], axis=0)
                                                 ).then_inc(s_g[par], 16)

        @block.scalar
        def _(act):
            for t in range(TILES):
                n = rows_of(t)
                act.wait_ge(s_var, t + 1)
                nc.scalar.activation(w.sd[0:n, :], w.sd[0:n, :], ACT.Sqrt)
                act.drain()
                act.sem_inc(s_sd, 1)

        @block.vector
        def _(v):
            V = nc.vector
            v.wait_ge(s_ld, 32)
            v.wait_ge(s_mods, 16 + 16 * BATCHES)
            for t in range(TILES):
                n, par = rows_of(t), t % 2
                z, x = w.z[0:n, :], g.x[0:n, t, :]
                v.wait_ge(s_g[par], 32 * (t // 2) + 32)
                V.tensor_scalar(z, ya[0:n, par, :], g.weight[0:n, 0, t:t + 1], None, ALU.mult)
                v.drain()
                V.scalar_tensor_tensor(out=z, in0=yb[0:n, par, :], scalar=g.weight[0:n, 1, t:t + 1], in1=z,
                                       op0=ALU.mult, op1=ALU.add)
                v.drain()
                v.sem_inc(s_used, 1)
                V.tensor_tensor(z, z, gate[0:n, t // PT, :], ALU.mult)
                v.drain()
                V.scalar_tensor_tensor(out=z, in0=x, scalar=ALPHA, in1=z, op0=ALU.mult, op1=ALU.add)
                v.drain()
                norm_steps(nc, v, w, n, s_var, s_sd, t + 1)
                V.tensor_tensor(x, z, lb[0:n, :], ALU.add)
                v.drain()
                v.sem_inc(s_x, 1)


def stage_latents(nc, g):
    with nc.cleanup_on_exit(), ExitStack() as ctx:
        def sb(n, s, d=F32):
            return ctx.enter_context(nc.sbuf_tensor(f"l_{n}", s, d))

        def sem(n):
            return nc.alloc_semaphore(f"l_{n}")

        KVA = KVR + ROPE
        half = ROPE // 2
        wkv, wdq = sb("wkv", [P, KD, KVA]), sb("wdq", [P, KD, QR])
        scale, shift = sb("scale", [P, 2, D]), sb("shift", [P, 2, D])
        trig = sb("trig", [P, TILES, 2, half])
        gkv, gq = sb("gkv", [P, KVR]), sb("gq", [P, QR])
        h, xrow = sb("h", [P, D]), sb("xrow", [P, D])
        xT, hT = sb("xT", [P, KD, P]), sb("hT", [P, KD, P])
        junk = sb("junk", [P, QR])
        ss, rs = sb("ss", [P, 2]), sb("rs", [P, 2])
        lat, kr, cq = sb("lat", [P, 2, KVR]), sb("kr", [P, 2, 2, ROPE]), sb("cq", [P, QR])
        r4 = sb("r4", [P, 4, half])
        psT = ctx.enter_context(nc.psum_tensor("l_psT", [P, 2 * KD, P], F32))
        psK = ctx.enter_context(nc.psum_tensor("l_psK", [P, HALF], F32))
        psQ = ctx.enter_context(nc.psum_tensor("l_psQ", [P, HALF], F32))
        psC = ctx.enter_context(nc.psum_tensor("l_psC", [P, 4, P], F32))
        psL = ctx.enter_context(nc.psum_tensor("l_psL", [P, 4, P], F32))
        s_ld, s_mods, s_h, s_T, s_xT, s_mm, s_ss, s_ms, s_sd, s_nrm, s_post, s_out = (sem(x) for x in (
            "side_loaded", "mods_loaded", "h_ready", "turned", "xT_ready", "projected", "squares_summed",
            "mean_squares", "roots", "normalised", "latents_turned", "latents_out"))
        s_st = [sem("rows_stored0"), sem("rows_stored1")]
        block = ctx.enter_context(nc.Block())

        @block.sync
        def _(sp):
            sp.dma_start(wkv[:], g.w_kv_a.rearrange("(k p) n -> p k n", p=P)).then_inc(s_ld, 16)
            sp.dma_start(wdq[:], g.w_dq.rearrange("(k p) n -> p k n", p=P)).then_inc(s_ld, 16)
            sp.dma_start(gkv[:], g.kv_norm_g.broadcast_to([P, KVR])).then_inc(s_ld, 16)
            sp.dma_start(gq[:], g.q_norm_g.broadcast_to([P, QR])).then_inc(s_ld, 16)
            sp.dma_start(trig[:], g.const["trig_tok"]).then_inc(s_ld, 16)
            for z in range(2):
                load_mods(sp, g, shift[:, z, :], 1, SHIFT1, bool(z), s_mods)
                load_mods(sp, g, scale[:, z, :], 1, SCALE1, bool(z), s_mods)

            def store(t, par, n):
                sp.wait_ge(s_nrm, t + 1)
                sp.dma_start(g.lat[bass.ds(t * P, n), :], lat[0:n, par, :]).then_inc(s_st[par], 16)
                sp.dma_start(g.krope[bass.ds(t * P, n), :], kr[0:n, par, 0, :]).then_inc(s_st[par], 16)

            with sp.Fori(0, PT // 2) as i:
                for par in range(2):
                    store(i * 2 + par, par, P)
            store(PT, 0, NSAMP)
            sp.wait_ge(s_st[0], 32 * (PT // 2 + 1) + 32)
            sp.wait_ge(s_st[1], 32 * (PT // 2) + 32)

        @block.tensor
        def _(pe):
            T = nc.tensor
            pe.sem_inc(s_T, 1)
            pe.wait_ge(s_ld, 80)

            def project(t, n):
                pe.wait_ge(s_h, t + 1)
                pe.wait_ge(s_xT, t + 1)
                for k in range(KD):
                    T.transpose(psT[:, k, 0:n], xrow[0:n, k * P:(k + 1) * P], g.ident[0:n, 0:n])
                for k in range(KD):
                    mm = T.transpose(psT[:, KD + k, 0:n], h[0:n, k * P:(k + 1) * P], g.ident[0:n, 0:n])
                mm.then_inc(s_T, 1)
                pe.wait_ge(s_xT, t + 2)
                if not (isinstance(t, int) and t == 0):
                    pe.wait_ge(s_nrm, t)
                for k in range(KD):
                    T.matmul(psK[0:n, 0:KVA], xT[:, k, 0:n], wkv[:, k, :], start=(k == 0), stop=(k == KD - 1))
                for k in range(KD):
                    mm = T.matmul(psQ[0:n, :], hT[:, k, 0:n], wdq[:, k, :], start=(k == 0), stop=(k == KD - 1))
                mm.then_inc(s_mm, 1)

            def turn_latents(t, par, n):
                pe.wait_ge(s_nrm, t + 1)
                pe.wait_ge(s_out, t + 1)
                for k in range(4):
                    T.transpose(psC[:, k, 0:n], cq[0:n, k * P:(k + 1) * P], g.ident[0:n, 0:n])
                for k in range(2):
                    T.transpose(psL[:, k, 0:n], lat[0:n, par, k * P:(k + 1) * P], g.ident[0:n, 0:n])
                T.transpose(psL[:, 2, 0:n], kr[0:n, par, :, :].rearrange("p a r -> p (a r)"),
                            g.ident[0:n, 0:n]).then_inc(s_post, 1)

            project(0, P)
            with pe.Fori(0, PT // 2 - 1) as i:
                for par in range(2):
                    t = i * 2 + par
                    project(t + 1, P)
                    turn_latents(t, par, P)
            project(PT - 1, P)
            turn_latents(PT - 2, 0, P)
            project(PT, NSAMP)
            turn_latents(PT - 1, 1, P)
            turn_latents(PT, 0, NSAMP)

        @block.scalar
        def _(act):
            S = nc.scalar
            act.sem_inc(s_xT, 1)
            act.sem_inc(s_out, 1)

            def front(t, n):
                act.wait_ge(s_T, t + 2)
                if not (isinstance(t, int) and t == 0):
                    act.wait_ge(s_mm, t)
                for z in range(2):
                    S.copy(xT[:, z * 4:z * 4 + 4, 0:n], psT[:, z * 4:z * 4 + 4, 0:n])
                    S.copy(hT[:, z * 4:z * 4 + 4, 0:n], psT[:, KD + z * 4:KD + z * 4 + 4, 0:n])
                act.drain()
                act.sem_inc(s_xT, 1)
                act.wait_ge(s_mm, t + 1)
                S.activation(junk[0:n, 0:KVR], psK[0:n, 0:KVR], ACT.Square, accum_out=ss[0:n, 0:1])
                act.drain()
                S.activation(junk[0:n, :], psQ[0:n, :], ACT.Square, accum_out=ss[0:n, 1:2])
                act.drain()
                act.sem_inc(s_ss, 1)
                act.wait_ge(s_ms, t + 1)
                S.activation(rs[0:n, :], rs[0:n, :], ACT.Sqrt)
                act.drain()
                act.sem_inc(s_sd, 1)

            def back(t, n):
                act.wait_ge(s_post, t + 1)
                S.copy(g.cqT[:, :, bass.ds(t * P, n)], psC[:, :, 0:n])
                S.copy(g.latT[:, :, bass.ds(t * P, n)], psL[:, 0:2, 0:n])
                S.copy(g.krT[:, bass.ds(t * P, n)], psL[:, 2, 0:n])
                act.drain()
                act.sem_inc(s_out, 1)

            front(0, P)
            with act.Fori(0, PT - 1) as t:
                front(t + 1, P)
                back(t, P)
            front(PT, NSAMP)
            back(PT - 1, P)
            back(PT, NSAMP)

        @block.vector
        def _(v):
            V = nc.vector
            v.sem_inc(s_st[0], 32)
            v.sem_inc(s_st[1], 32)
            v.wait_ge(s_ld, 80)
            v.wait_ge(s_mods, 32 + 32 * BATCHES)

            def modulate(t, n, z):
                x = g.x[0:n, bass.ds(t, 1), :].rearrange("p o d -> p (o d)")
                v.wait_ge(s_T, t + 1)
                V.tensor_copy(xrow[0:n, :], x)
                V.scalar_tensor_tensor(out=h[0:n, :], in0=scale[0:n, z, :], scalar=1.0, in1=x,
                                       op0=ALU.add, op1=ALU.mult)
                v.drain()
                V.tensor_tensor(h[0:n, :], h[0:n, :], shift[0:n, z, :], ALU.add)
                v.drain()
                v.sem_inc(s_h, 1)

            def normalise(t, par, i, n):
                v.wait_ge(s_ss, t + 1)
                V.tensor_scalar(rs[0:n, 0:1], ss[0:n, 0:1], 1.0 / KVR, EPS, ALU.mult, ALU.add)
                V.tensor_scalar(rs[0:n, 1:2], ss[0:n, 1:2], 1.0 / QR, EPS, ALU.mult, ALU.add)
                v.drain()
                v.sem_inc(s_ms, 1)
                v.wait_ge(s_st[par], 32 * i + 32)
                if not (isinstance(t, int) and t == 0):
                    v.wait_ge(s_post, t)
                c = trig[0:n, bass.ds(t, 1), 0, :].rearrange("p o r -> p (o r)")
                s = trig[0:n, bass.ds(t, 1), 1, :].rearrange("p o r -> p (o r)")
                a, b = psK[0:n, KVR:KVR + half], psK[0:n, KVR + half:KVA]
                V.tensor_tensor(r4[0:n, 0, :], a, c, ALU.mult)
                V.tensor_tensor(r4[0:n, 1, :], b, s, ALU.mult)
                V.tensor_tensor(r4[0:n, 2, :], a, s, ALU.mult)
                V.tensor_tensor(r4[0:n, 3, :], b, c, ALU.mult)
                v.drain()
                for z in range(2):
                    V.tensor_tensor(kr[0:n, par, z, 0:half], r4[0:n, 0, :], r4[0:n, 1, :], ALU.subtract)
                    V.tensor_tensor(kr[0:n, par, z, half:ROPE], r4[0:n, 2, :], r4[0:n, 3, :], ALU.add)
                v.wait_ge(s_sd, t + 1)
                V.reciprocal(rs[0:n, :], rs[0:n, :])
                v.drain()
                V.scalar_tensor_tensor(out=lat[0:n, par, :], in0=psK[0:n, 0:KVR], scalar=rs[0:n, 0:1],
                                       in1=gkv[0:n, :], op0=ALU.mult, op1=ALU.mult)
                V.scalar_tensor_tensor(out=cq[0:n, :], in0=psQ[0:n, :], scalar=rs[0:n, 1:2], in1=gq[0:n, :],
                                       op0=ALU.mult, op1=ALU.mult)
                v.drain()
                v.sem_inc(s_nrm, 1)

            modulate(0, P, 0)
            with v.Fori(0, PT // 2 - 1) as i:
                for par in range(2):
                    t = i * 2 + par
                    modulate(t + 1, P, 0)
                    normalise(t, par, i, P)
            modulate(PT - 1, P, 0)
            normalise(PT - 2, 0, PT // 2 - 1, P)
            modulate(PT, NSAMP, 1)
            normalise(PT - 1, 1, PT // 2 - 1, P)
            normalise(PT, 0, PT // 2, NSAMP)


def stage_heads(nc, g):
    with nc.cleanup_on_exit(), ExitStack() as ctx:
        def sb(n, s, d=F32):
            return ctx.enter_context(nc.sbuf_tensor(f"a_{n}", s, d))

        def sem(n):
            return nc.alloc_semaphore(f"a_{n}")

        wq, wk = sb("wq", [P, 4, 2 * P]), sb("wk", [P, 2, NOPE])
        wkT, wv = sb("wkT", [P, KVR]), sb("wv", [P, 2, DV])
        trig = sb("trig", [P, N])
        qn, qr, kT = sb("qn", [P, N]), sb("qr", [P, N]), sb("kT", [P, SEQ])
        vv = sb("v", [P, PT, DV])
        pb = sb("p", [P, 2, SEQ])
        pT = sb("pT", [P, PT, P])
        nm, rsum, rinv = sb("nm", [P, 2]), sb("rsum", [P, 2]), sb("rinv", [P, 2])
        psS = ctx.enter_context(nc.psum_tensor("a_psS", [P, 2, SEQ], F32))
        psP = ctx.enter_context(nc.psum_tensor("a_psP", [P, PT, P], F32))
        psJ = ctx.enter_context(nc.psum_tensor("a_psJ", [P, 2, HALF], F32))
        s_c, s_w, s_job, s_ja, s_jv, s_S, s_max, s_exp, s_nrm, s_T, s_pT, s_o = (sem(x) for x in (
            "trig_loaded", "weights_loaded", "job_summed", "jobs_out_act", "jobs_out_dve", "scores", "maxima",
            "exp_ready", "weights_ready", "weights_turned", "pT_ready", "outputs_summed"))
        block = ctx.enter_context(nc.Block())

        RUNS = ((0, HALF), (HALF, HALF), (SEQ, NSAMP))
        JOBS = 11
        ACT_JOBS = 8 + PT

        @block.sync
        def _(sp):
            sp.dma_start(trig[:], g.const["trig_feat"]).then_inc(s_c, 16)
            with sp.Fori(0, H) as h:
                sp.wait_ge(s_job, JOBS * h + JOBS)
                for dst, src in ((wq[:].rearrange("p k n -> p (k n)"), g.w_uq), (wk[:].rearrange("p k n -> p (k n)"), g.w_uk),
                                 (wkT[:], g.w_ukT), (wv[:].rearrange("p k n -> p (k n)"), g.w_uv)):
                    sp.dma_start(dst, src[bass.ds(h, 1)].rearrange("o p n -> (o p) n")).then_inc(s_w, 16)

        @block.tensor
        def _(pe):
            T = nc.tensor
            pe.sem_inc(s_job, JOBS)
            pe.wait_ge(s_c, 16)
            with pe.Fori(0, H) as h:
                A = h * ACT_JOBS + ACT_JOBS
                pe.wait_ge(s_w, 64 * h + 64)
                for r, (lo, n) in enumerate(RUNS):
                    for z in range(2):
                        if z == 0:
                            pe.wait_ge(s_ja, A + r)
                        elif r == 0:
                            pe.wait_ge(s_ja, A - 1)
                        else:
                            pe.wait_ge(s_jv, 3 * h + r)
                        for k in range(4):
                            mm = T.matmul(psJ[:, z, 0:n], wq[:, k, z * P:(z + 1) * P], g.cqT[:, k, lo:lo + n],
                                          start=(k == 0), stop=(k == 3))
                        mm.then_inc(s_job, 1)
                for c in range(2):
                    if c == 0:
                        pe.wait_ge(s_ja, A + 3)
                    else:
                        pe.wait_ge(s_jv, 3 * h + 3)
                    for k in range(2):
                        mm = T.matmul(psJ[:, c, :], wk[:, k, :], g.latT[:, k, c * HALF:(c + 1) * HALF],
                                      start=(k == 0), stop=(k == 1))
                    mm.then_inc(s_job, 1)
                for c in range(2):
                    pe.wait_ge(s_ja, A + 4 + c)
                    for j in range(4):
                        for k in range(2):
                            mm = T.matmul(psJ[:, c, j * DV:(j + 1) * DV],
                                          g.latT[:, k, (c * 4 + j) * P:(c * 4 + j + 1) * P], wv[:, k, :],
                                          start=(k == 0), stop=(k == 1))
                    mm.then_inc(s_job, 1)
                pe.wait_ge(s_ja, A + 6)
                for c in range(2):
                    mm = T.matmul(psJ[:, 0, c * NSAMP:(c + 1) * NSAMP], wkT[:, c * P:(c + 1) * P], qn[:, SEQ:N],
                                  start=True, stop=True)
                mm.then_inc(s_job, 1)

                def scores(i):
                    par, width = i % 2, (i + 1) * P
                    pe.wait_ge(s_exp, h * PT + i + 1)
                    q = slice(i * P, (i + 1) * P)
                    for lo in range(0, width, HALF):
                        hi = min(width, lo + HALF)
                        T.matmul(psS[:, par, lo:hi], qn[:, q], kT[:, lo:hi], start=True, stop=False)
                        last = hi == width
                        mm = T.matmul(psS[:, par, lo:hi], qr[:, q], g.krT[:, lo:hi], start=False, stop=not last)
                        if last:
                            mm = T.matmul(psS[:, par, i * P:width], g.ident[:], g.qmask[:], start=False, stop=True)
                    mm.then_inc(s_S, 1)

                pe.wait_ge(s_ja, A + 7)
                pe.wait_ge(s_jv, 3 * h + 3)
                scores(0)
                for i in range(PT):
                    if i + 1 < PT:
                        scores(i + 1)
                    pe.wait_ge(s_nrm, h * PT + i + 1)
                    pe.wait_ge(s_pT, h * PT + i + 1)
                    for j in range(i + 1):
                        mm = T.transpose(psP[:, j, :], pb[:, i % 2, j * P:(j + 1) * P], g.ident[:])
                    mm.then_inc(s_T, 1)
                    pe.wait_ge(s_pT, h * PT + i + 2)
                    pe.wait_ge(s_ja, A + 7 + i)
                    for j in range(i + 1):
                        mm = T.matmul(psJ[:, (i + 1) % 2, 0:P], vv[:, j, :], pT[:, j, :], start=(j == 0), stop=(j == i))
                    mm.then_inc(s_o, 1)

        @block.scalar
        def _(act):
            S = nc.scalar
            act.sem_inc(s_ja, ACT_JOBS)
            act.sem_inc(s_exp, 2)
            act.sem_inc(s_pT, 1)
            with act.Fori(0, H) as h:
                J = JOBS * h + JOBS
                for r, (lo, n) in enumerate(RUNS):
                    act.wait_ge(s_job, J + 2 * r + 1)
                    S.copy(qn[:, lo:lo + n], psJ[:, 0, 0:n]).then_inc(s_ja, 1)
                for c in range(2):
                    act.wait_ge(s_job, J + 7 + c)
                    S.copy(kT[:, c * HALF:(c + 1) * HALF], psJ[:, c, :]).then_inc(s_ja, 1)
                for c in range(2):
                    act.wait_ge(s_job, J + 9 + c)
                    S.copy(vv[:, c * 4:c * 4 + 4, :], psJ[:, c, :].rearrange("p (j v) -> p j v", j=4)).then_inc(s_ja, 1)
                act.wait_ge(s_job, J + 11)
                act.wait_ge(s_jv, 3 * h + 3)
                for z in range(3):
                    src = psJ[:, 0, z * NSAMP:(z + 1) * NSAMP] if z < 2 else qr[:, SEQ:N]
                    S.copy(g.qS[:, z, :, bass.ds(h, 1), :].rearrange("p b o t -> p b (o t)"),
                           src.rearrange("p (b t) -> p b t", b=BATCHES))
                act.drain()
                act.sem_inc(s_ja, 1)

                def exp(i):
                    par, width = i % 2, (i + 1) * P
                    act.wait_ge(s_max, h * PT + i + 1)
                    act.wait_ge(s_T, h * PT + i + 1)
                    S.activation(pb[:, par, 0:width], psS[:, par, 0:width], ACT.Exp, bias=nm[:, par:par + 1],
                                 scale=SCALE, accum_out=rsum[:, par:par + 1])
                    act.drain()
                    act.sem_inc(s_exp, 1)

                def output(i):
                    act.wait_ge(s_o, h * PT + i + 2)
                    S.copy(g.mixT[:, bass.ds(h, 1), i * P:(i + 1) * P].rearrange("p o t -> p (o t)"),
                           psJ[:, (i + 1) % 2, 0:P]).then_inc(s_ja, 1)

                exp(0)
                for i in range(PT):
                    if i + 1 < PT:
                        exp(i + 1)
                    act.wait_ge(s_T, h * PT + i + 3)
                    act.wait_ge(s_o, h * PT + i + 1)
                    for lo in range(0, i + 1, 4):
                        hi = min(i + 1, lo + 4)
                        S.copy(pT[:, lo:hi, :], psP[:, lo:hi, :])
                    act.drain()
                    act.sem_inc(s_pT, 1)
                    if i >= 1:
                        output(i - 1)
                output(PT - 1)

        @block.vector
        def _(v):
            V = nc.vector
            v.sem_inc(s_T, 2)
            v.sem_inc(s_o, 1)
            v.wait_ge(s_c, 16)
            with v.Fori(0, H) as h:
                for r, (lo, n) in enumerate(RUNS):
                    v.wait_ge(s_job, JOBS * h + JOBS + 2 * r + 2)
                    V.tensor_tensor(qr[:, lo:lo + n], psJ[:, 1, 0:n], trig[:, lo:lo + n], ALU.mult).then_inc(s_jv, 1)

                def maximum(i):
                    par, width = i % 2, (i + 1) * P
                    v.wait_ge(s_S, h * PT + i + 1)
                    V.tensor_reduce(nm[:, par:par + 1], psS[:, par, 0:width], AX, ALU.max)
                    v.drain()
                    V.tensor_scalar(nm[:, par:par + 1], nm[:, par:par + 1], -SCALE, None, ALU.mult)
                    v.drain()
                    v.sem_inc(s_max, 1)

                maximum(0)
                for i in range(PT):
                    if i + 1 < PT:
                        maximum(i + 1)
                    par, width = i % 2, (i + 1) * P
                    v.wait_ge(s_exp, h * PT + i + 3)
                    V.reciprocal(rinv[:, par:par + 1], rsum[:, par:par + 1])
                    v.drain()
                    V.tensor_scalar(pb[:, par, 0:width], pb[:, par, 0:width], rinv[:, par:par + 1], None, ALU.mult)
                    v.drain()
                    v.sem_inc(s_nrm, 1)


def stage_sample(nc, g):
    NQ = H * STEPS
    with nc.cleanup_on_exit(), ExitStack() as ctx:
        def sb(n, s, d=F32):
            return ctx.enter_context(nc.sbuf_tensor(f"s_{n}", s, d))

        def sem(n):
            return nc.alloc_semaphore(f"s_{n}")

        pt = sb("page_table", [1, BATCHES * PAGES], I32)
        kv = sb("pages", [P, 2, PAGES, KVW])
        new = sb("new", [STEPS, 2, KVR])
        qB = sb("q", [P, 2, 3, NQ])
        pb = sb("p", [NQ, CTX])
        pT = sb("pT", [P, PAGES + 1, NQ])
        wv = sb("wv", [P, H, 2 * DV])
        oS = sb("o", [P, 2, BATCHES, NQ])
        nm, rsum = sb("nm", [NQ, 1]), sb("rsum", [NQ, 2])
        psS = ctx.enter_context(nc.psum_tensor("s_psS", [P, 5 * HALF], F32))
        psP = ctx.enter_context(nc.psum_tensor("s_psP", [P, PAGES, NQ], F32))
        psO = ctx.enter_context(nc.psum_tensor("s_psO", [P, HALF], F32))
        s_pt, s_wv, s_q, s_S, s_max, s_exp, s_nrm, s_T, s_pT, s_o, s_oS, s_fin, s_new = (sem(x) for x in (
            "table_loaded", "wv_loaded", "queries_staged", "scores", "maximum", "exp_ready", "weights_ready",
            "weights_turned", "pT_ready", "outputs_summed", "outputs_kept", "values_summed", "new_loaded"))
        s_kv = [sem("pages_loaded0"), sem("pages_loaded1")]
        s_turning = sem("turning")
        block = ctx.enter_context(nc.Block())

        @block.sync
        def _(sp):
            sp.dma_start(pt[:], g.page_table).then_inc(s_pt, 16)
            sp.dma_start(wv[:], g.w_uv.rearrange("h p n -> p h n")).then_inc(s_wv, 16)
            sp.wait_ge(s_pt, 16)
            with sp.Fori(0, BATCHES // 2) as i:
                for par in range(2):
                    b = i * 2 + par
                    sp.wait_ge(s_o, b + 1)
                    for j in range(PAGES):
                        page = sp.value_load(pt[0:1, bass.ds(b * PAGES + j, 1)], min_val=0, max_val=g.cache.shape[0] - 1)
                        sp.dma_start(kv[:, par, j, :], g.cache[bass.ds(page, 1)].rearrange("o p n -> (o p) n")
                                     ).then_inc(s_kv[par], 16)
                    sp.dma_start(new[:, par, :], g.lat[bass.ds(SEQ + b * STEPS, STEPS), :]).then_inc(s_kv[par], 16)

        @block.gpsimd
        def _(po):
            with po.Fori(0, BATCHES // 2) as i:
                for par in range(2):
                    b = i * 2 + par
                    po.wait_ge(s_o, b + 1)
                    nc.gpsimd.tensor_copy(qB[:, par, :, :],
                                          g.qS[:, :, bass.ds(b, 1), :, :].rearrange("p z o h t -> p z (o h t)"))
                    po.drain()
                    po.sem_inc(s_q, 1)

        @block.tensor
        def _(pe):
            T = nc.tensor
            pe.sem_inc(s_o, 2)
            with pe.Fori(0, BATCHES // 2) as i:
                for par in range(2):
                    b = i * 2 + par
                    pe.wait_ge(s_q, b + 1)
                    pe.wait_ge(s_kv[par], 16 * (PAGES + 1) * (i + 1))
                    pe.wait_ge(s_exp, b + 1)
                    for c in range(4):
                        for z in range(3):
                            T.matmul(psS[0:NQ, c * HALF:(c + 1) * HALF], qB[:, par, z, :],
                                     kv[:, par, c * 4:c * 4 + 4, z * PAGE:(z + 1) * PAGE],
                                     start=(z == 0), stop=(z == 2))
                    cols = bass.ds(SEQ + b * STEPS, STEPS)
                    for z in range(2):
                        T.matmul(psS[0:NQ, PAST:CTX], qB[:, par, z, :],
                                 g.latT[:, z, cols], start=(z == 0), stop=False)
                    T.matmul(psS[0:NQ, PAST:CTX], qB[:, par, 2, :], g.krT[:, cols], start=False, stop=False)
                    T.matmul(psS[0:NQ, PAST:CTX], g.ident[0:NQ, 0:NQ], g.smask[0:NQ, :],
                             start=False, stop=True).then_inc(s_S, 1)
                    pe.wait_ge(s_nrm, b + 1)
                    pe.wait_ge(s_oS, b + 1)
                    pe.sem_inc(s_turning, 1)
                    for j in range(PAGES):
                        T.transpose(psP[:, j, :], pb[:, j * PAGE:(j + 1) * PAGE], g.ident[0:NQ, 0:NQ])
                    T.transpose(psO[0:STEPS, 2 * NQ:3 * NQ], pb[:, PAST:CTX], g.ident[0:NQ, 0:NQ]).then_inc(s_T, 1)
                    pe.wait_ge(s_pT, b + 1)
                    for c in range(2):
                        v0 = 3 * PAGE + c * P
                        for j in range(PAGES):
                            T.matmul(psO[:, c * NQ:(c + 1) * NQ], kv[:, par, j, v0:v0 + P], pT[:, j, :],
                                     start=(j == 0), stop=False)
                        mm = T.matmul(psO[:, c * NQ:(c + 1) * NQ], new[:, par, c * P:(c + 1) * P],
                                      pT[0:STEPS, PAGES, :], start=False, stop=True)
                    mm.then_inc(s_o, 1)
            pe.wait_ge(s_oS, BATCHES + 1)
            pe.wait_ge(s_wv, 16)
            for h in range(H):
                for c in range(2):
                    mm = T.matmul(psO[:, h * NSAMP:(h + 1) * NSAMP], wv[:, h, c * DV:(c + 1) * DV],
                                  oS[:, c, :, h * STEPS:(h + 1) * STEPS], start=(c == 0), stop=(c == 1))
            mm.then_inc(s_fin, 1)

        @block.scalar
        def _(act):
            S = nc.scalar
            act.sem_inc(s_exp, 1)
            act.sem_inc(s_oS, 1)
            with act.Fori(0, BATCHES) as b:
                act.wait_ge(s_max, b + 1)
                act.wait_ge(s_T, b + 1)
                S.activation(pb[:], psS[0:NQ, 0:CTX], ACT.Exp, bias=nm[:], scale=SCALE, accum_out=rsum[:, 0:1])
                act.drain()
                act.sem_inc(s_exp, 1)
                act.wait_ge(s_T, b + 2)
                act.wait_ge(s_o, b + 2)
                for z in range(2):
                    S.copy(pT[:, z * 8:z * 8 + 8, :], psP[:, z * 8:z * 8 + 8, :])
                S.copy(pT[0:STEPS, PAGES, :], psO[0:STEPS, 2 * NQ:3 * NQ])
                act.drain()
                act.sem_inc(s_pT, 1)
                act.wait_ge(s_o, b + 3)
                S.copy(oS[:, :, bass.ds(b, 1), :].rearrange("p c o q -> p c (o q)"),
                       psO[:, 0:2 * NQ].rearrange("p (c q) -> p c q", c=2))
                act.drain()
                act.sem_inc(s_oS, 1)
            act.wait_ge(s_fin, 1)
            S.copy(g.mixT[:, :, SEQ:N], psO[:].rearrange("p (h t) -> p h t", h=H))

        @block.vector
        def _(v):
            V = nc.vector
            v.sem_inc(s_T, 1)
            with v.Fori(0, BATCHES) as b:
                v.wait_ge(s_S, b + 1)
                V.tensor_reduce(nm[:], psS[0:NQ, 0:CTX], AX, ALU.max)
                v.drain()
                V.tensor_scalar(nm[:], nm[:], -SCALE, None, ALU.mult)
                v.drain()
                v.sem_inc(s_max, 1)
                v.wait_ge(s_exp, b + 2)
                V.reciprocal(rsum[:, 1:2], rsum[:, 0:1])
                v.drain()
                V.tensor_scalar(pb[:], pb[:], rsum[:, 1:2], None, ALU.mult)
                v.drain()
                v.sem_inc(s_nrm, 1)


OUTPUTS = {
    "y_prompt": (SEQ, D), "y_sample": (NSAMP, D),
    "C_p": (P, PAIRS, AUG), "C_s": (P, BATCHES, PAIRS, AUG), "m_out": (H, 1 + BATCHES),
    "lat": (N, KVR), "krope": (N, ROPE),
}


def laid_out(inputs):
    a = {k: np.asarray(v) for k, v in inputs.items()}
    o = {}
    o["x_prompt"] = a["x_prompt"].reshape(SEQ, D)
    o["x_sample"] = a["x_sample"].reshape(NSAMP, D)
    c = np.concatenate([a["c_prompt"], a["c_sample"]], 0)
    o["cT"] = c.T.reshape(KD, P, 9).transpose(1, 0, 2).reshape(P, KD * 9)
    o["ada_w"] = a["ada_w"].reshape(2, KD, P, 12, HALF).transpose(0, 3, 2, 1, 4).reshape(24, P, KD * HALF)
    o["ada_b"] = a["ada_b"].reshape(24, HALF)
    o["ln_g"] = a["ln_g"].reshape(4, D)
    o["ln_b"] = a["ln_b"].reshape(4, D)
    o["a_w_in"] = a["a_w_in"][0]
    o["a_b_gates"] = a["a_b_gates"]
    o["a_norm_g"] = a["a_norm_g"]
    o["a_w_out"] = a["a_w_out"][0]
    st = np.concatenate([a["state_C"][0], a["state_n"][0][..., None]], -1)
    o["state"] = st.reshape(BATCHES, PAIRS, 2, DK, AUG).transpose(2, 3, 0, 1, 4).reshape(P, BATCHES, PAIRS, AUG)
    o["state_mT"] = a["state_m"][0].T
    o["w_kv_a"] = a["b_w_kv_a"]
    o["kv_norm_g"] = a["b_kv_norm_g"].reshape(1, KVR)
    o["q_norm_g"] = a["b_q_norm_g"]
    o["w_dq"] = a["b_w_dq"][0]
    uq = a["b_w_uq"][0].reshape(4, P, H, NOPE + ROPE)
    half = ROPE // 2
    uq = np.concatenate([uq, uq[..., NOPE + half:], uq[..., NOPE:NOPE + half]], -1)
    o["w_uq"] = uq.transpose(2, 1, 0, 3).reshape(H, P, 4 * 2 * P)
    uk, uv = a["b_w_uk"], a["b_w_uv"]
    o["w_uk"] = uk.reshape(2, P, H, NOPE).transpose(2, 1, 0, 3).reshape(H, P, 2 * NOPE)
    o["w_ukT"] = uk.transpose(1, 2, 0)
    o["w_uv"] = uv.reshape(2, P, H, DV).transpose(2, 1, 0, 3).reshape(H, P, 2 * DV)
    o["w_o"] = a["b_w_o"][0]
    o["router_w"] = a["router_w"]
    o["router_b"] = a["router_b"].reshape(1, E)
    for n in ("gate", "up", "down"):
        w = a[f"e_w_{n}"]
        o[f"e_{n}"] = w.reshape((2 * E,) + w.shape[2:])
    cl, ck = a["cache_latent"], a["cache_krope"]
    lt = cl.transpose(0, 2, 1).reshape(-1, 2, P, PAGE).transpose(0, 2, 1, 3).reshape(-1, P, 2 * PAGE)
    kt = ck.transpose(0, 2, 1)
    o["cache"] = np.concatenate([lt, np.concatenate([kt, kt], 1), cl], -1)
    o["page_table"] = a["page_table"].reshape(1, BATCHES * PAGES).astype(np.int32)
    return {k: np.ascontiguousarray(v) for k, v in o.items()}


def constants():
    o = {}
    s, t = np.arange(P)[:, None], np.arange(P)[None, :]
    same = (s // STEPS == t // STEPS) & (s < NSAMP) & (t < NSAMP)
    o["ident"] = np.eye(P)
    o["tri"] = np.stack([s <= t, (s <= t) & same, s < t], 1)
    o["lmask"] = np.stack([np.where(s <= t, 0.0, NEG), np.where((s <= t) & same, 0.0, NEG)], 1)
    o["qmask"] = np.where(t <= s, 0.0, NEG)
    o["smask"] = np.where(np.arange(STEPS)[None, :] <= np.arange(NSAMP)[:, None] % STEPS, 0.0, NEG)
    o["bmask"] = (np.arange(NSAMP)[:, None] // STEPS == np.arange(BATCHES)[None, :])
    o["bmaskT"] = np.broadcast_to(o["bmask"].T.reshape(1, BATCHES, NSAMP), (P, BATCHES, NSAMP))
    o["count_down"] = np.broadcast_to(E - np.arange(E)[None], (P, E))
    o["count_up"] = np.broadcast_to(np.arange(SLOTS + 1)[None], (P, SLOTS + 1))
    o["steps"] = np.broadcast_to(P * np.arange(TILES)[None], (P, TILES))
    pos = np.concatenate([np.arange(SEQ), PAST + np.arange(NSAMP) % STEPS]).astype(np.float32)
    half = ROPE // 2
    inv = (10000.0 ** (-np.arange(half) / half)).astype(np.float32)
    ang = pos[:, None] * inv[None]
    cos, sin = np.cos(ang).astype(np.float32), np.sin(ang).astype(np.float32)
    cs = np.zeros((TILES * P, 2, half), np.float32)
    cs[:N, 0], cs[:N, 1] = cos, sin
    o["trig_tok"] = cs.reshape(TILES, P, 2, half).transpose(1, 0, 2, 3)
    o["trig_feat"] = np.concatenate([cos, cos, -sin, sin], 1).T
    o = {k: np.ascontiguousarray(v, dtype=np.float32) for k, v in o.items()}
    ids = np.arange(TILES * P).reshape(TILES, P).T
    o["token_ids"] = np.ascontiguousarray(ids.astype(np.int32))
    o["no_token"] = np.full((SLOTS, P), N, np.int32)
    return o


CONST_SHAPES = {k: (v.shape, v.dtype) for k, v in constants().items()}
RESIDENT = ("ident", "tri", "lmask", "qmask", "smask", "bmask", "count_down", "count_up", "steps")


def stage_constants(nc, g):
    with nc.cleanup_on_exit(), ExitStack() as ctx:
        s, s_one = nc.alloc_semaphore("constants"), nc.alloc_semaphore("ones")
        block = ctx.enter_context(nc.Block())

        @block.sync
        def _(sp):
            for k in RESIDENT:
                t = g.resident[k]
                sp.dma_start(t[:], g.const[k]).then_inc(s, 16)
            sp.wait_ge(s, 16 * len(RESIDENT))
            sp.wait_ge(s_one, 1)

        @block.vector
        def _(v):
            nc.vector.memset(g.ones[:], 1.0)
            v.drain()
            v.sem_inc(s_one, 1)


def build(nc, ins, const, outs, stages=99):
    g = Shared()
    g.x_prompt = ins["x_prompt"]
    g.x_sample = ins["x_sample"]
    g.cT = ins["cT"]
    g.ada_w = ins["ada_w"]
    g.ada_b = ins["ada_b"]
    g.ln_g = ins["ln_g"]
    g.ln_b = ins["ln_b"]
    g.a_w_in = ins["a_w_in"]
    g.a_b_gates = ins["a_b_gates"]
    g.a_norm_g = ins["a_norm_g"]
    g.a_w_out = ins["a_w_out"]
    g.state = ins["state"]
    g.state_mT = ins["state_mT"]
    g.w_kv_a = ins["w_kv_a"]
    g.kv_norm_g = ins["kv_norm_g"]
    g.q_norm_g = ins["q_norm_g"]
    g.w_dq = ins["w_dq"]
    g.w_uq = ins["w_uq"]
    g.w_uk = ins["w_uk"]
    g.w_ukT = ins["w_ukT"]
    g.w_uv = ins["w_uv"]
    g.w_o = ins["w_o"]
    g.router_w = ins["router_w"]
    g.router_b = ins["router_b"]
    g.e_gate = ins["e_gate"]
    g.e_up = ins["e_up"]
    g.e_down = ins["e_down"]
    g.cache = ins["cache"]
    g.page_table = ins["page_table"]
    g.y_prompt = outs["y_prompt"]
    g.y_sample = outs["y_sample"]
    g.C_p = outs["C_p"]
    g.C_s = outs["C_s"]
    g.m_out = outs["m_out"]
    g.lat = outs["lat"]
    g.krope = outs["krope"]
    g.const = const
    ctx = ExitStack()
    with ctx:
        def dram(n, s, d=F32):
            return nc.dram_tensor(n, s, d, kind="Internal").ap()

        def sb(n, s, d=F32):
            return ctx.enter_context(nc.sbuf_tensor(n, s, d))

        g.mods = dram("mods", [9, 12 * D])
        g.qkvo = dram("qkvo", [N, A_IN])
        g.h2 = dram("h2", [N + 1, D])
        g.yrows = dram("yrows", [SLOTS * P, D])
        g.slot_token = dram("slot_token", [SLOTS * P, 1], I32)
        g.x = sb("x", [P, TILES, D])
        g.ones = sb("ones", [P, P])
        g.resident = {}
        for k in RESIDENT:
            shape, _ = CONST_SHAPES[k]
            g.resident[k] = sb(f"c_{k}", list(shape))
        g.ident = g.resident["ident"]
        g.tri = g.resident["tri"]
        g.lmask = g.resident["lmask"]
        g.qmask = g.resident["qmask"]
        g.smask = g.resident["smask"]
        g.bmask = g.resident["bmask"]
        g.count_down = g.resident["count_down"]
        g.count_up = g.resident["count_up"]
        g.steps = g.resident["steps"]
        g.s_w_in = ctx.enter_context(nc.semaphore("w_in_loaded"))
        g.s_x = ctx.enter_context(nc.semaphore("x_loaded"))
        stage_constants(nc, g)
        g.gates = sb("gates", [P, TILES, GATES])
        with nc.sbuf_tensor("w_in", [P, KD, A_IN + GATES], F32) as g.w_in:
            if stages >= 1:
                stage_ada(nc, g)
            if stages >= 2:
                stage_in_proj(nc, g)
        g.mixT = sb("mixT", [P, KD, N])
        with ExitStack() as gated:
            def gsb(n, s):
                return gated.enter_context(nc.sbuf_tensor(n, s, F32))

            g.u = gsb("u", [P, TILES, H])
            g.factors = gsb("factors", [P, 3, TILES, H])
            g.decay = gsb("decay", [P, H, 2 * BATCHES])
            g.M = gsb("M", [H, N])
            if stages >= 3:
                stage_gates(nc, g)
            if stages >= 4:
                stage_mlstm(nc, g)
        g.logits = sb("logits", [P, TILES, E])
        if stages >= 5:
            stage_out_proj(nc, g, 0, g.a_w_out)
        g.weight = sb("weight", [P, 2, TILES])
        g.dest = sb("dest", [P, 2, TILES], I32)
        g.slot_expert = sb("slot_expert", [P, SLOTS], I32)
        if stages >= 6:
            stage_route(nc, g, 0)
        if stages >= 7:
            stage_experts(nc, g, 0)
        if stages >= 8:
            stage_combine(nc, g, 0, stages == 8)
        with ExitStack() as attending:
            def asb(n, s):
                return attending.enter_context(nc.sbuf_tensor(n, s, F32))

            g.qS = asb("qS", [P, 3, BATCHES, H, STEPS])
            g.latT = asb("latT", [P, 2, N])
            g.krT = asb("krT", [P, N])
            with nc.sbuf_tensor("cqT", [P, 4, N], F32) as g.cqT:
                if stages >= 9:
                    stage_latents(nc, g)
                if stages >= 10:
                    stage_heads(nc, g)
            if stages >= 11:
                stage_sample(nc, g)
        if stages >= 12:
            stage_out_proj(nc, g, 1, g.w_o)
        if stages >= 13:
            stage_route(nc, g, 1)
            stage_experts(nc, g, 1)
            stage_combine(nc, g, 1, True)
    return g


def kernel(**inputs):
    from concourse import bacc
    from concourse.bass_utils import run_bass_kernel_spmd

    nc = bacc.Bacc("TRN2", target_bir_lowering=False, num_devices=1)
    arrays = laid_out(inputs)
    ins = {k: nc.dram_tensor(f"in_{k}", v.shape, mybir.dt.from_np(v.dtype), kind="ExternalInput").ap()
           for k, v in arrays.items()}
    table = constants()
    const = {k: nc.dram_tensor(f"const_{k}", v.shape, mybir.dt.from_np(v.dtype), kind="ExternalInput").ap()
             for k, v in table.items()}
    outs = {k: nc.dram_tensor(f"out_{k}", list(s), F32, kind="ExternalOutput").ap() for k, s in OUTPUTS.items()}
    build(nc, ins, const, outs)
    fed = {f"in_{k}": v for k, v in arrays.items()} | {f"const_{k}": v for k, v in table.items()}
    r = run_bass_kernel_spmd(nc, [fed], core_ids=[0]).results[0]
    o = {k: r[f"out_{k}"] for k in OUTPUTS}

    def state(c):
        c = c.reshape(2, DK, -1, PAIRS, AUG).transpose(2, 3, 0, 1, 4).reshape(-1, H, DK, AUG)
        return c[None, ..., :DV], c[None, ..., DV]

    Cp, np_ = state(o["C_p"])
    Cs, ns = state(o["C_s"])
    m = o["m_out"].T
    return (o["y_prompt"].reshape(1, SEQ, D), o["y_sample"].reshape(BATCHES, STEPS, D),
            Cp, np_, m[None, 0:1], o["lat"][:SEQ][None], o["krope"][:SEQ][None],
            Cs, ns, m[None, 1:], o["lat"][SEQ:].reshape(BATCHES, STEPS, KVR),
            o["krope"][SEQ:].reshape(BATCHES, STEPS, ROPE))
```

```python
from contextlib import ExitStack

import numpy as np

import concourse.bass as bass
from concourse import mybir

F32 = mybir.dt.float32
F32R = mybir.dt.float32r
I32 = mybir.dt.int32
ALU = mybir.AluOpType
ACT = mybir.ActivationFunctionType
AX = mybir.AxisListType.X

P = 128
D = 1024
KD = D // P
HALF = 512
SEQ = 1024
BATCHES, STEPS = 8, 8
NSAMP = BATCHES * STEPS
N = SEQ + NSAMP
PT = SEQ // P
TILES = PT + 1
H = 8
DK = 64
DV = 128
AUG = DV + 1
PAIRS = H // 2
A_IN = 3072
GATES = 2 * H
KVR, ROPE, QR = 256, 64, 512
NOPE = 128
PAST, PAGE = 2048, 128
PAGES = PAST // PAGE
CTX = PAST + STEPS
KVW = 2 * PAGE + PAGE + KVR
E, GROUPS, PER = 16, 4, 4
FE = 512
FT = FE // P
SLOTS = (2 * N + E * (P - 1)) // P
ALPHA = 4.0 ** 0.25
EPS = 1e-6
SCALE = float(NOPE + ROPE) ** -0.5
NEG = -1.0e30
SHIFT1, SCALE1, GATE1, SHIFT2, SCALE2, GATE2 = range(6)


class Shared:
    pass


def rows_of(t):
    return NSAMP if t is TILES - 1 else P


def load_mods(eng, g, dst, layer, which, sample, sem):
    at = (layer * 6 + which) * D
    if not sample:
        eng.dma_start(dst[:, :], g.mods[0:1, at:at + D].broadcast_to([P, D])).then_inc(sem, 16)
    else:
        for b in range(BATCHES):
            src = g.mods[1 + b:2 + b, at:at + D].broadcast_to([STEPS, D])
            eng.dma_start(dst[b * STEPS:(b + 1) * STEPS, :], src).then_inc(sem, 16)


def stage_ada(nc, g):
    CH = 2 * 6 * D // HALF
    RING = 3
    with nc.cleanup_on_exit(), ExitStack() as ctx:
        def sb(n, s, d=F32):
            return ctx.enter_context(nc.sbuf_tensor(n, s, d))

        def sem(n):
            return nc.alloc_semaphore(f"ada_{n}")

        w = sb("ada_w_ring", [P, RING, KD * HALF])
        bias = sb("ada_bias_ring", [9, RING, HALF])
        out = sb("ada_out", [9, RING, HALF])
        c = sb("ada_c", [P, KD * 9])
        ex = sb("ada_exp", [P, KD * 9])
        sc = sb("ada_silu", [P, KD * 9])
        ps = ctx.enter_context(nc.psum_tensor("ada_ps", [P, RING, HALF], F32))
        s_c, s_exp, s_silu = sem("c_loaded"), sem("c_exp"), sem("silu_ready")
        s_w = [sem(f"w_loaded{i}") for i in range(RING)]
        s_mm, s_ev = sem("chunk_summed"), sem("chunk_out")
        s_st = [sem(f"mods_stored{i}") for i in range(RING)]
        block = ctx.enter_context(nc.Block())

        @block.sync
        def _(sp):
            sp.dma_start(c[:], g.cT).then_inc(s_c, 16)
            with sp.Fori(0, CH // RING) as i:
                for r in range(RING):
                    j = i * RING + r
                    sp.wait_ge(s_mm, j + 1)
                    sp.dma_start(w[:, r, :], g.ada_w[bass.ds(j, 1)].rearrange("o p n -> (o p) n")).then_inc(s_w[r], 16)
                    sp.wait_ge(s_ev, j + 1)
                    sp.dma_start(bias[:, r, :], g.ada_b[bass.ds(j, 1)].broadcast_to([9, HALF])).then_inc(s_w[r], 16)

        @block.scalar
        def _(act):
            for k in range(KD):
                act.dma_start(g.w_in[:, k, :], g.a_w_in[k * P:(k + 1) * P, :]).then_inc(g.s_w_in, 16)
            act.dma_start(g.x[:, 0:PT, :], g.x_prompt.rearrange("(t p) d -> p t d", p=P)).then_inc(g.s_x, 16)
            act.dma_start(g.x[0:NSAMP, PT, :], g.x_sample).then_inc(g.s_x, 16)
            act.wait_ge(s_c, 16)
            nc.scalar.activation(ex[:], c[:], ACT.Exp, scale=-1.0).then_inc(s_exp, 1)
            with act.Fori(0, CH // RING) as i:
                for r in range(RING):
                    j = i * RING + r
                    act.wait_ge(s_ev, j + 1 + RING)
                    act.dma_start(g.mods[:, bass.ds(j * HALF, HALF)], out[:, r, :]).then_inc(s_st[r], 16)
            for r in range(RING):
                act.wait_ge(s_st[r], 16 * (CH // RING) + 16)

        @block.vector
        def _(v):
            v.wait_ge(s_exp, 1)
            nc.vector.tensor_scalar(ex[:], ex[:], 1.0, None, ALU.add)
            v.drain()
            nc.vector.reciprocal(ex[:], ex[:])
            v.drain()
            nc.vector.tensor_tensor(sc[:], c[:], ex[:], ALU.mult).then_inc(s_silu, 1)
            v.sem_inc(s_ev, RING)
            for r in range(RING):
                v.sem_inc(s_st[r], 16)
            with v.Fori(0, CH // RING) as i:
                for r in range(RING):
                    j = i * RING + r
                    v.wait_ge(s_mm, j + 1 + RING)
                    v.wait_ge(s_w[r], 32 * i + 32)
                    v.wait_ge(s_st[r], 16 * i + 16)
                    nc.vector.tensor_tensor(out[:, r, :], ps[0:9, r, :], bias[:, r, :], ALU.add).then_inc(s_ev, 1)

        @block.tensor
        def _(pe):
            pe.sem_inc(s_mm, RING)
            pe.wait_ge(s_silu, 1)
            with pe.Fori(0, CH // RING) as i:
                for r in range(RING):
                    j = i * RING + r
                    pe.wait_ge(s_w[r], 32 * i + 32)
                    pe.wait_ge(s_ev, j + 1)
                    for k in range(KD):
                        mm = nc.tensor.matmul(ps[0:9, r, :], sc[:, k * 9:(k + 1) * 9],
                                              w[:, r, k * HALF:(k + 1) * HALF], start=(k == 0), stop=(k == KD - 1))
                    mm.then_inc(s_mm, 1)


def stage_in_proj(nc, g):
    OUTS = A_IN // HALF
    with nc.cleanup_on_exit(), ExitStack() as ctx:
        def sb(n, s, d=F32):
            return ctx.enter_context(nc.sbuf_tensor(n, s, d))

        def sem(n):
            return nc.alloc_semaphore(f"in_{n}")

        shift = sb("in_shift", [P, D])
        scale = sb("in_scale", [P, D])
        h = sb("in_h", [P, D])
        hT = sb("in_hT", [P, 2, KD, P])
        out = sb("in_out", [P, 2, A_IN])
        psT = ctx.enter_context(nc.psum_tensor("in_psT", [P, KD, P], F32))
        ps = ctx.enter_context(nc.psum_tensor("in_ps", [P, OUTS, HALF], F32))
        s_mods, s_modfree = sem("mods_loaded"), sem("mods_used")
        s_h, s_T, s_hT, s_mm, s_ev = sem("h_ready"), sem("h_turned"), sem("hT_ready"), sem("chunk_summed"), sem("chunk_out")
        s_st = [sem("qkvo_stored0"), sem("qkvo_stored1")]
        block = ctx.enter_context(nc.Block())

        @block.sync
        def _(sp):
            load_mods(sp, g, shift, 0, SHIFT1, False, s_mods)
            load_mods(sp, g, scale, 0, SCALE1, False, s_mods)

            def store(t, par, i, n):
                for c in range(2):
                    sp.wait_ge(s_ev, 7 * t + 3 * c + 3 + 7)
                    sp.dma_start(g.qkvo[bass.ds(t * P, n), c * 1536:(c + 1) * 1536],
                                 out[0:n, par, c * 1536:(c + 1) * 1536]).then_inc(s_st[par], 16)

            with sp.Fori(0, PT // 2) as i:
                for par in range(2):
                    store(i * 2 + par, par, i, P)
            sp.wait_ge(s_modfree, PT)
            load_mods(sp, g, shift, 0, SHIFT1, True, s_mods)
            load_mods(sp, g, scale, 0, SCALE1, True, s_mods)
            store(PT, 0, PT // 2, NSAMP)
            sp.wait_ge(s_st[0], 32 * (PT // 2 + 1) + 32)
            sp.wait_ge(s_st[1], 32 * (PT // 2) + 32)

        @block.vector
        def _(v):
            nc.vector.memset(g.gates[:], 0.0)
            v.wait_ge(g.s_x, 32)

            def tile(t, n, mods):
                v.wait_ge(s_mods, mods)
                v.wait_ge(s_T, t + 1)
                x = g.x[0:n, bass.ds(t, 1), :].rearrange("p o d -> p (o d)")
                nc.vector.scalar_tensor_tensor(out=h[0:n, :], in0=scale[0:n, :], scalar=1.0, in1=x,
                                               op0=ALU.add, op1=ALU.mult)
                v.drain()
                nc.vector.tensor_tensor(h[0:n, :], h[0:n, :], shift[0:n, :], ALU.add)
                v.drain()
                v.sem_inc(s_h, 1)
                v.sem_inc(s_modfree, 1)

            with v.Fori(0, PT) as t:
                tile(t, P, 32)
            tile(PT, NSAMP, 32 + 2 * 16 * BATCHES)

        @block.tensor
        def _(pe):
            pe.sem_inc(s_T, 1)
            pe.wait_ge(g.s_w_in, 16 * KD)

            def tile(t, par, n):
                pe.wait_ge(s_h, t + 1)
                pe.wait_ge(s_hT, t + 1)
                for k in range(KD):
                    mm = nc.tensor.transpose(psT[:, k, 0:n], h[0:n, k * P:(k + 1) * P], g.ident[0:n, 0:n])
                mm.then_inc(s_T, 1)
                pe.wait_ge(s_hT, t + 2)
                for c in range(OUTS):
                    if c == 0:
                        pe.wait_ge(s_ev, 7 * t + 7)
                    else:
                        pe.wait_ge(s_ev, 7 * t + c + 1)
                    for k in range(KD):
                        mm = nc.tensor.matmul(ps[0:n, c, :], hT[:, par, k, 0:n], g.w_in[:, k, c * HALF:(c + 1) * HALF],
                                              start=(k == 0), stop=(k == KD - 1))
                    mm.then_inc(s_mm, 1)
                pe.wait_ge(s_ev, 7 * t + 1 + 7)
                for k in range(KD):
                    mm = nc.tensor.matmul(ps[0:n, 0, 0:GATES], hT[:, par, k, 0:n], g.w_in[:, k, A_IN:A_IN + GATES],
                                          start=(k == 0), stop=(k == KD - 1))
                mm.then_inc(s_mm, 1)

            with pe.Fori(0, PT // 2) as i:
                for par in range(2):
                    tile(i * 2 + par, par, P)
            tile(PT, 0, NSAMP)

        @block.scalar
        def _(act):
            act.sem_inc(s_hT, 1)
            act.sem_inc(s_ev, 7)
            act.sem_inc(s_st[0], 32)
            act.sem_inc(s_st[1], 32)

            def turn(t, par, n):
                act.wait_ge(s_T, t + 2)
                for z in range(2):
                    cp = nc.scalar.copy(hT[:, par, z * 4:z * 4 + 4, 0:n], psT[:, z * 4:z * 4 + 4, 0:n])
                act.drain()
                act.sem_inc(s_hT, 1)

            def tile(t, par, i, n):
                turn(t, par, n)
                act.wait_ge(s_st[par], 32 * i + 32)
                for c in range(OUTS):
                    act.wait_ge(s_mm, 7 * t + c + 1)
                    nc.scalar.activation(out[0:n, par, c * HALF:(c + 1) * HALF], ps[0:n, c, :],
                                         ACT.Sigmoid if c >= 4 else ACT.Copy).then_inc(s_ev, 1)
                act.wait_ge(s_mm, 7 * t + 7)
                nc.scalar.copy(g.gates[0:n, bass.ds(t, 1), :].rearrange("p o d -> p (o d)"),
                               ps[0:n, 0, 0:GATES]).then_inc(s_ev, 1)

            with act.Fori(0, PT // 2) as i:
                for par in range(2):
                    tile(i * 2 + par, par, i, P)
            tile(PT, 0, PT // 2, NSAMP)


def stage_gates(nc, g):
    with nc.cleanup_on_exit(), ExitStack() as ctx:
        def sb(n, s, d=F32):
            return ctx.enter_context(nc.sbuf_tensor(n, s, d))

        def sem(n):
            return nc.alloc_semaphore(f"g_{n}")

        bg = sb("g_bias", [P, GATES])
        mn = sb("g_min", [P, TILES, H])
        ab = sb("g_abs", [P, TILES, H])
        lf = sb("g_logf", [P, TILES, H])
        btok = sb("g_btok", [P, TILES, H])
        bh = sb("g_bh", [H, N])
        uh = sb("g_uh", [H, N])
        ca = sb("g_ca", [H, N])
        cb = sb("g_cb", [H, N])
        e3 = sb("g_e3", [H, 3, N])
        mend = sb("g_mend", [H, 2 * BATCHES])
        bend = sb("g_bend", [H, 2 * BATCHES])
        dec = sb("g_dec", [H, 2 * BATCHES])
        decd = sb("g_decd", [H, H, 2 * BATCHES])
        mprev = sb("g_mprev", [H, 2 * BATCHES])
        mout = sb("g_mout", [H, 1 + BATCHES])
        psb = ctx.enter_context(nc.psum_tensor("g_psb", [P, HALF], F32))
        psh = ctx.enter_context(nc.psum_tensor("g_psh", [P, 6, HALF], F32))
        s_ld, s_ab, s_e, s_ln, s_lf, s_b, s_u, s_t = (sem(x) for x in (
            "loaded", "abs_ready", "exp_ready", "ln_ready", "logf_ready", "b_summed", "u_ready", "turned_in"))
        s_args, s_exps, s_dd, s_back, s_st, s_gates = (sem(x) for x in (
            "exp_args", "exps_ready", "decay_diag", "turned_back", "m_stored", "gates_out"))
        block = ctx.enter_context(nc.Block())
        CP, CS = P, STEPS
        NC = PT + BATCHES

        def chunks(a):
            return (a[:, 0:SEQ].rearrange("h (c t) -> h c t", t=CP), a[:, SEQ:N].rearrange("h (c t) -> h c t", t=CS))

        @block.sync
        def _(sp):
            sp.dma_start(bg[:], g.a_b_gates.broadcast_to([P, GATES])).then_inc(s_ld, 16)
            sp.dma_start(mprev[:, PT:NC], g.state_mT).then_inc(s_ld, 16)
            sp.wait_ge(s_args, 1)
            sp.dma_start(g.m_out, mout[:]).then_inc(s_st, 16)
            sp.wait_ge(s_st, 16)

        @block.vector
        def _(v):
            V = nc.vector
            v.wait_ge(s_ld, 32)
            V.tensor_tensor(g.gates[:], g.gates[:], bg[:].unsqueeze(1).broadcast_to([P, TILES, GATES]), ALU.add)
            v.drain()
            xf = g.gates[:, :, H:GATES]
            V.tensor_scalar(mn[:], xf, 0.0, None, ALU.min)
            V.tensor_scalar(ab[:], xf, 0.0, None, ALU.max)
            v.drain()
            V.tensor_tensor(ab[:], mn[:], ab[:], ALU.subtract)
            v.drain()
            v.sem_inc(s_ab, 1)
            v.wait_ge(s_e, 1)
            V.tensor_scalar(ab[:], ab[:], 1.0, None, ALU.add)
            v.drain()
            v.sem_inc(s_ab, 1)
            v.wait_ge(s_ln, 1)
            V.tensor_tensor(lf[:], mn[:], ab[:], ALU.subtract)
            v.drain()
            v.sem_inc(s_lf, 1)
            v.wait_ge(s_b, 1)
            V.tensor_copy(btok[:, 0:PT, :], psb[:, 0:PT * H].rearrange("p (t h) -> p t h", h=H))
            V.memset(btok[:, PT, :], 0.0)
            v.drain()
            V.tensor_copy(btok[0:NSAMP, PT, :], psb[0:NSAMP, 128:128 + H])
            v.drain()
            V.tensor_tensor(g.u[:], g.gates[:, :, 0:H], btok[:], ALU.subtract)
            v.drain()
            v.sem_inc(s_u, 1)
            v.wait_ge(s_t, 1)
            V.tensor_copy(uh[:, 0:SEQ], psh[0:H, 0:2, :])
            V.tensor_copy(uh[:, SEQ:N], psh[0:H, 4, 0:NSAMP])
            V.tensor_copy(bh[:, 0:SEQ], psh[0:H, 2:4, :])
            V.tensor_copy(bh[:, SEQ:N], psh[0:H, 4, NSAMP:2 * NSAMP])
            v.drain()
            V.tensor_copy(ca[:], uh[:])
            v.drain()
            src, dst = ca, cb
            k = 1
            while k < CP:
                for part, n in zip(range(2), (CP, CS)):
                    s, d = chunks(src)[part], chunks(dst)[part]
                    if k < n:
                        V.tensor_tensor(d[:, :, k:n], s[:, :, k:n], s[:, :, 0:n - k], ALU.max)
                        V.tensor_copy(d[:, :, 0:k], s[:, :, 0:k])
                    else:
                        V.tensor_copy(d, s)
                v.drain()
                src, dst = dst, src
                k *= 2
            cm, tmp = src, dst
            for part, (lo, n) in enumerate(((0, CP), (PT, CS))):
                V.tensor_copy(mend[:, lo:lo + PT], chunks(cm)[part][:, :, n - 1])
                V.tensor_copy(bend[:, lo:lo + PT], chunks(bh)[part][:, :, n - 1])
            V.memset(mprev[:, 0:1], 0.0)
            v.drain()
            for c in range(PT):
                V.tensor_tensor(mend[:, c:c + 1], mend[:, c:c + 1], mprev[:, c:c + 1], ALU.max)
                v.drain()
                nxt = mprev[:, c + 1:c + 2] if c + 1 < PT else mout[:, 0:1]
                V.tensor_tensor(nxt, mend[:, c:c + 1], bend[:, c:c + 1], ALU.add)
                v.drain()
            V.tensor_tensor(mend[:, PT:NC], mend[:, PT:NC], mprev[:, PT:NC], ALU.max)
            v.drain()
            V.tensor_tensor(mout[:, 1:1 + BATCHES], mend[:, PT:NC], bend[:, PT:NC], ALU.add)
            for part, (lo, n) in enumerate(((0, CP), (PT, CS))):
                mp = mprev[:, lo:lo + PT].unsqueeze(2).broadcast_to([H, PT, n])
                me = mend[:, lo:lo + PT].unsqueeze(2).broadcast_to([H, PT, n])
                M = chunks(g.M)[part]
                V.tensor_tensor(M, chunks(cm)[part], mp, ALU.max)
                v.drain()
                V.tensor_tensor(chunks(e3[:, 0, :])[part], mp, M, ALU.subtract)
                V.tensor_tensor(chunks(tmp)[part], chunks(bh)[part], M, ALU.add)
                V.tensor_tensor(chunks(e3[:, 2, :])[part], chunks(uh)[part], me, ALU.subtract)
            v.drain()
            V.tensor_scalar(e3[:, 1, :], tmp[:], -1.0, None, ALU.mult)
            V.tensor_tensor(dec[:], mprev[:], mend[:], ALU.subtract)
            v.drain()
            v.sem_inc(s_args, 1)
            v.wait_ge(s_exps, 1)
            V.tensor_tensor(decd[:], g.ident[0:H, 0:H].unsqueeze(2).broadcast_to([H, H, NC]),
                            dec[:].unsqueeze(1).broadcast_to([H, H, NC]), ALU.mult)
            v.drain()
            v.sem_inc(s_dd, 1)
            v.wait_ge(s_back, 1)
            V.memset(g.factors[:], 0.0)
            v.drain()
            for x in range(3):
                V.tensor_copy(g.factors[:, x, 0:PT, :], psh[:, x, 0:PT * H].rearrange("p (t h) -> p t h", h=H))
                V.tensor_copy(g.factors[0:NSAMP, x, PT, :], psh[0:NSAMP, x, PT * H:TILES * H])
            V.tensor_copy(g.decay[:], psh[:, 3, 0:H * NC].rearrange("p (h c) -> p h c", h=H))

        @block.scalar
        def _(act):
            act.wait_ge(s_ab, 1)
            nc.scalar.activation(ab[:], ab[:], ACT.Exp)
            act.drain()
            act.sem_inc(s_e, 1)
            act.wait_ge(s_ab, 2)
            nc.scalar.activation(ab[:], ab[:], ACT.Ln)
            act.drain()
            act.sem_inc(s_ln, 1)
            act.wait_ge(s_args, 1)
            nc.scalar.activation(e3[:], e3[:], ACT.Exp)
            nc.scalar.activation(dec[:], dec[:], ACT.Exp)
            act.drain()
            act.sem_inc(s_exps, 1)

        @block.tensor
        def _(pe):
            T = nc.tensor
            pe.wait_ge(s_lf, 1)
            T.matmul(psb[:, 0:PT * H], g.tri[:, 0, :], lf[:, 0:PT, :], start=True, stop=True)
            T.matmul(psb[0:NSAMP, 128:128 + H], g.tri[0:NSAMP, 1, 0:NSAMP], lf[0:NSAMP, PT, :],
                     start=True, stop=True)
            pe.drain()
            pe.sem_inc(s_b, 1)
            pe.wait_ge(s_u, 1)
            for bank, src in ((0, g.u), (2, btok)):
                for t in range(PT):
                    T.transpose(psh[0:H, bank + t // 4, (t % 4) * P:(t % 4 + 1) * P], src[:, t, :], g.ident[:])
                o = 0 if bank == 0 else NSAMP
                T.transpose(psh[0:H, 4, o:o + NSAMP], src[0:NSAMP, PT, :], g.ident[0:NSAMP, 0:NSAMP])
            pe.drain()
            pe.sem_inc(s_t, 1)
            pe.wait_ge(s_dd, 1)
            for x in range(3):
                for t in range(TILES):
                    n = rows_of(t)
                    T.transpose(psh[0:n, x, t * H:(t + 1) * H], e3[:, x, t * P:t * P + n], g.ident[0:H, 0:H])
            T.matmul(psh[:, 3, 0:H * NC], g.ones[0:H, :], decd[:], start=True, stop=True)
            pe.drain()
            pe.sem_inc(s_back, 1)


def stage_mlstm(nc, g):
    with nc.cleanup_on_exit(), ExitStack() as ctx:
        def sb(n, s, d=F32):
            return ctx.enter_context(nc.sbuf_tensor(n, s, d))

        def sem(n):
            return nc.alloc_semaphore(f"m_{n}")

        qkvo = sb("m_qkvo", [P, 2, A_IN])
        qT = sb("m_qT", [P, PAIRS, P])
        kT = sb("m_kT", [P, PAIRS, P])
        negid = sb("m_negid", [H, H])
        kfac = sb("m_kfac", [P, TILES, H])
        Md = sb("m_Md", [H, H, P])
        mask = [sb("m_mask_prompt", [P, 4, P]), sb("m_mask_sample", [P, 4, NSAMP])]
        ex = sb("m_ex", [P, H, P])
        va = sb("m_va", [P, H, AUG])
        kw = sb("m_kw", [P, H, DK])
        kwb = sb("m_kwb", [NSAMP, BATCHES, H * DK])
        qb = sb("m_qb", [P, BATCHES, PAIRS, NSAMP])
        C = sb("m_C", [P, PAIRS, AUG])
        Cs = sb("m_Cs", [P, BATCHES, PAIRS, AUG])
        hh = sb("m_hh", [P, H, AUG])
        sg = sb("m_sg", [P, D])
        y = sb("m_y", [P, D])
        ng = sb("m_ng", [P, D])
        dn = sb("m_dn", [P, 2, H])
        st = sb("m_st", [P, H, 6])
        mv = sb("m_mv", [P, H, 2])
        rs = sb("m_rs", [P, H])
        bmT = sb("m_bmT", [P, BATCHES, NSAMP])
        ps = ctx.enter_context(nc.psum_tensor("m_ps", [P, 8, HALF], F32))
        TS, AA, NN, QQ = 0, 2, 4, 6
        OWN, CARRIED = (NN, TS), (QQ, AA)
        ADDED = (NN, NN + 1, QQ, QQ + 1)
        s_ld = [sem("qkvo_loaded0"), sem("qkvo_loaded1")]
        s_c, s_T, s_qk, s_Md, s_A, s_E, s_S, s_P, s_kv = (sem(x) for x in (
            "side_loaded", "qk_turned", "qkT_ready", "M_diag", "exponents", "exp_ready", "scores", "weighted", "keys_values_ready"))
        s_N, s_comb, s_U, s_C, s_free, s_var, s_sd, s_gate, s_y, s_yT, s_out, s_set, s_qb, s_st, s_turning = (sem(x) for x in (
            "heads_summed", "heads_combined", "state_added", "state_ready", "slot_read", "variance",
            "deviation", "gate_ready", "y_ready", "y_turned", "y_out", "tables_set", "by_batch", "states_stored", "turning"))
        block = ctx.enter_context(nc.Block())

        @block.sync
        def _(sp):
            sp.dma_start(ng[:], g.a_norm_g.broadcast_to([P, D])).then_inc(s_c, 16)
            sp.dma_start(Cs[:], g.state).then_inc(s_c, 16)
            sp.dma_start(bmT[:], g.const["bmaskT"]).then_inc(s_c, 16)
            with sp.Fori(0, PT // 2) as i:
                for par in range(2):
                    t = i * 2 + par
                    sp.wait_ge(s_free, t + 1)
                    sp.dma_start(qkvo[:, par, :], g.qkvo[bass.ds(t * P, P), :]).then_inc(s_ld[par], 16)
            sp.wait_ge(s_free, PT + 1)
            sp.dma_start(qkvo[0:NSAMP, 0, :], g.qkvo[SEQ:N, :]).then_inc(s_ld[0], 16)
            sp.wait_ge(s_C, PT)
            sp.dma_start(g.C_p, C[:]).then_inc(s_st, 16)
            sp.wait_ge(s_C, PT + BATCHES)
            sp.dma_start(g.C_s, Cs[:]).then_inc(s_st, 16)
            sp.wait_ge(s_st, 32)

        def half(h):
            return slice(DK * (h % 2), DK * (h % 2) + DK)

        @block.tensor
        def _(pe):
            T = nc.tensor

            def front(t, par, i, n, sample):
                pe.wait_ge(s_ld[par], 16 * i + 16)
                if not (isinstance(t, int) and t == 0):
                    pe.wait_ge(s_comb, 2 * t)
                    pe.sem_inc(s_turning, 1)
                for z in range(2):
                    for p in range(PAIRS):
                        mm = T.transpose(ps[:, TS + z, p * P:p * P + n],
                                         qkvo[0:n, par, z * 512 + p * P:z * 512 + (p + 1) * P], g.ident[0:n, 0:n])
                mm.then_inc(s_T, 1)
                pe.wait_ge(s_Md, t + 1)
                for a in range(2):
                    T.matmul(ps[0:n, AA + a, 0:4 * n], g.ident[0:n, 0:n], mask[sample][0:n, :, 0:n],
                             start=True, stop=False)
                    mm = T.matmul(ps[0:n, AA + a, 0:4 * n], g.ones[0:H, 0:n], Md[:, a * 4:a * 4 + 4, 0:n],
                                  start=False, stop=True)
                mm.then_inc(s_A, 1)

            def scores(t, n):
                pe.wait_ge(s_qk, t + 1)
                for h in range(H):
                    T.matmul(ps[0:n, TS + h % 2, (h // 2) * n:(h // 2 + 1) * n], kT[half(h), h // 2, 0:n],
                             qT[half(h), h // 2, 0:n], start=True, stop=True, skip_group_check=True)
                pe.drain()
                pe.sem_inc(s_S, 1)

            def products(t, n, sample, a):
                if sample and a == 1:
                    pe.wait_ge(s_qb, 1)
                if a == 1:
                    pe.wait_ge(s_P, 2 * t + 2)
                else:
                    pe.wait_ge(s_out, t + 1)
                for h in range(4 * a, 4 * a + 4):
                    b, o = h % 2, (h // 2 % 2) * AUG
                    T.matmul(ps[0:n, OWN[a] + b, o:o + AUG], ex[0:n, h, 0:n], va[0:n, h, :],
                             start=True, stop=True, skip_group_check=True)
                    if not sample:
                        T.matmul(ps[0:n, CARRIED[a] + b, o:o + AUG], qT[half(h), h // 2, 0:n], C[half(h), h // 2, :],
                                 start=True, stop=True, skip_group_check=True)
                    else:
                        for z in range(BATCHES):
                            T.matmul(ps[0:n, CARRIED[a] + b, o:o + AUG], qb[half(h), z, h // 2, :],
                                     Cs[half(h), z, h // 2, :], start=(z == 0), stop=(z == BATCHES - 1),
                                     skip_group_check=True)
                pe.drain()
                pe.sem_inc(s_N, 1)

            def add(t, n, sample):
                pe.wait_ge(s_comb, 2 * t + 3)
                if not sample:
                    for p in range(PAIRS):
                        mm = T.matmul(ps[:, ADDED[p], 0:2 * AUG],
                                      kw[:, 2 * p:2 * p + 2, :], va[:, 2 * p:2 * p + 2, :], start=True, stop=True)
                    mm.then_inc(s_U, 1)
                else:
                    for z in range(BATCHES):
                        if z >= 1:
                            pe.wait_ge(s_C, PT + z)
                        for p in range(PAIRS):
                            mm = T.matmul(ps[:, ADDED[p], 0:2 * AUG],
                                          kwb[:, z, p * P:(p + 1) * P], va[0:n, 2 * p:2 * p + 2, :],
                                          start=True, stop=True)
                        mm.then_inc(s_U, 1)

            def turn_y(t, n):
                pe.wait_ge(s_C, t + (BATCHES if n == NSAMP else 1))
                pe.wait_ge(s_y, t + 2)
                pe.sem_inc(s_turning, 1)
                for k in range(KD):
                    mm = T.transpose(ps[:, NN + k // 4, (k % 4) * P:(k % 4) * P + n], y[0:n, k * P:(k + 1) * P],
                                     g.ident[0:n, 0:n])
                mm.then_inc(s_yT, 1)

            pe.sem_inc(s_A, 1)
            pe.sem_inc(s_U, 1)
            pe.sem_inc(s_yT, 1)
            pe.wait_ge(s_set, 1)
            front(0, 0, 0, P, 0)
            scores(0, P)
            products(0, P, False, 1)
            products(0, P, False, 0)
            add(0, P, False)

            def step(t, par, i, n, last):
                front(t, par, i, n, int(last))
                scores(t, n)
                products(t, n, last, 1)
                turn_y(t - 1, P)
                products(t, n, last, 0)
                add(t, n, last)

            with pe.Fori(0, PT // 2 - 1) as i:
                for par in range(2):
                    step(i * 2 + par + 1, 1 - par, i + par, P, False)
            step(PT - 1, 1, PT // 2 - 1, P, False)
            step(PT, 0, PT // 2, NSAMP, True)
            turn_y(PT, NSAMP)

        @block.gpsimd
        def _(po):
            G = nc.gpsimd
            G.memset(va[:, :, DV:AUG], 1.0)
            po.sem_inc(s_free, 2)
            po.wait_ge(s_c, 48)
            po.wait_ge(s_set, 1)

            def chunk(t, par, i, n):
                po.wait_ge(s_A, t + 1)
                G.tensor_tensor(Md[:, :, 0:n], g.M[:, bass.ds(t * P, n)].unsqueeze(1).broadcast_to([H, H, n]),
                                negid[:].unsqueeze(2).broadcast_to([H, H, n]), ALU.mult)
                po.drain()
                po.sem_inc(s_Md, 1)
                po.wait_ge(s_ld[par], 16 * i + 16)
                po.wait_ge(s_U, t + 1)
                L = qkvo[0:n, par, :]
                f = kfac[0:n, bass.ds(t, 1), :].rearrange("p o h -> p (o h)")
                G.tensor_tensor(kw[0:n, :, :], L[:, 512:D].rearrange("p (h k) -> p h k", h=H),
                                f.unsqueeze(2).broadcast_to([n, H, DK]), ALU.mult)
                G.tensor_copy(va[0:n, :, 0:DV], L[:, D:2 * D].rearrange("p (h v) -> p h v", h=H))
                po.drain()
                po.sem_inc(s_kv, 1)
                po.wait_ge(s_y, t + 1)
                G.tensor_tensor(sg[0:n, :], L[:, 2 * D:3 * D], ng[0:n, :], ALU.mult)
                po.drain()
                po.sem_inc(s_gate, 1)
                po.wait_ge(s_T, t + 1)
                po.sem_inc(s_free, 1)

            with po.Fori(0, PT // 2) as i:
                for par in range(2):
                    chunk(i * 2 + par, par, i, P)
            chunk(PT, 0, PT // 2, NSAMP)

        @block.scalar
        def _(act):
            S = nc.scalar
            act.sem_inc(s_out, 1)

            def queries_keys(t, n):
                act.wait_ge(s_T, t + 1)
                S.copy(qT[:, :, 0:n], ps[:, TS, :].rearrange("p (a s) -> p a s", a=PAIRS)[:, :, 0:n])
                S.mul(kT[:, :, 0:n], ps[:, TS + 1, :].rearrange("p (a s) -> p a s", a=PAIRS)[:, :, 0:n], DK ** -0.5)
                act.drain()
                act.sem_inc(s_qk, 1)

            def exponentials(t, n):
                act.wait_ge(s_A, t + 2)
                act.wait_ge(s_N, 2 * t + 2)
                for h in range(H):
                    a = ps[0:n, AA + h // 4, (h % 4) * n:(h % 4 + 1) * n]
                    S.activation(ex[0:n, h, 0:n], a, ACT.Exp,
                                 bias=g.u[0:n, bass.ds(t, 1), h:h + 1].rearrange("p o h -> p (o h)"))
                act.drain()
                act.sem_inc(s_E, 1)

            def root(t, n):
                act.wait_ge(s_var, t + 1)
                S.activation(rs[0:n, :], rs[0:n, :], ACT.Sqrt)
                act.drain()
                act.sem_inc(s_sd, 1)

            def keep(t, n):
                act.wait_ge(s_yT, t + 2)
                for z in range(2):
                    S.copy(g.mixT[:, z * 4:z * 4 + 4, bass.ds(t * P, n)],
                           ps[:, NN + z, :].rearrange("p (k s) -> p k s", k=4)[:, :, 0:n])
                act.drain()
                act.sem_inc(s_out, 1)

            queries_keys(0, P)
            exponentials(0, P)
            with act.Fori(0, PT - 1) as t:
                queries_keys(t + 1, P)
                exponentials(t + 1, P)
                root(t, P)
                keep(t, P)
            queries_keys(PT, NSAMP)
            exponentials(PT, NSAMP)
            root(PT - 1, P)
            keep(PT - 1, P)
            root(PT, NSAMP)
            keep(PT, NSAMP)

        @block.vector
        def _(v):
            V = nc.vector
            v.sem_inc(s_comb, 1)
            v.sem_inc(s_y, 1)
            V.memset(C[:], 0.0)
            V.tensor_scalar(negid[:], g.ident[0:H, 0:H], -1.0, None, ALU.mult)
            V.tensor_scalar(kfac[:], g.factors[:, 2, :, :], DK ** -0.5, None, ALU.mult)
            for z, n in enumerate((P, NSAMP)):
                V.tensor_copy(mask[z][:], g.lmask[:, z, 0:n].unsqueeze(1).broadcast_to([P, 4, n]))
            v.drain()
            v.sem_inc(s_set, 1)
            v.sem_inc(s_N, 2)
            v.wait_ge(s_c, 48)

            def weigh(t, n, sample):
                if sample:
                    v.wait_ge(s_qk, t + 1)
                    v.wait_ge(s_kv, t + 1)
                    for z in range(BATCHES):
                        V.tensor_scalar(kwb[:, z, :], kw[0:n, :, :].rearrange("p h k -> p (h k)"),
                                        g.bmask[0:n, z:z + 1], None, ALU.mult)
                        V.tensor_tensor(qb[:, z, :, :], qT[:, :, 0:n],
                                        bmT[:, z, :].unsqueeze(1).broadcast_to([P, PAIRS, n]), ALU.mult)
                    v.drain()
                    v.sem_inc(s_qb, 1)
                v.wait_ge(s_E, t + 1)
                v.wait_ge(s_kv, t + 1)
                v.wait_ge(s_S, t + 1)
                for a in range(2):
                    V.tensor_tensor(ex[0:n, a:H:2, 0:n], ex[0:n, a:H:2, 0:n],
                                    ps[0:n, TS + a, 0:4 * n].rearrange("p (h s) -> p h s", h=4), ALU.mult)
                    v.drain()
                    v.sem_inc(s_P, 1)

            def chunk(t, n, sample, last=False):
                f = g.factors[0:n, :, bass.ds(t, 1), :].rearrange("p x o h -> p x (o h)")
                for a in (1, 0):
                    v.wait_ge(s_N, 2 * t + 4 - a)
                    for b in range(2):
                        hs = slice(4 * a + b, 4 * a + 4, 2)
                        two = ps[0:n, CARRIED[a] + b, 0:2 * AUG].rearrange("p (h v) -> p h v", h=2)
                        V.tensor_tensor(hh[0:n, hs, :], two,
                                        f[:, 0, hs].unsqueeze(2).broadcast_to([n, 2, AUG]), ALU.mult)
                        v.drain()
                        V.tensor_tensor(hh[0:n, hs, :], hh[0:n, hs, :],
                                        ps[0:n, OWN[a] + b, 0:2 * AUG].rearrange("p (h v) -> p h v", h=2), ALU.add)
                    v.drain()
                    v.sem_inc(s_comb, 1)
                for z in range(BATCHES if sample else 1):
                    v.wait_ge(s_U, t + z + 2)
                    for h in range(H):
                        U = ps[half(h), ADDED[h // 2], (h % 2) * AUG:(h % 2 + 1) * AUG]
                        old = Cs[half(h), z, h // 2, :] if sample else C[half(h), h // 2, :]
                        V.scalar_tensor_tensor(out=old, in0=old, scalar=g.decay[half(h), h, bass.ds(t + z, 1)], in1=U,
                                               op0=ALU.mult, op1=ALU.add)
                    v.drain()
                    v.sem_inc(s_C, 1)
                den = hh[0:n, :, DV]
                V.tensor_scalar(dn[0:n, 0, :], den, -1.0, None, ALU.mult)
                v.drain()
                V.tensor_tensor(dn[0:n, 0, :], dn[0:n, 0, :], den, ALU.max)
                v.drain()
                V.tensor_tensor(dn[0:n, 0, :], dn[0:n, 0, :], f[:, 1, :], ALU.max)
                v.drain()
                V.reciprocal(dn[0:n, 1, :], dn[0:n, 0, :])
                v.drain()
                v.wait_ge(s_yT, t + 1)
                yh = y[0:n, :].rearrange("p (h v) -> p h v", h=H)
                V.tensor_tensor(yh, hh[0:n, :, 0:DV], dn[0:n, 1, :].unsqueeze(2).broadcast_to([n, H, DV]), ALU.mult)
                v.drain()
                for h in range(H):
                    V.bn_stats(st[0:n, h, :], yh[:, h, :])
                v.drain()
                for h in range(H):
                    V.bn_aggr(mv[0:n, h, :], st[0:n, h, :])
                v.drain()
                V.tensor_scalar(rs[0:n, :], mv[0:n, :, 1], EPS, None, ALU.add)
                v.drain()
                v.sem_inc(s_var, 1)
                if not sample:
                    weigh(t + 1, NSAMP if last else P, last)
                V.tensor_tensor(yh, yh, mv[0:n, :, 0].unsqueeze(2).broadcast_to([n, H, DV]), ALU.subtract)
                v.drain()
                v.wait_ge(s_gate, t + 1)
                V.tensor_tensor(y[0:n, :], y[0:n, :], sg[0:n, :], ALU.mult)
                v.wait_ge(s_sd, t + 1)
                V.reciprocal(rs[0:n, :], rs[0:n, :])
                v.drain()
                V.tensor_tensor(yh, yh, rs[0:n, :].unsqueeze(2).broadcast_to([n, H, DV]), ALU.mult)
                v.drain()
                v.sem_inc(s_y, 1)

            weigh(0, P, False)
            with v.Fori(0, PT - 1) as t:
                chunk(t, P, False)
            chunk(PT - 1, P, False, True)
            chunk(PT, NSAMP, True)


def norm_steps(nc, v, w, n, ask, answer, have):
    V = nc.vector
    z = w.z[0:n, :]
    for a in range(2):
        V.bn_stats(w.stats[0:n, a, :], z[:, a * HALF:(a + 1) * HALF])
    v.drain()
    V.bn_aggr(w.mv[0:n, :], w.stats[0:n, :, :].rearrange("p a s -> p (a s)"))
    v.drain()
    V.tensor_scalar(w.sd[0:n, :], w.mv[0:n, 1:2], EPS, None, ALU.add)
    v.drain()
    v.sem_inc(ask, 1)
    v.wait_ge(answer, have)
    V.reciprocal(w.sd[0:n, :], w.sd[0:n, :])
    v.drain()
    V.tensor_scalar(z, z, w.mv[0:n, 0:1], w.sd[0:n, 0:1], ALU.subtract, ALU.mult)
    v.drain()
    V.tensor_tensor(z, z, w.g[0:n, :], ALU.mult)
    v.drain()


def stage_out_proj(nc, g, layer, weight):
    with nc.cleanup_on_exit(), ExitStack() as ctx:
        def sb(n, s, d=F32):
            return ctx.enter_context(nc.sbuf_tensor(f"o{layer}_{n}", s, d))

        def sem(n):
            return nc.alloc_semaphore(f"o{layer}_{n}")

        w = Shared()
        wt = sb("w", [P, KD, D])
        rw = sb("rw", [P, KD, E])
        mix = sb("mix", [P, 2, KD, P])
        w.z, w.stats, w.mv, w.sd = sb("z", [P, D]), sb("stats", [P, 2, 6]), sb("mv", [P, 2]), sb("sd", [P, 1])
        w.g, lb = sb("lg", [P, D]), sb("lb", [P, D])
        gate, scale, shift = sb("gate", [P, D]), sb("scale", [P, D]), sb("shift", [P, D])
        h2 = sb("h2", [P, 2, D])
        hT = sb("hT", [P, KD, P])
        ps = ctx.enter_context(nc.psum_tensor(f"o{layer}_ps", [P, 2, D], F32))
        psT = ctx.enter_context(nc.psum_tensor(f"o{layer}_psT", [P, KD, P], F32))
        psR = ctx.enter_context(nc.psum_tensor(f"o{layer}_psR", [P, HALF], F32))
        s_w, s_ld, s_mods, s_mix, s_Y, s_read, s_var, s_sd, s_h2, s_T, s_hT, s_R, s_done, s_z = (sem(x) for x in (
            "w_loaded", "side_loaded", "mods_loaded", "mix_staged", "y_summed", "y_read", "variance", "deviation",
            "h2_ready", "h2_turned", "h2T_ready", "logits_summed", "logits_out", "zero_row"))
        s_st = [sem("h2_stored0"), sem("h2_stored1")]
        block = ctx.enter_context(nc.Block())

        @block.sync
        def _(sp):
            sp.dma_start(wt[:], weight.rearrange("(k p) n -> p k n", p=P)).then_inc(s_w, 16)
            sp.dma_start(w.g[:], g.ln_g[2 * layer:2 * layer + 1, :].broadcast_to([P, D])).then_inc(s_ld, 16)
            sp.dma_start(lb[:], g.ln_b[2 * layer:2 * layer + 1, :].broadcast_to([P, D])).then_inc(s_ld, 16)
            sp.dma_start(rw[:], g.router_w.rearrange("(k p) e -> p k e", p=P)).then_inc(s_ld, 16)
            for which, dst in ((GATE1, gate), (SHIFT2, shift), (SCALE2, scale)):
                load_mods(sp, g, dst, layer, which, False, s_mods)

            def store(t, par, n):
                sp.wait_ge(s_h2, t + 2)
                sp.dma_start(g.h2[bass.ds(t * P, n), :], h2[0:n, par, :]).then_inc(s_st[par], 16)

            with sp.Fori(0, PT // 2) as i:
                for par in range(2):
                    store(i * 2 + par, par, P)
            for which, dst in ((GATE1, gate), (SHIFT2, shift), (SCALE2, scale)):
                load_mods(sp, g, dst, layer, which, True, s_mods)
            store(PT, 0, NSAMP)
            sp.wait_ge(s_z, 1)
            sp.wait_ge(s_st[1], 16 * (PT // 2) + 16)
            sp.dma_start(g.h2[N:N + 1, :], h2[0:1, 1, :]).then_inc(s_st[1], 16)
            sp.wait_ge(s_st[0], 16 * (PT // 2 + 1) + 16)
            sp.wait_ge(s_st[1], 16 * (PT // 2 + 1) + 16)

        @block.gpsimd
        def _(po):
            po.sem_inc(s_mix, 1)

            def stage(t, par, n):
                po.wait_ge(s_Y, t + 1)
                nc.gpsimd.tensor_copy(mix[:, par, :, 0:n], g.mixT[:, :, bass.ds(t * P, n)])
                po.drain()
                po.sem_inc(s_mix, 1)

            with po.Fori(0, PT // 2) as i:
                for par in range(2):
                    stage(i * 2 + par, par, P)
            stage(PT, 0, NSAMP)

        @block.tensor
        def _(pe):
            T = nc.tensor
            pe.sem_inc(s_Y, 2)
            pe.wait_ge(s_w, 16)
            pe.wait_ge(s_ld, 48)

            def route(t, n):
                pe.wait_ge(s_h2, t + 2)
                pe.wait_ge(s_hT, t + 1)
                for k in range(KD):
                    mm = T.transpose(psT[:, k, 0:n], hcur(t)[0:n, k * P:(k + 1) * P], g.ident[0:n, 0:n])
                mm.then_inc(s_T, 1)
                pe.wait_ge(s_hT, t + 2)
                pe.wait_ge(s_done, t + 1)
                for k in range(KD):
                    mm = T.matmul(psR[0:n, 0:E], hT[:, k, 0:n], rw[:, k, :], start=(k == 0), stop=(k == KD - 1))
                mm.then_inc(s_R, 1)

            def project(t, par, n):
                pe.wait_ge(s_mix, t + 2)
                pe.wait_ge(s_read, t + 1)
                for c in range(2):
                    for k in range(KD):
                        mm = T.matmul(ps[0:n, par, c * HALF:(c + 1) * HALF], mix[:, par, k, 0:n],
                                      wt[:, k, c * HALF:(c + 1) * HALF], start=(k == 0), stop=(k == KD - 1))
                mm.then_inc(s_Y, 1)

            slot = [0]

            def hcur(t):
                return h2[:, slot[0], :]

            project(0, 0, P)
            with pe.Fori(0, PT // 2 - 1) as i:
                for par in range(2):
                    t = i * 2 + par
                    project(t + 1, 1 - par, P)
                    slot[0] = par
                    route(t, P)
            project(PT - 1, 1, P)
            slot[0] = 0
            route(PT - 2, P)
            project(PT, 0, NSAMP)
            slot[0] = 1
            route(PT - 1, P)
            slot[0] = 0
            route(PT, NSAMP)

        @block.scalar
        def _(act):
            act.sem_inc(s_hT, 1)
            act.sem_inc(s_done, 1)

            def tile(t, n):
                act.wait_ge(s_var, t + 1)
                nc.scalar.activation(w.sd[0:n, :], w.sd[0:n, :], ACT.Sqrt)
                act.drain()
                act.sem_inc(s_sd, 1)
                act.wait_ge(s_T, t + 1)
                act.wait_ge(s_R, t + 1)
                for z in range(2):
                    nc.scalar.copy(hT[:, z * 4:z * 4 + 4, 0:n], psT[:, z * 4:z * 4 + 4, 0:n])
                act.drain()
                act.sem_inc(s_hT, 1)
                act.wait_ge(s_R, t + 2)
                nc.scalar.copy(g.logits[0:n, bass.ds(t, 1), :].rearrange("p o e -> p (o e)"), psR[0:n, 0:E])
                act.drain()
                act.sem_inc(s_done, 1)

            with act.Fori(0, PT) as t:
                tile(t, P)
            tile(PT, NSAMP)

        @block.vector
        def _(v):
            V = nc.vector
            v.sem_inc(s_read, 2)
            v.sem_inc(s_h2, 1)
            v.sem_inc(s_R, 1)
            v.sem_inc(s_st[0], 16)
            v.sem_inc(s_st[1], 16)
            V.memset(g.logits[:], 0.0)
            v.wait_ge(s_ld, 48)

            def tile(t, par, i, n, mods):
                x = g.x[0:n, bass.ds(t, 1), :].rearrange("p o d -> p (o d)")
                z = w.z[0:n, :]
                v.wait_ge(s_mods, mods)
                v.wait_ge(s_Y, t + 3)
                V.tensor_tensor(z, ps[0:n, par, :], gate[0:n, :], ALU.mult)
                v.drain()
                v.sem_inc(s_read, 1)
                V.scalar_tensor_tensor(out=z, in0=x, scalar=ALPHA, in1=z, op0=ALU.mult, op1=ALU.add)
                v.drain()
                norm_steps(nc, v, w, n, s_var, s_sd, t + 1)
                V.tensor_tensor(x, z, lb[0:n, :], ALU.add)
                v.drain()
                v.wait_ge(s_st[par], 16 * i + 16)
                o = h2[0:n, par, :]
                V.scalar_tensor_tensor(out=o, in0=scale[0:n, :], scalar=1.0, in1=x, op0=ALU.add, op1=ALU.mult)
                v.drain()
                V.tensor_tensor(o, o, shift[0:n, :], ALU.add)
                v.drain()
                v.sem_inc(s_h2, 1)

            with v.Fori(0, PT // 2) as i:
                for par in range(2):
                    tile(i * 2 + par, par, i, P, 48)
            tile(PT, 0, PT // 2, NSAMP, 48 + 3 * 16 * BATCHES)
            v.wait_ge(s_st[1], 16 * (PT // 2) + 16)
            v.wait_ge(s_R, PT + 1)
            V.memset(h2[0:1, 1, :], 0.0)
            v.drain()
            v.sem_inc(s_z, 1)


def stage_route(nc, g, layer):
    with nc.cleanup_on_exit(), ExitStack() as ctx:
        def sb(n, s, d=F32):
            return ctx.enter_context(nc.sbuf_tensor(f"r{layer}_{n}", s, d))

        def sem(n):
            return nc.alloc_semaphore(f"r{layer}_{n}")

        sh3 = [P, TILES, E]
        rb = sb("bias", [P, E])
        sc, sel, work = sb("scores", sh3), sb("sel", sh3), sb("work", sh3)
        oh = [sb("first", sh3), sb("second", sh3)]
        gs, gm, gi = sb("gs", [P, TILES, GROUPS]), sb("gm", [P, TILES, GROUPS]), sb("gi", [P, TILES, GROUPS])
        pr = sb("pairs", [P, TILES, GROUPS, 3])
        mx = sb("mx", [P, TILES])
        ws = sb("ws", [P, TILES])
        both = sb("both", sh3)
        tot = sb("tot", sh3)
        carry = sb("carry", [P, TILES + 1, E])
        place = sb("place", sh3)
        more = sb("more", [P, E, TILES])
        blocks, ends, tmp = sb("blocks", [P, E]), sb("ends", [P, 2, E]), sb("start", [P, E])
        destf = sb("destf", [P, 2, TILES])
        full = sb("full", [P, SLOTS + 1, E])
        slotf = sb("slotf", [P, SLOTS + 1])
        fresh = sb("fresh", [P, SLOTS + 1])
        taken = sb("taken", [P, SLOTS + 1])
        ids = sb("ids", [P, TILES], I32)
        ps = ctx.enter_context(nc.psum_tensor(f"r{layer}_ps", [P, 2, HALF], F32))
        s_ld, s_e, s_oh, s_cnt, s_dest, s_sc = (sem(x) for x in (
            "loaded", "exp_ready", "choices", "counted", "dest_ready", "scattered"))
        block = ctx.enter_context(nc.Block())

        @block.sync
        def _(sp):
            sp.dma_start(rb[:], g.router_b.broadcast_to([P, E])).then_inc(s_ld, 16)
            sp.dma_start(ids[:], g.const["token_ids"]).then_inc(s_ld, 16)
            sp.dma_start(g.slot_token, g.const["no_token"].rearrange("s (p o) -> (s p) o", o=1)).then_inc(s_ld, 16)

        @block.scalar
        def _(act):
            nc.scalar.activation(sc[:], g.logits[:], ACT.Exp, scale=-1.0)
            act.drain()
            act.sem_inc(s_e, 1)

        @block.tensor
        def _(pe):
            pe.wait_ge(s_oh, 1)
            b2 = both[:].rearrange("p t e -> p (t e)")
            nc.tensor.matmul(ps[:, 0, 0:TILES * E], g.tri[:, 2, :], b2, start=True, stop=True)
            nc.tensor.matmul(ps[:, 1, 0:TILES * E], g.ones[:], b2, start=True, stop=True)
            pe.drain()
            pe.sem_inc(s_cnt, 1)

        @block.gpsimd
        def _(po):
            po.wait_ge(s_ld, 48)
            po.wait_ge(s_dest, 1)
            n = 0
            for k in range(2):
                for t in range(TILES):
                    r = rows_of(t)
                    nc.gpsimd.indirect_dma_start(
                        g.slot_token, bass.IndirectOffsetOnAxis(g.dest[0:r, k, t:t + 1], axis=0),
                        ids[0:r, t:t + 1], None).then_inc(s_sc, 16)
                    n += 16
            po.wait_ge(s_sc, n)

        @block.vector
        def _(v):
            V = nc.vector

            def wide(a, n=E):
                return a.unsqueeze(2).broadcast_to([P, TILES, n])

            v.wait_ge(s_ld, 48)
            v.wait_ge(s_e, 1)
            V.tensor_scalar(sc[:], sc[:], 1.0, None, ALU.add)
            v.drain()
            V.reciprocal(sc[:], sc[:])
            v.drain()
            V.tensor_tensor(sel[:], sc[:], rb[:].unsqueeze(1).broadcast_to(sh3), ALU.add)
            v.drain()
            s4 = sel[:].rearrange("p t (g x) -> p t g x", g=GROUPS)
            V.tensor_tensor(pr[:], s4[:, :, :, 0:3], s4[:, :, :, 1:4], ALU.add)
            V.tensor_tensor(gs[:], s4[:, :, :, 0], s4[:, :, :, 3], ALU.add)
            v.drain()
            V.tensor_reduce(gm[:], pr[:], AX, ALU.max)
            v.drain()
            V.tensor_tensor(pr[:, :, :, 0:2], s4[:, :, :, 0:2], s4[:, :, :, 2:4], ALU.add)
            V.tensor_tensor(gs[:], gs[:], gm[:], ALU.max)
            v.drain()
            V.tensor_tensor(gs[:], gs[:], pr[:, :, :, 0], ALU.max)
            v.drain()
            V.tensor_tensor(gs[:], gs[:], pr[:, :, :, 1], ALU.max)
            v.drain()

            def first_largest(values, hot, n):
                down = g.count_down[:, E - n:E].unsqueeze(1).broadcast_to([P, TILES, n])
                V.tensor_reduce(mx[:], values, AX, ALU.max)
                v.drain()
                V.tensor_tensor(hot, values, wide(mx[:], n), ALU.is_equal)
                v.drain()
                V.tensor_tensor(hot, hot, down, ALU.mult)
                v.drain()
                V.tensor_reduce(mx[:], hot, AX, ALU.max)
                v.drain()
                V.tensor_tensor(hot, down, wide(mx[:], n), ALU.is_equal)
                v.drain()

            first_largest(gs[:], gi[:], GROUPS)
            V.tensor_scalar(gm[:], gi[:], -1.0, -NEG, ALU.add, ALU.mult)
            V.tensor_tensor(work[:].rearrange("p t (g x) -> p t g x", g=GROUPS), s4,
                            gi[:].unsqueeze(3).broadcast_to([P, TILES, GROUPS, PER]), ALU.mult)
            v.drain()
            V.tensor_tensor(work[:].rearrange("p t (g x) -> p t g x", g=GROUPS),
                            work[:].rearrange("p t (g x) -> p t g x", g=GROUPS),
                            gm[:].unsqueeze(3).broadcast_to([P, TILES, GROUPS, PER]), ALU.add)
            v.drain()
            first_largest(work[:], oh[0][:], E)
            V.scalar_tensor_tensor(out=work[:], in0=oh[0][:], scalar=4 * NEG, in1=work[:], op0=ALU.mult, op1=ALU.add)
            v.drain()
            first_largest(work[:], oh[1][:], E)
            for k in range(2):
                V.tensor_tensor(work[:], sc[:], oh[k][:], ALU.mult)
                v.drain()
                V.tensor_reduce(g.weight[:, k, :], work[:], AX, ALU.add)
                v.drain()
            V.tensor_tensor(ws[:], g.weight[:, 0, :], g.weight[:, 1, :], ALU.add)
            v.drain()
            V.reciprocal(ws[:], ws[:])
            V.tensor_tensor(both[:], oh[0][:], oh[1][:], ALU.add)
            v.drain()
            for k in range(2):
                V.tensor_tensor(g.weight[:, k, :], g.weight[:, k, :], ws[:], ALU.mult)
            V.memset(both[NSAMP:P, TILES - 1, :], 0.0)
            V.memset(carry[:, 0, :], 0.0)
            v.drain()
            v.sem_inc(s_oh, 1)
            v.wait_ge(s_cnt, 1)
            V.tensor_copy(tot[:].rearrange("p t e -> p (t e)"), ps[:, 1, 0:TILES * E])
            v.drain()
            for t in range(TILES):
                V.tensor_tensor(carry[:, t + 1, :], carry[:, t, :], tot[:, t, :], ALU.add)
                v.drain()
            V.tensor_tensor(more[:], carry[:, TILES, :].unsqueeze(2).broadcast_to([P, E, TILES]),
                            g.steps[:].unsqueeze(1).broadcast_to([P, E, TILES]), ALU.is_gt)
            v.drain()
            V.tensor_reduce(blocks[:], more[:], AX, ALU.add)
            v.drain()
            V.tensor_copy(ends[:, 0, :], blocks[:])
            v.drain()
            a, k = 0, 1
            while k < E:
                V.tensor_tensor(ends[:, 1 - a, k:E], ends[:, a, k:E], ends[:, a, 0:E - k], ALU.add)
                V.tensor_copy(ends[:, 1 - a, 0:k], ends[:, a, 0:k])
                v.drain()
                a, k = 1 - a, 2 * k
            V.tensor_tensor(tmp[:], ends[:, a, :], blocks[:], ALU.subtract)
            V.tensor_tensor(full[:], ends[:, a, :].unsqueeze(1).broadcast_to([P, SLOTS + 1, E]),
                            g.count_up[:].unsqueeze(2).broadcast_to([P, SLOTS + 1, E]), ALU.is_le)
            v.drain()
            V.tensor_reduce(slotf[:], full[:], AX, ALU.add)
            V.tensor_scalar(tmp[:], tmp[:], float(P), None, ALU.mult)
            v.drain()
            V.tensor_scalar(slotf[:], slotf[:], float(E - 1), None, ALU.min)
            V.tensor_tensor(place[:], carry[:, 0:TILES, :], tmp[:].unsqueeze(1).broadcast_to(sh3), ALU.add)
            v.drain()
            V.tensor_copy(g.slot_expert[:], slotf[:])
            V.memset(fresh[:, 0:1], 1.0)
            V.tensor_tensor(fresh[:, 1:], slotf[:, 1:], slotf[:, 0:SLOTS], ALU.is_gt)
            V.tensor_tensor(taken[:], ends[:, a, E - 1:E].broadcast_to([P, SLOTS + 1]), g.count_up[:], ALU.is_gt)
            V.tensor_copy(g.slots_used[:], ends[:, a, E - 1:E])
            v.drain()
            V.tensor_tensor(fresh[:], fresh[:], taken[:], ALU.mult)
            v.drain()
            V.tensor_copy(g.slot_fresh[:], fresh[:])
            V.tensor_tensor(place[:], place[:], ps[:, 0, 0:TILES * E].rearrange("p (t e) -> p t e", e=E), ALU.add)
            v.drain()
            for k in range(2):
                V.tensor_tensor(work[:], place[:], oh[k][:], ALU.mult)
                v.drain()
                V.tensor_reduce(destf[:, k, :], work[:], AX, ALU.add)
                v.drain()
            V.tensor_copy(g.dest[:], destf[:])
            v.drain()
            v.sem_inc(s_dest, 1)


def stage_experts(nc, g, layer):
    with nc.cleanup_on_exit(), ExitStack() as ctx:
        def sb(n, s, d=F32):
            return ctx.enter_context(nc.sbuf_tensor(f"e{layer}_{n}", s, d))

        def sem(n):
            return nc.alloc_semaphore(f"e{layer}_{n}")

        UNIT = KD * FE
        PIECES = 4
        PC = UNIT // PIECES
        raw = sb("raw", [P, 3, UNIT])
        wh, wl = sb("wh", [P, 3, UNIT], F32R), sb("wl", [P, 3, UNIT], F32R)
        tok = sb("tok", [P, 1], I32)
        xg = sb("xg", [P, D])
        xh, xl = sb("xh", [P, KD, P], F32R), sb("xl", [P, KD, P], F32R)
        hid = sb("hid", [P, FE])
        hh, hl = sb("hh", [P, FT, P], F32R), sb("hl", [P, FT, P], F32R)
        y = sb("y", [P, D])
        psX = ctx.enter_context(nc.psum_tensor(f"e{layer}_psX", [P, KD, P], F32))
        psG = ctx.enter_context(nc.psum_tensor(f"e{layer}_psG", [P, 2, FE], F32))
        psH = ctx.enter_context(nc.psum_tensor(f"e{layer}_psH", [P, FT, P], F32))
        psY = ctx.enter_context(nc.psum_tensor(f"e{layer}_psY", [P, 2, HALF], F32))
        s_raw = [sem(f"weights_loaded{z}") for z in range(3)]
        s_hi = [sem(f"upper_parts{z}") for z in range(3)]
        s_lo = [sem(f"lower_parts{z}") for z in range(3)]
        s_used = [sem(f"weights_used{z}") for z in range(3)]
        s_tok, s_ask, s_x, s_xt, s_xh, s_xl = (sem(n) for n in (
            "tokens_loaded", "tokens_known", "rows_gathered", "rows_turned", "xT_upper", "xT_lower"))
        s_silu, s_hid, s_ht, s_hh, s_hl, s_out, s_st, s_fill, s_end = (sem(n) for n in (
            "silu_ready", "hidden_ready", "hidden_turned", "hT_upper", "hT_lower", "y_out", "y_stored", "unused_filled", "passed"))
        block = ctx.enter_context(nc.Block())

        def table(eng, t, at):
            most = E - 1 if t is g.slot_expert else SLOTS
            return eng.value_load(t[0:1, bass.ds(at, 1)], min_val=0, max_val=most)

        def slots(eng, body):
            used = table(eng, g.slots_used, 0)
            with eng.Fori(0, SLOTS) as b:
                with eng.If(used > b):
                    body(b)
                eng.drain()

        @block.sync
        def _(sp):
            def load(e):
                for z, src in enumerate((g.e_gate, g.e_up, g.e_down)):
                    sp.dma_start(raw[:, z, :].rearrange("p (k f) -> p k f", k=KD if z < 2 else FT),
                                 src[bass.ds(e, 1)].rearrange("o (k p) f -> p (o k) f", p=P)).then_inc(s_raw[z], 16)

            load(table(sp, g.slot_expert, 0) + layer * E)

            def slot(b):
                with sp.If(table(sp, g.slot_fresh, b + 1) > 0):
                    e = table(sp, g.slot_expert, b + 1) + layer * E
                    for z, src in enumerate((g.e_gate, g.e_up, g.e_down)):
                        sp.wait_ge(s_lo[z], b * PIECES + PIECES)
                        sp.dma_start(raw[:, z, :].rearrange("p (k f) -> p k f", k=KD if z < 2 else FT),
                                     src[bass.ds(e, 1)].rearrange("o (k p) f -> p (o k) f", p=P)
                                     ).then_inc(s_raw[z], 16)
                with sp.Else():
                    for z in range(3):
                        sp.wait_ge(s_raw[z], b * 16 + 16)
                        sp.sem_inc(s_raw[z], 16)
                sp.drain()

            slots(sp, slot)
            if layer == 0:
                used = table(sp, g.slots_used, 0)
                with sp.Fori(0, SLOTS) as b:
                    with sp.If(used > b):
                        sp.sem_inc(s_fill, 16)
                    with sp.Else():
                        sp.dma_start(g.yrows[bass.ds(b * P, P), :], g.h2[0:P, :]).then_inc(s_fill, 16)
                    sp.drain()
                sp.wait_ge(s_fill, 16 * SLOTS)

        @block.gpsimd
        def _(po):
            def gather(b):
                po.dma_start(tok[:], g.slot_token[bass.ds(b * P, P), :]).then_inc(s_tok, 16)
                po.wait_ge(s_tok, 16 * b + 16)
                po.sem_inc(s_ask, 1)
                nc.gpsimd.indirect_dma_start(xg[:], None, g.h2, bass.IndirectOffsetOnAxis(tok[:], axis=0)
                                             ).then_inc(s_x, 16)

            gather(0)

            def slot(b):
                po.wait_ge(s_xt, b + 1)
                po.wait_ge(s_x, 16 * b + 16)
                gather(b + 1)

            slots(po, slot)

        @block.tensor
        def _(pe):
            T = nc.tensor

            def turn(b):
                pe.wait_ge(s_x, 16 * b + 16)
                pe.sem_inc(s_end, 1)
                for k in range(KD):
                    mm = T.transpose(psX[:, k, :], xg[:, k * P:(k + 1) * P], g.ident[:])
                mm.then_inc(s_xt, 1)

            def product(out, upper, lower, z, piece, n, w, first, last):
                for i in range(n):
                    k = piece * n + i
                    cols = w(k)
                    T.matmul(out, upper[:, k, :], wh[:, z, cols], start=first and i == 0, stop=False)
                    T.matmul(out, upper[:, k, :], wl[:, z, cols], start=False, stop=False)
                    mm = T.matmul(out, lower[:, k, :], wh[:, z, cols], start=False, stop=last and i == n - 1)
                return mm

            def slot(b):
                pe.wait_ge(s_xl, b + 1)
                pe.wait_ge(s_hid, b + 1)
                for z in range(2):
                    for c in range(PIECES):
                        pe.wait_ge(s_lo[z], b * PIECES + c + 1)
                        mm = product(psG[:, z, :], xh, xl, z, c, KD // PIECES, lambda k: slice(k * FE, (k + 1) * FE),
                                     c == 0, c == PIECES - 1)
                    mm.then_inc(s_used[z], 1)
                turn(b + 1)
                pe.wait_ge(s_hid, b + 2)
                pe.sem_inc(s_end, 1)
                for f in range(FT):
                    mm = T.transpose(psH[:, f, :], hid[:, f * P:(f + 1) * P], g.ident[:])
                mm.then_inc(s_ht, 1)
                pe.wait_ge(s_hl, b + 1)
                pe.wait_ge(s_out, b + 1)
                for c in range(PIECES):
                    pe.wait_ge(s_lo[2], b * PIECES + c + 1)
                    for y2 in range(2):
                        mm = product(psY[:, y2, :], hh, hl, 2, c, 1,
                                     lambda k: slice(k * D + y2 * HALF, k * D + (y2 + 1) * HALF),
                                     c == 0, c == PIECES - 1)
                mm.then_inc(s_used[2], 1)

            turn(0)
            slots(pe, slot)

        @block.scalar
        def _(act):
            S = nc.scalar

            def upper(z, b):
                act.wait_ge(s_raw[z], b * 16 + 16)
                for c in range(PIECES):
                    S.copy(wh[:, z, c * PC:(c + 1) * PC], raw[:, z, c * PC:(c + 1) * PC]).then_inc(s_hi[z], 1)

            def next_upper(z, b, fresh):
                with act.If(fresh > 0):
                    act.wait_ge(s_used[z], b + 1)
                    upper(z, b + 1)
                with act.Else():
                    act.sem_inc(s_hi[z], PIECES)
                act.drain()

            def copy_x(b):
                act.wait_ge(s_xt, b + 1)
                for z in range(2):
                    S.copy(xh[:, z * 4:z * 4 + 4, :], psX[:, z * 4:z * 4 + 4, :])
                act.drain()
                act.sem_inc(s_xh, 1)

            def slot(b):
                fresh = table(act, g.slot_fresh, b + 1)
                act.wait_ge(s_used[0], b + 1)
                S.activation(hid[:], psG[:, 0, :], ACT.Silu).then_inc(s_silu, 1)
                next_upper(0, b, fresh)
                act.wait_ge(s_ht, b + 1)
                S.copy(hh[:], psH[:]).then_inc(s_hh, 1)
                copy_x(b + 1)
                next_upper(1, b, fresh)
                act.wait_ge(s_used[2], b + 1)
                act.wait_ge(s_st, 16 * b + 16)
                for z in range(2):
                    S.copy(y[:, z * HALF:(z + 1) * HALF], psY[:, z, :])
                act.drain()
                act.sem_inc(s_out, 1)
                act.dma_start(g.yrows[bass.ds(b * P, P), :], y[:]).then_inc(s_st, 16)
                next_upper(2, b, fresh)

            act.sem_inc(s_st, 16)
            act.sem_inc(s_out, 1)
            for z in range(3):
                upper(z, 0)
            copy_x(0)
            slots(act, slot)
            act.wait_ge(s_st, table(act, g.slots_used, 0) * 16 + 16)
            act.sem_inc(s_end, 1)

        @block.vector
        def _(v):
            V = nc.vector

            def lower(z, b, pieces=range(PIECES)):
                for c in pieces:
                    v.wait_ge(s_hi[z], b * PIECES + c + 1)
                    at = slice(c * PC, (c + 1) * PC)
                    V.tensor_tensor(wl[:, z, at], raw[:, z, at], wh[:, z, at].bitcast(F32), ALU.subtract
                                    ).then_inc(s_lo[z], 1)

            def next_lower(z, b, fresh, pieces=range(PIECES)):
                with v.If(fresh > 0):
                    lower(z, b + 1, pieces)
                with v.Else():
                    v.wait_ge(s_hi[z], b * PIECES + 2 * PIECES)
                    v.sem_inc(s_lo[z], len(pieces))
                v.drain()

            def lower_x(b):
                v.wait_ge(s_xh, b + 1)
                V.tensor_tensor(xl[:], psX[:], xh[:].bitcast(F32), ALU.subtract).then_inc(s_xl, 1)

            def slot(b):
                fresh = table(v, g.slot_fresh, b + 1)
                next_lower(0, b, fresh, range(2))
                v.wait_ge(s_silu, b + 1)
                v.wait_ge(s_used[1], b + 1)
                V.tensor_tensor(hid[:], hid[:], psG[:, 1, :], ALU.mult).then_inc(s_hid, 1)
                v.wait_ge(s_hh, b + 1)
                V.tensor_tensor(hl[:], psH[:], hh[:].bitcast(F32), ALU.subtract).then_inc(s_hl, 1)
                lower_x(b + 1)
                next_lower(0, b, fresh, range(2, PIECES))
                next_lower(1, b, fresh)
                next_lower(2, b, fresh)

            v.sem_inc(s_hid, 1)
            for z in range(3):
                lower(z, 0)
            lower_x(0)
            slots(v, slot)


def stage_combine(nc, g, layer, last):
    with nc.cleanup_on_exit(), ExitStack() as ctx:
        def sb(n, s, d=F32):
            return ctx.enter_context(nc.sbuf_tensor(f"c{layer}_{n}", s, d))

        def sem(n):
            return nc.alloc_semaphore(f"c{layer}_{n}")

        RING = 3
        zr, stats = sb("z", [P, RING, D]), sb("stats", [P, 2, 6])
        mv, sd, off = sb("mv", [P, 2]), sb("sd", [P, 2]), sb("off", [P, 2])
        lg, lb, gate = sb("lg", [P, D]), sb("lb", [P, D]), sb("gate", [P, 2, D])
        ya, yb = sb("ya", [P, 2, D]), sb("yb", [P, 2, D])
        s_ld, s_mods, s_first, s_both, s_gated, s_var, s_sd, s_off, s_norm, s_x, s_st = (sem(x) for x in (
            "side_loaded", "mods_loaded", "first_weighted", "both_summed", "gated", "variance", "deviation",
            "offset_ready", "normalised", "x_ready", "y_stored"))
        s_g = [sem("rows_gathered0"), sem("rows_gathered1")]
        block = ctx.enter_context(nc.Block())

        @block.sync
        def _(sp):
            r = 2 * layer + 1
            sp.dma_start(lg[:], g.ln_g[r:r + 1, :].broadcast_to([P, D])).then_inc(s_ld, 16)
            sp.dma_start(lb[:], g.ln_b[r:r + 1, :].broadcast_to([P, D])).then_inc(s_ld, 16)
            load_mods(sp, g, gate[:, 0, :], layer, GATE2, False, s_mods)
            load_mods(sp, g, gate[:, 1, :], layer, GATE2, True, s_mods)
            if last:
                with sp.Fori(0, PT) as t:
                    sp.wait_ge(s_x, t + 1)
                    sp.dma_start(g.y_prompt[bass.ds(t * P, P), :],
                                 g.x[:, bass.ds(t, 1), :].rearrange("p o d -> p (o d)")).then_inc(s_st, 16)
                sp.wait_ge(s_x, TILES)
                sp.dma_start(g.y_sample, g.x[0:NSAMP, PT, :]).then_inc(s_st, 16)
                sp.wait_ge(s_st, 16 * TILES)

        @block.gpsimd
        def _(po):
            def gather(t):
                n, par = rows_of(t), t % 2
                for k, y in enumerate((ya, yb)):
                    nc.gpsimd.indirect_dma_start(y[0:n, par, :], None, g.yrows,
                                                 bass.IndirectOffsetOnAxis(g.dest[0:n, k, t:t + 1], axis=0)
                                                 ).then_inc(s_g[par], 16)

            gather(0)
            gather(1)
            po.wait_ge(s_mods, 16 + 16 * BATCHES)
            for t in range(TILES):
                n = rows_of(t)
                po.wait_ge(s_both, t + 1)
                z = zr[0:n, t % RING, :]
                nc.gpsimd.tensor_tensor(z, z, gate[0:n, t // PT, :], ALU.mult).then_inc(s_gated, 1)
                if t + 2 < TILES:
                    gather(t + 2)

        @block.scalar
        def _(act):
            def first(t):
                n, par = rows_of(t), t % 2
                act.wait_ge(s_g[par], 32 * (t // 2) + 32)
                if t >= RING:
                    act.wait_ge(s_x, t - RING + 1)
                nc.scalar.activation(zr[0:n, t % RING, :], ya[0:n, par, :], ACT.Copy,
                                     scale=g.weight[0:n, 0, t:t + 1]).then_inc(s_first, 1)

            first(0)
            first(1)
            for t in range(TILES):
                n, par = rows_of(t), t % 2
                act.wait_ge(s_var, t + 1)
                nc.scalar.activation(sd[0:n, par:par + 1], sd[0:n, par:par + 1], ACT.Sqrt).then_inc(s_sd, 1)
                act.wait_ge(s_off, t + 1)
                z = zr[0:n, t % RING, :]
                nc.scalar.activation(z, z, ACT.Identity, bias=off[0:n, par:par + 1], scale=sd[0:n, par:par + 1]
                                     ).then_inc(s_norm, 1)
                if t + 2 < TILES:
                    first(t + 2)

        @block.vector
        def _(v):
            V = nc.vector
            v.wait_ge(s_ld, 32)

            def both(t):
                n, z = rows_of(t), zr[0:rows_of(t), t % RING, :]
                v.wait_ge(s_first, t + 1)
                V.scalar_tensor_tensor(out=z, in0=yb[0:n, t % 2, :], scalar=g.weight[0:n, 1, t:t + 1], in1=z,
                                       op0=ALU.mult, op1=ALU.add).then_inc(s_both, 1)

            def finish(t):
                n, z = rows_of(t), zr[0:rows_of(t), t % RING, :]
                v.wait_ge(s_norm, t + 1)
                V.tensor_tensor(z, z, lg[0:n, :], ALU.mult)
                v.drain()
                V.tensor_tensor(g.x[0:n, t, :], z, lb[0:n, :], ALU.add).then_inc(s_x, 1)

            both(0)
            for t in range(TILES):
                n, par, z = rows_of(t), t % 2, zr[0:rows_of(t), t % RING, :]
                if t + 1 < TILES:
                    both(t + 1)
                v.wait_ge(s_gated, t + 1)
                V.scalar_tensor_tensor(out=z, in0=g.x[0:n, t, :], scalar=ALPHA, in1=z, op0=ALU.mult, op1=ALU.add)
                v.drain()
                for a in range(2):
                    V.bn_stats(stats[0:n, a, :], z[:, a * HALF:(a + 1) * HALF])
                v.drain()
                V.bn_aggr(mv[0:n, :], stats[0:n, :, :].rearrange("p a s -> p (a s)"))
                v.drain()
                s = sd[0:n, par:par + 1]
                V.tensor_scalar(s, mv[0:n, 1:2], EPS, None, ALU.add).then_inc(s_var, 1)
                if t >= 1:
                    finish(t - 1)
                v.wait_ge(s_sd, t + 1)
                V.reciprocal(s, s)
                v.drain()
                V.tensor_scalar(off[0:n, par:par + 1], mv[0:n, 0:1], s, -1.0, ALU.mult, ALU.mult).then_inc(s_off, 1)
            finish(TILES - 1)


def stage_latents(nc, g):
    with nc.cleanup_on_exit(), ExitStack() as ctx:
        def sb(n, s, d=F32):
            return ctx.enter_context(nc.sbuf_tensor(f"l_{n}", s, d))

        def sem(n):
            return nc.alloc_semaphore(f"l_{n}")

        KVA = KVR + ROPE
        half = ROPE // 2
        wkv, wdq = sb("wkv", [P, KD, KVA]), sb("wdq", [P, KD, QR])
        scale, shift = sb("scale", [P, 2, D]), sb("shift", [P, 2, D])
        trig = sb("trig", [P, TILES, 2, half])
        gkv, gq = sb("gkv", [P, KVR]), sb("gq", [P, QR])
        h, xrow = sb("h", [P, D]), sb("xrow", [P, D])
        xT, hT = sb("xT", [P, KD, P]), sb("hT", [P, KD, P])
        junk = sb("junk", [P, QR])
        ss, rs = sb("ss", [P, 2]), sb("rs", [P, 2])
        lat, kr, cq = sb("lat", [P, 2, KVR]), sb("kr", [P, 2, 2, ROPE]), sb("cq", [P, QR])
        r4 = sb("r4", [P, 4, half])
        psT = ctx.enter_context(nc.psum_tensor("l_psT", [P, 2 * KD, P], F32))
        psK = ctx.enter_context(nc.psum_tensor("l_psK", [P, HALF], F32))
        psQ = ctx.enter_context(nc.psum_tensor("l_psQ", [P, HALF], F32))
        psC = ctx.enter_context(nc.psum_tensor("l_psC", [P, 4, P], F32))
        psL = ctx.enter_context(nc.psum_tensor("l_psL", [P, 4, P], F32))
        s_ld, s_mods, s_h, s_T, s_xT, s_mm, s_ss, s_ms, s_sd, s_nrm, s_post, s_out = (sem(x) for x in (
            "side_loaded", "mods_loaded", "h_ready", "turned", "xT_ready", "projected", "squares_summed",
            "mean_squares", "roots", "normalised", "latents_turned", "latents_out"))
        s_st = [sem("rows_stored0"), sem("rows_stored1")]
        block = ctx.enter_context(nc.Block())

        @block.sync
        def _(sp):
            sp.dma_start(wkv[:], g.w_kv_a.rearrange("(k p) n -> p k n", p=P)).then_inc(s_ld, 16)
            sp.dma_start(wdq[:], g.w_dq.rearrange("(k p) n -> p k n", p=P)).then_inc(s_ld, 16)
            sp.dma_start(gkv[:], g.kv_norm_g.broadcast_to([P, KVR])).then_inc(s_ld, 16)
            sp.dma_start(gq[:], g.q_norm_g.broadcast_to([P, QR])).then_inc(s_ld, 16)
            sp.dma_start(trig[:], g.const["trig_tok"]).then_inc(s_ld, 16)
            for z in range(2):
                load_mods(sp, g, shift[:, z, :], 1, SHIFT1, bool(z), s_mods)
                load_mods(sp, g, scale[:, z, :], 1, SCALE1, bool(z), s_mods)

            def store(t, par, n):
                sp.wait_ge(s_nrm, t + 1)
                sp.dma_start(g.lat[bass.ds(t * P, n), :], lat[0:n, par, :]).then_inc(s_st[par], 16)
                sp.dma_start(g.krope[bass.ds(t * P, n), :], kr[0:n, par, 0, :]).then_inc(s_st[par], 16)

            with sp.Fori(0, PT // 2) as i:
                for par in range(2):
                    store(i * 2 + par, par, P)
            store(PT, 0, NSAMP)
            sp.wait_ge(s_st[0], 32 * (PT // 2 + 1) + 32)
            sp.wait_ge(s_st[1], 32 * (PT // 2) + 32)

        @block.tensor
        def _(pe):
            T = nc.tensor
            pe.sem_inc(s_T, 1)
            pe.wait_ge(s_ld, 80)

            def project(t, n):
                pe.wait_ge(s_h, t + 1)
                pe.wait_ge(s_xT, t + 1)
                for k in range(KD):
                    T.transpose(psT[:, k, 0:n], xrow[0:n, k * P:(k + 1) * P], g.ident[0:n, 0:n])
                for k in range(KD):
                    mm = T.transpose(psT[:, KD + k, 0:n], h[0:n, k * P:(k + 1) * P], g.ident[0:n, 0:n])
                mm.then_inc(s_T, 1)
                pe.wait_ge(s_xT, t + 2)
                if not (isinstance(t, int) and t == 0):
                    pe.wait_ge(s_nrm, t)
                for k in range(KD):
                    T.matmul(psK[0:n, 0:KVA], xT[:, k, 0:n], wkv[:, k, :], start=(k == 0), stop=(k == KD - 1))
                for k in range(KD):
                    mm = T.matmul(psQ[0:n, :], hT[:, k, 0:n], wdq[:, k, :], start=(k == 0), stop=(k == KD - 1))
                mm.then_inc(s_mm, 1)

            def turn_latents(t, par, n):
                pe.wait_ge(s_nrm, t + 1)
                pe.wait_ge(s_out, t + 1)
                for k in range(4):
                    T.transpose(psC[:, k, 0:n], cq[0:n, k * P:(k + 1) * P], g.ident[0:n, 0:n])
                for k in range(2):
                    T.transpose(psL[:, k, 0:n], lat[0:n, par, k * P:(k + 1) * P], g.ident[0:n, 0:n])
                T.transpose(psL[:, 2, 0:n], kr[0:n, par, :, :].rearrange("p a r -> p (a r)"),
                            g.ident[0:n, 0:n]).then_inc(s_post, 1)

            project(0, P)
            with pe.Fori(0, PT // 2 - 1) as i:
                for par in range(2):
                    t = i * 2 + par
                    project(t + 1, P)
                    turn_latents(t, par, P)
            project(PT - 1, P)
            turn_latents(PT - 2, 0, P)
            project(PT, NSAMP)
            turn_latents(PT - 1, 1, P)
            turn_latents(PT, 0, NSAMP)

        @block.scalar
        def _(act):
            S = nc.scalar
            act.sem_inc(s_xT, 1)
            act.sem_inc(s_out, 1)

            def front(t, n):
                act.wait_ge(s_T, t + 2)
                if not (isinstance(t, int) and t == 0):
                    act.wait_ge(s_mm, t)
                for z in range(2):
                    S.copy(xT[:, z * 4:z * 4 + 4, 0:n], psT[:, z * 4:z * 4 + 4, 0:n])
                    S.copy(hT[:, z * 4:z * 4 + 4, 0:n], psT[:, KD + z * 4:KD + z * 4 + 4, 0:n])
                act.drain()
                act.sem_inc(s_xT, 1)
                act.wait_ge(s_mm, t + 1)
                S.activation(junk[0:n, 0:KVR], psK[0:n, 0:KVR], ACT.Square, accum_out=ss[0:n, 0:1])
                act.drain()
                S.activation(junk[0:n, :], psQ[0:n, :], ACT.Square, accum_out=ss[0:n, 1:2])
                act.drain()
                act.sem_inc(s_ss, 1)
                act.wait_ge(s_ms, t + 1)
                S.activation(rs[0:n, :], rs[0:n, :], ACT.Sqrt)
                act.drain()
                act.sem_inc(s_sd, 1)

            def back(t, n):
                act.wait_ge(s_post, t + 1)
                S.copy(g.cqT[:, :, bass.ds(t * P, n)], psC[:, :, 0:n])
                S.copy(g.latT[:, :, bass.ds(t * P, n)], psL[:, 0:2, 0:n])
                S.copy(g.krT[:, bass.ds(t * P, n)], psL[:, 2, 0:n])
                act.drain()
                act.sem_inc(s_out, 1)

            front(0, P)
            with act.Fori(0, PT - 1) as t:
                front(t + 1, P)
                back(t, P)
            front(PT, NSAMP)
            back(PT - 1, P)
            back(PT, NSAMP)

        @block.vector
        def _(v):
            V = nc.vector
            v.sem_inc(s_st[0], 32)
            v.sem_inc(s_st[1], 32)
            v.wait_ge(s_ld, 80)
            v.wait_ge(s_mods, 32 + 32 * BATCHES)

            def modulate(t, n, z):
                x = g.x[0:n, bass.ds(t, 1), :].rearrange("p o d -> p (o d)")
                v.wait_ge(s_T, t + 1)
                V.tensor_copy(xrow[0:n, :], x)
                V.scalar_tensor_tensor(out=h[0:n, :], in0=scale[0:n, z, :], scalar=1.0, in1=x,
                                       op0=ALU.add, op1=ALU.mult)
                v.drain()
                V.tensor_tensor(h[0:n, :], h[0:n, :], shift[0:n, z, :], ALU.add)
                v.drain()
                v.sem_inc(s_h, 1)

            def normalise(t, par, i, n):
                v.wait_ge(s_ss, t + 1)
                V.tensor_scalar(rs[0:n, 0:1], ss[0:n, 0:1], 1.0 / KVR, EPS, ALU.mult, ALU.add)
                V.tensor_scalar(rs[0:n, 1:2], ss[0:n, 1:2], 1.0 / QR, EPS, ALU.mult, ALU.add)
                v.drain()
                v.sem_inc(s_ms, 1)
                v.wait_ge(s_st[par], 32 * i + 32)
                if not (isinstance(t, int) and t == 0):
                    v.wait_ge(s_post, t)
                c = trig[0:n, bass.ds(t, 1), 0, :].rearrange("p o r -> p (o r)")
                s = trig[0:n, bass.ds(t, 1), 1, :].rearrange("p o r -> p (o r)")
                a, b = psK[0:n, KVR:KVR + half], psK[0:n, KVR + half:KVA]
                V.tensor_tensor(r4[0:n, 0, :], a, c, ALU.mult)
                V.tensor_tensor(r4[0:n, 1, :], b, s, ALU.mult)
                V.tensor_tensor(r4[0:n, 2, :], a, s, ALU.mult)
                V.tensor_tensor(r4[0:n, 3, :], b, c, ALU.mult)
                v.drain()
                for z in range(2):
                    V.tensor_tensor(kr[0:n, par, z, 0:half], r4[0:n, 0, :], r4[0:n, 1, :], ALU.subtract)
                    V.tensor_tensor(kr[0:n, par, z, half:ROPE], r4[0:n, 2, :], r4[0:n, 3, :], ALU.add)
                v.wait_ge(s_sd, t + 1)
                V.reciprocal(rs[0:n, :], rs[0:n, :])
                v.drain()
                V.scalar_tensor_tensor(out=lat[0:n, par, :], in0=psK[0:n, 0:KVR], scalar=rs[0:n, 0:1],
                                       in1=gkv[0:n, :], op0=ALU.mult, op1=ALU.mult)
                V.scalar_tensor_tensor(out=cq[0:n, :], in0=psQ[0:n, :], scalar=rs[0:n, 1:2], in1=gq[0:n, :],
                                       op0=ALU.mult, op1=ALU.mult)
                v.drain()
                v.sem_inc(s_nrm, 1)

            modulate(0, P, 0)
            with v.Fori(0, PT // 2 - 1) as i:
                for par in range(2):
                    t = i * 2 + par
                    modulate(t + 1, P, 0)
                    normalise(t, par, i, P)
            modulate(PT - 1, P, 0)
            normalise(PT - 2, 0, PT // 2 - 1, P)
            modulate(PT, NSAMP, 1)
            normalise(PT - 1, 1, PT // 2 - 1, P)
            normalise(PT, 0, PT // 2, NSAMP)


def stage_heads(nc, g):
    with nc.cleanup_on_exit(), ExitStack() as ctx:
        def sb(n, s, d=F32):
            return ctx.enter_context(nc.sbuf_tensor(f"a_{n}", s, d))

        def sem(n):
            return nc.alloc_semaphore(f"a_{n}")

        wq, wk = sb("wq", [P, 4, 2 * P]), sb("wk", [P, 2, NOPE])
        wkT, wv = sb("wkT", [P, KVR]), sb("wv", [P, 2, DV])
        trig = sb("trig", [P, N])
        qn, qr, kT = sb("qn", [P, N]), sb("qr", [P, N]), sb("kT", [P, SEQ])
        vv = sb("v", [P, PT, DV])
        pb = sb("p", [P, 2, SEQ])
        pT = sb("pT", [P, 2, PT, P])
        nm, rsum, rinv = sb("nm", [P, 2]), sb("rsum", [P, 2]), sb("rinv", [P, 2])
        psS = ctx.enter_context(nc.psum_tensor("a_psS", [P, 2, SEQ], F32))
        psP = ctx.enter_context(nc.psum_tensor("a_psP", [P, PT, P], F32))
        psJ = ctx.enter_context(nc.psum_tensor("a_psJ", [P, 2, HALF], F32))
        s_c, s_w, s_job, s_ja, s_jv, s_S, s_max, s_exp, s_nrm, s_T, s_pT, s_o = (sem(x) for x in (
            "trig_loaded", "weights_loaded", "job_summed", "jobs_out_act", "jobs_out_dve", "scores", "maxima",
            "exp_ready", "weights_ready", "weights_turned", "pT_ready", "outputs_summed"))
        block = ctx.enter_context(nc.Block())

        RUNS = ((0, HALF), (HALF, HALF), (SEQ, NSAMP))
        JOBS = 11
        ACT_JOBS = 8 + PT

        @block.sync
        def _(sp):
            sp.dma_start(trig[:], g.const["trig_feat"]).then_inc(s_c, 16)
            with sp.Fori(0, H) as h:
                sp.wait_ge(s_job, JOBS * h + JOBS)
                for dst, src in ((wq[:].rearrange("p k n -> p (k n)"), g.w_uq), (wk[:].rearrange("p k n -> p (k n)"), g.w_uk),
                                 (wkT[:], g.w_ukT), (wv[:].rearrange("p k n -> p (k n)"), g.w_uv)):
                    sp.dma_start(dst, src[bass.ds(h, 1)].rearrange("o p n -> (o p) n")).then_inc(s_w, 16)

        @block.tensor
        def _(pe):
            T = nc.tensor
            pe.sem_inc(s_job, JOBS)
            pe.wait_ge(s_c, 16)
            with pe.Fori(0, H) as h:
                A = h * ACT_JOBS + ACT_JOBS
                pe.wait_ge(s_w, 64 * h + 64)
                for r, (lo, n) in enumerate(RUNS):
                    for z in range(2):
                        if z == 0:
                            pe.wait_ge(s_ja, A + r)
                        elif r == 0:
                            pe.wait_ge(s_ja, A - 1)
                        else:
                            pe.wait_ge(s_jv, 3 * h + r)
                        for k in range(4):
                            mm = T.matmul(psJ[:, z, 0:n], wq[:, k, z * P:(z + 1) * P], g.cqT[:, k, lo:lo + n],
                                          start=(k == 0), stop=(k == 3))
                        mm.then_inc(s_job, 1)
                for c in range(2):
                    if c == 0:
                        pe.wait_ge(s_ja, A + 3)
                    else:
                        pe.wait_ge(s_jv, 3 * h + 3)
                    for k in range(2):
                        mm = T.matmul(psJ[:, c, :], wk[:, k, :], g.latT[:, k, c * HALF:(c + 1) * HALF],
                                      start=(k == 0), stop=(k == 1))
                    mm.then_inc(s_job, 1)
                for c in range(2):
                    pe.wait_ge(s_ja, A + 4 + c)
                    for j in range(4):
                        for k in range(2):
                            mm = T.matmul(psJ[:, c, j * DV:(j + 1) * DV],
                                          g.latT[:, k, (c * 4 + j) * P:(c * 4 + j + 1) * P], wv[:, k, :],
                                          start=(k == 0), stop=(k == 1))
                    mm.then_inc(s_job, 1)
                pe.wait_ge(s_ja, A + 6)
                for c in range(2):
                    mm = T.matmul(psJ[:, 0, c * NSAMP:(c + 1) * NSAMP], wkT[:, c * P:(c + 1) * P], qn[:, SEQ:N],
                                  start=True, stop=True)
                mm.then_inc(s_job, 1)

                def scores(i):
                    par, width = i % 2, (i + 1) * P
                    pe.wait_ge(s_exp, h * PT + i + 1)
                    q = slice(i * P, (i + 1) * P)
                    for lo in range(0, width, HALF):
                        hi = min(width, lo + HALF)
                        T.matmul(psS[:, par, lo:hi], qn[:, q], kT[:, lo:hi], start=True, stop=False)
                        last = hi == width
                        mm = T.matmul(psS[:, par, lo:hi], qr[:, q], g.krT[:, lo:hi], start=False, stop=not last)
                        if last:
                            mm = T.matmul(psS[:, par, i * P:width], g.ident[:], g.qmask[:], start=False, stop=True)
                    mm.then_inc(s_S, 1)

                def outputs(i):
                    pe.wait_ge(s_pT, h * PT + i + 2)
                    pe.wait_ge(s_ja, A + 7 + i)
                    for j in range(i + 1):
                        mm = T.matmul(psJ[:, (i + 1) % 2, 0:P], vv[:, j, :], pT[:, i % 2, j, :],
                                      start=(j == 0), stop=(j == i))
                    mm.then_inc(s_o, 1)

                pe.wait_ge(s_ja, A + 7)
                pe.wait_ge(s_jv, 3 * h + 3)
                scores(0)
                for i in range(PT):
                    if i + 1 < PT:
                        scores(i + 1)
                    pe.wait_ge(s_nrm, h * PT + i + 1)
                    pe.wait_ge(s_pT, h * PT + i + 1)
                    for j in range(i + 1):
                        mm = T.transpose(psP[:, j, :], pb[:, i % 2, j * P:(j + 1) * P], g.ident[:])
                    mm.then_inc(s_T, 1)
                    if i >= 1:
                        outputs(i - 1)
                outputs(PT - 1)

        @block.scalar
        def _(act):
            S = nc.scalar
            act.sem_inc(s_ja, ACT_JOBS)
            act.sem_inc(s_exp, 2)
            act.sem_inc(s_pT, 1)
            with act.Fori(0, H) as h:
                J = JOBS * h + JOBS
                for r, (lo, n) in enumerate(RUNS):
                    act.wait_ge(s_job, J + 2 * r + 1)
                    S.copy(qn[:, lo:lo + n], psJ[:, 0, 0:n]).then_inc(s_ja, 1)
                for c in range(2):
                    act.wait_ge(s_job, J + 7 + c)
                    S.copy(kT[:, c * HALF:(c + 1) * HALF], psJ[:, c, :]).then_inc(s_ja, 1)
                for c in range(2):
                    act.wait_ge(s_job, J + 9 + c)
                    S.copy(vv[:, c * 4:c * 4 + 4, :], psJ[:, c, :].rearrange("p (j v) -> p j v", j=4)).then_inc(s_ja, 1)
                act.wait_ge(s_job, J + 11)
                act.wait_ge(s_jv, 3 * h + 3)
                for z in range(3):
                    src = psJ[:, 0, z * NSAMP:(z + 1) * NSAMP] if z < 2 else qr[:, SEQ:N]
                    S.copy(g.qS[:, z, :, bass.ds(h, 1), :].rearrange("p b o t -> p b (o t)"),
                           src.rearrange("p (b t) -> p b t", b=BATCHES))
                act.drain()
                act.sem_inc(s_ja, 1)

                def exp(i):
                    par, width = i % 2, (i + 1) * P
                    act.wait_ge(s_max, h * PT + i + 1)
                    act.wait_ge(s_T, h * PT + i + 1)
                    S.activation(pb[:, par, 0:width], psS[:, par, 0:width], ACT.Exp, bias=nm[:, par:par + 1],
                                 scale=SCALE, accum_out=rsum[:, par:par + 1])
                    act.drain()
                    act.sem_inc(s_exp, 1)

                def output(i):
                    act.wait_ge(s_o, h * PT + i + 3)
                    S.copy(g.mixT[:, bass.ds(h, 1), i * P:(i + 1) * P].rearrange("p o t -> p (o t)"),
                           psJ[:, (i + 1) % 2, 0:P]).then_inc(s_ja, 1)

                exp(0)
                for i in range(PT):
                    if i + 1 < PT:
                        exp(i + 1)
                    act.wait_ge(s_T, h * PT + i + 3)
                    act.wait_ge(s_o, h * PT + i + 1)
                    for lo in range(0, i + 1, 4):
                        hi = min(i + 1, lo + 4)
                        S.copy(pT[:, i % 2, lo:hi, :], psP[:, lo:hi, :])
                    act.drain()
                    act.sem_inc(s_pT, 1)
                    if i >= 1:
                        output(i - 1)
                output(PT - 1)

        @block.vector
        def _(v):
            V = nc.vector
            v.sem_inc(s_T, 2)
            v.sem_inc(s_o, 2)
            v.wait_ge(s_c, 16)
            with v.Fori(0, H) as h:
                for r, (lo, n) in enumerate(RUNS):
                    v.wait_ge(s_job, JOBS * h + JOBS + 2 * r + 2)
                    V.tensor_tensor(qr[:, lo:lo + n], psJ[:, 1, 0:n], trig[:, lo:lo + n], ALU.mult).then_inc(s_jv, 1)

                def maximum(i):
                    par, width = i % 2, (i + 1) * P
                    v.wait_ge(s_S, h * PT + i + 1)
                    V.tensor_reduce(nm[:, par:par + 1], psS[:, par, 0:width], AX, ALU.max)
                    v.drain()
                    V.tensor_scalar(nm[:, par:par + 1], nm[:, par:par + 1], -SCALE, None, ALU.mult)
                    v.drain()
                    v.sem_inc(s_max, 1)

                maximum(0)
                for i in range(PT):
                    par, width = i % 2, (i + 1) * P
                    v.wait_ge(s_exp, h * PT + i + 3)
                    V.reciprocal(rinv[:, par:par + 1], rsum[:, par:par + 1])
                    v.drain()
                    V.tensor_scalar(pb[:, par, 0:width], pb[:, par, 0:width], rinv[:, par:par + 1], None, ALU.mult)
                    v.drain()
                    v.sem_inc(s_nrm, 1)
                    if i + 1 < PT:
                        maximum(i + 1)


def stage_sample(nc, g):
    NQ = H * STEPS
    with nc.cleanup_on_exit(), ExitStack() as ctx:
        def sb(n, s, d=F32):
            return ctx.enter_context(nc.sbuf_tensor(f"s_{n}", s, d))

        def sem(n):
            return nc.alloc_semaphore(f"s_{n}")

        pt = sb("page_table", [1, BATCHES * PAGES], I32)
        KW = 3 * PAGE
        keys = sb("page_keys", [P, 2, PAGES, KW])
        vals = sb("page_values", [P, 2, PAGES, KVR])
        new = sb("new", [STEPS, 2, KVR])
        qB = sb("q", [P, 2, 3, NQ])
        pb = sb("p", [NQ, CTX])
        pT = sb("pT", [P, PAGES + 1, NQ])
        wv = sb("wv", [P, H, 2 * DV])
        oQ = sb("o_rows", [NQ, BATCHES, KVR])
        oS = pT[:, 0:2 * BATCHES, :].rearrange("p (c b) q -> p c b q", c=2)
        nm, rsum = sb("nm", [NQ, 1]), sb("rsum", [NQ, 2])
        psS = ctx.enter_context(nc.psum_tensor("s_psS", [P, 5 * HALF], F32))
        psP = ctx.enter_context(nc.psum_tensor("s_psP", [P, PAGES, NQ], F32))
        psO = ctx.enter_context(nc.psum_tensor("s_psO", [P, HALF], F32))
        s_pt, s_wv, s_q, s_S, s_max, s_exp, s_nrm, s_T, s_pT, s_o, s_oS, s_fin, s_new = (sem(x) for x in (
            "table_loaded", "wv_loaded", "queries_staged", "scores", "maximum", "exp_ready", "weights_ready",
            "weights_turned", "pT_ready", "outputs_summed", "outputs_kept", "values_summed", "new_loaded"))
        s_keys = [sem("keys_loaded0"), sem("keys_loaded1")]
        s_vals = [sem("values_loaded0"), sem("values_loaded1")]
        s_turning = sem("turning")
        block = ctx.enter_context(nc.Block())

        def load_pages(eng, b, par, dst, cols, done):
            for j in range(PAGES):
                page = eng.value_load(pt[0:1, bass.ds(b * PAGES + j, 1)], min_val=0, max_val=g.cache.shape[0] - 1)
                eng.dma_start(dst[:, par, j, :], g.cache[bass.ds(page, 1), :, cols].rearrange("o p n -> (o p) n")
                              ).then_inc(done[par], 16)

        @block.sync
        def _(sp):
            sp.dma_start(pt[:], g.page_table).then_inc(s_pt, 16)
            sp.dma_start(wv[:], g.w_uv.rearrange("h p n -> p h n")).then_inc(s_wv, 16)
            sp.wait_ge(s_pt, 16)
            with sp.Fori(0, BATCHES // 2) as i:
                for par in range(2):
                    b = i * 2 + par
                    sp.wait_ge(s_S, b + 1)
                    load_pages(sp, b, par, keys, slice(0, KW), s_keys)

        @block.gpsimd
        def _(po):
            def stage_queries(b, par):
                po.wait_ge(s_S, b + 1)
                nc.gpsimd.tensor_copy(qB[:, par, :, :].rearrange("p z (h t) -> p z h t", h=H),
                                      g.qS[:, :, bass.ds(b, 1), :, :].rearrange("p z o h t -> p z (o h) t"))
                po.drain()
                po.sem_inc(s_q, 1)

            def values(b, par):
                po.wait_ge(s_o, b + 1)
                load_pages(po, b, par, vals, slice(KW, KVW), s_vals)
                po.dma_start(new[:, par, :], g.lat[bass.ds(SEQ + b * STEPS, STEPS), :]).then_inc(s_vals[par], 16)

            po.wait_ge(s_pt, 16)
            po.sem_inc(s_turning, 1)
            stage_queries(0, 0)
            with po.Fori(0, BATCHES // 2 - 1) as i:
                for par in range(2):
                    stage_queries(i * 2 + par + 1, 1 - par)
                    values(i * 2 + par, par)
            stage_queries(BATCHES - 1, 1)
            values(BATCHES - 2, 0)
            values(BATCHES - 1, 1)

        @block.tensor
        def _(pe):
            T = nc.tensor

            def scores(b, par, i):
                pe.wait_ge(s_q, b + 1)
                pe.wait_ge(s_keys[par], 16 * PAGES * (i + 1))
                pe.wait_ge(s_exp, b + 1)
                for c in range(4):
                    for z in range(3):
                        T.matmul(psS[0:NQ, c * HALF:(c + 1) * HALF], qB[:, par, z, :],
                                 keys[:, par, c * 4:c * 4 + 4, z * PAGE:(z + 1) * PAGE],
                                 start=(z == 0), stop=(z == 2))
                cols = bass.ds(SEQ + b * STEPS, STEPS)
                for z in range(2):
                    T.matmul(psS[0:NQ, PAST:CTX], qB[:, par, z, :],
                             g.latT[:, z, cols], start=(z == 0), stop=False)
                T.matmul(psS[0:NQ, PAST:CTX], qB[:, par, 2, :], g.krT[:, cols], start=False, stop=False)
                T.matmul(psS[0:NQ, PAST:CTX], g.ident[0:NQ, 0:NQ], g.smask[0:NQ, :],
                         start=False, stop=True).then_inc(s_S, 1)

            def turn(b):
                pe.wait_ge(s_nrm, b + 1)
                pe.wait_ge(s_oS, b + 1)
                pe.sem_inc(s_turning, 1)
                for j in range(PAGES):
                    T.transpose(psP[:, j, :], pb[:, j * PAGE:(j + 1) * PAGE], g.ident[0:NQ, 0:NQ])
                T.transpose(psO[0:STEPS, KVR:KVR + NQ], pb[:, PAST:CTX], g.ident[0:NQ, 0:NQ]).then_inc(s_T, 1)

            def outputs(b, par, i):
                pe.wait_ge(s_vals[par], 16 * (PAGES + 1) * (i + 1))
                pe.wait_ge(s_pT, b + 1)
                for j in range(PAGES):
                    T.matmul(psO[0:NQ, 0:KVR], pT[:, j, :], vals[:, par, j, :],
                             start=(j == 0), stop=False)
                T.matmul(psO[0:NQ, 0:KVR], pT[0:STEPS, PAGES, :], new[:, par, :],
                         start=False, stop=True).then_inc(s_o, 1)

            pe.sem_inc(s_o, 2)
            pe.sem_inc(s_S, 2)
            scores(0, 0, 0)
            with pe.Fori(0, BATCHES // 2 - 1) as i:
                for par in range(2):
                    b = i * 2 + par
                    turn(b)
                    scores(b + 1, 1 - par, i + par)
                    outputs(b, par, i)
            turn(BATCHES - 2)
            scores(BATCHES - 1, 1, BATCHES // 2 - 1)
            outputs(BATCHES - 2, 0, BATCHES // 2 - 1)
            turn(BATCHES - 1)
            outputs(BATCHES - 1, 1, BATCHES // 2 - 1)
            pe.wait_ge(s_oS, BATCHES + 1)
            pe.sem_inc(s_turning, 1)
            for b in range(BATCHES):
                for c in range(2):
                    mm = T.transpose(psP[:, c * BATCHES + b, :], oQ[:, b, c * P:(c + 1) * P], g.ident[0:NQ, 0:NQ])
            mm.then_inc(s_T, 1)
            pe.wait_ge(s_oS, BATCHES + 2)
            pe.wait_ge(s_wv, 16)
            for h in range(H):
                for c in range(2):
                    mm = T.matmul(psO[:, h * NSAMP:(h + 1) * NSAMP], wv[:, h, c * DV:(c + 1) * DV],
                                  oS[:, c, :, h * STEPS:(h + 1) * STEPS], start=(c == 0), stop=(c == 1))
            mm.then_inc(s_fin, 1)

        @block.scalar
        def _(act):
            S = nc.scalar
            act.sem_inc(s_exp, 1)
            act.sem_inc(s_oS, 1)

            def exp(b):
                act.wait_ge(s_max, b + 1)
                act.wait_ge(s_T, b + 1)
                S.activation(pb[:], psS[0:NQ, 0:CTX], ACT.Exp, bias=nm[:], scale=SCALE, accum_out=rsum[:, 0:1])
                act.drain()
                act.sem_inc(s_exp, 1)

            def copy_turned(b):
                act.wait_ge(s_T, b + 2)
                act.wait_ge(s_o, b + 2)
                for z in range(2):
                    S.copy(pT[:, z * 8:z * 8 + 8, :], psP[:, z * 8:z * 8 + 8, :])
                S.copy(pT[0:STEPS, PAGES, :], psO[0:STEPS, KVR:KVR + NQ])
                act.drain()
                act.sem_inc(s_pT, 1)

            def keep(b):
                act.wait_ge(s_o, b + 3)
                S.copy(oQ[:, bass.ds(b, 1), :].rearrange("p o n -> p (o n)"), psO[0:NQ, 0:KVR])
                act.drain()
                act.sem_inc(s_oS, 1)

            exp(0)
            with act.Fori(0, BATCHES - 1) as b:
                copy_turned(b)
                exp(b + 1)
                keep(b)
            copy_turned(BATCHES - 1)
            keep(BATCHES - 1)
            act.wait_ge(s_T, BATCHES + 2)
            for c in range(2):
                S.copy(oS[:, c, :, :], psP[:, c * BATCHES:(c + 1) * BATCHES, :])
            act.drain()
            act.sem_inc(s_oS, 1)
            act.wait_ge(s_fin, 1)
            S.copy(g.mixT[:, :, SEQ:N], psO[:].rearrange("p (h t) -> p h t", h=H))

        @block.vector
        def _(v):
            V = nc.vector
            v.sem_inc(s_T, 1)
            with v.Fori(0, BATCHES) as b:
                v.wait_ge(s_S, b + 3)
                V.tensor_reduce(nm[:], psS[0:NQ, 0:CTX], AX, ALU.max)
                v.drain()
                V.tensor_scalar(nm[:], nm[:], -SCALE, None, ALU.mult)
                v.drain()
                v.sem_inc(s_max, 1)
                v.wait_ge(s_exp, b + 2)
                V.reciprocal(rsum[:, 1:2], rsum[:, 0:1])
                v.drain()
                V.tensor_scalar(pb[:], pb[:], rsum[:, 1:2], None, ALU.mult)
                v.drain()
                v.sem_inc(s_nrm, 1)


OUTPUTS = {
    "y_prompt": (SEQ, D), "y_sample": (NSAMP, D),
    "C_p": (P, PAIRS, AUG), "C_s": (P, BATCHES, PAIRS, AUG), "m_out": (H, 1 + BATCHES),
    "lat": (N, KVR), "krope": (N, ROPE),
}


def laid_out(inputs):
    a = {k: np.asarray(v) for k, v in inputs.items()}
    o = {}
    o["x_prompt"] = a["x_prompt"].reshape(SEQ, D)
    o["x_sample"] = a["x_sample"].reshape(NSAMP, D)
    c = np.concatenate([a["c_prompt"], a["c_sample"]], 0)
    o["cT"] = c.T.reshape(KD, P, 9).transpose(1, 0, 2).reshape(P, KD * 9)
    o["ada_w"] = a["ada_w"].reshape(2, KD, P, 12, HALF).transpose(0, 3, 2, 1, 4).reshape(24, P, KD * HALF)
    o["ada_b"] = a["ada_b"].reshape(24, HALF)
    o["ln_g"] = a["ln_g"].reshape(4, D)
    o["ln_b"] = a["ln_b"].reshape(4, D)
    o["a_w_in"] = a["a_w_in"][0]
    o["a_b_gates"] = a["a_b_gates"]
    o["a_norm_g"] = a["a_norm_g"]
    o["a_w_out"] = a["a_w_out"][0]
    st = np.concatenate([a["state_C"][0], a["state_n"][0][..., None]], -1)
    o["state"] = st.reshape(BATCHES, PAIRS, 2, DK, AUG).transpose(2, 3, 0, 1, 4).reshape(P, BATCHES, PAIRS, AUG)
    o["state_mT"] = a["state_m"][0].T
    o["w_kv_a"] = a["b_w_kv_a"]
    o["kv_norm_g"] = a["b_kv_norm_g"].reshape(1, KVR)
    o["q_norm_g"] = a["b_q_norm_g"]
    o["w_dq"] = a["b_w_dq"][0]
    uq = a["b_w_uq"][0].reshape(4, P, H, NOPE + ROPE)
    half = ROPE // 2
    uq = np.concatenate([uq, uq[..., NOPE + half:], uq[..., NOPE:NOPE + half]], -1)
    o["w_uq"] = uq.transpose(2, 1, 0, 3).reshape(H, P, 4 * 2 * P)
    uk, uv = a["b_w_uk"], a["b_w_uv"]
    o["w_uk"] = uk.reshape(2, P, H, NOPE).transpose(2, 1, 0, 3).reshape(H, P, 2 * NOPE)
    o["w_ukT"] = uk.transpose(1, 2, 0)
    o["w_uv"] = uv.reshape(2, P, H, DV).transpose(2, 1, 0, 3).reshape(H, P, 2 * DV)
    o["w_o"] = a["b_w_o"][0]
    o["router_w"] = a["router_w"]
    o["router_b"] = a["router_b"].reshape(1, E)
    for n in ("gate", "up", "down"):
        w = a[f"e_w_{n}"]
        o[f"e_{n}"] = w.reshape((2 * E,) + w.shape[2:])
    cl, ck = a["cache_latent"], a["cache_krope"]
    lt = cl.transpose(0, 2, 1).reshape(-1, 2, P, PAGE).transpose(0, 2, 1, 3).reshape(-1, P, 2 * PAGE)
    kt = ck.transpose(0, 2, 1)
    o["cache"] = np.concatenate([lt, np.concatenate([kt, kt], 1), cl], -1)
    o["page_table"] = a["page_table"].reshape(1, BATCHES * PAGES).astype(np.int32)
    return {k: np.ascontiguousarray(v) for k, v in o.items()}


def constants():
    o = {}
    s, t = np.arange(P)[:, None], np.arange(P)[None, :]
    same = (s // STEPS == t // STEPS) & (s < NSAMP) & (t < NSAMP)
    o["ident"] = np.eye(P)
    o["tri"] = np.stack([s <= t, (s <= t) & same, s < t], 1)
    o["lmask"] = np.stack([np.where(s <= t, 0.0, NEG), np.where((s <= t) & same, 0.0, NEG)], 1)
    o["qmask"] = np.where(t <= s, 0.0, NEG)
    o["smask"] = np.where(np.arange(STEPS)[None, :] <= np.arange(NSAMP)[:, None] % STEPS, 0.0, NEG)
    o["bmask"] = (np.arange(NSAMP)[:, None] // STEPS == np.arange(BATCHES)[None, :])
    o["bmaskT"] = np.broadcast_to(o["bmask"].T.reshape(1, BATCHES, NSAMP), (P, BATCHES, NSAMP))
    o["count_down"] = np.broadcast_to(E - np.arange(E)[None], (P, E))
    o["count_up"] = np.broadcast_to(np.arange(SLOTS + 1)[None], (P, SLOTS + 1))
    o["steps"] = np.broadcast_to(P * np.arange(TILES)[None], (P, TILES))
    pos = np.concatenate([np.arange(SEQ), PAST + np.arange(NSAMP) % STEPS]).astype(np.float32)
    half = ROPE // 2
    inv = (10000.0 ** (-np.arange(half) / half)).astype(np.float32)
    ang = pos[:, None] * inv[None]
    cos, sin = np.cos(ang).astype(np.float32), np.sin(ang).astype(np.float32)
    cs = np.zeros((TILES * P, 2, half), np.float32)
    cs[:N, 0], cs[:N, 1] = cos, sin
    o["trig_tok"] = cs.reshape(TILES, P, 2, half).transpose(1, 0, 2, 3)
    o["trig_feat"] = np.concatenate([cos, cos, -sin, sin], 1).T
    o = {k: np.ascontiguousarray(v, dtype=np.float32) for k, v in o.items()}
    ids = np.arange(TILES * P).reshape(TILES, P).T
    o["token_ids"] = np.ascontiguousarray(ids.astype(np.int32))
    o["no_token"] = np.full((SLOTS + 1, P), N, np.int32)
    return o


CONST_SHAPES = {k: (v.shape, v.dtype) for k, v in constants().items()}
RESIDENT = ("ident", "tri", "lmask", "qmask", "smask", "bmask", "count_down", "count_up", "steps")


def stage_constants(nc, g):
    with nc.cleanup_on_exit(), ExitStack() as ctx:
        s, s_one = nc.alloc_semaphore("constants"), nc.alloc_semaphore("ones")
        block = ctx.enter_context(nc.Block())

        @block.sync
        def _(sp):
            for k in RESIDENT:
                t = g.resident[k]
                sp.dma_start(t[:], g.const[k]).then_inc(s, 16)
            sp.wait_ge(s, 16 * len(RESIDENT))
            sp.wait_ge(s_one, 1)

        @block.vector
        def _(v):
            nc.vector.memset(g.ones[:], 1.0)
            v.drain()
            v.sem_inc(s_one, 1)


def build(nc, ins, const, outs, stages=99):
    g = Shared()
    g.x_prompt = ins["x_prompt"]
    g.x_sample = ins["x_sample"]
    g.cT = ins["cT"]
    g.ada_w = ins["ada_w"]
    g.ada_b = ins["ada_b"]
    g.ln_g = ins["ln_g"]
    g.ln_b = ins["ln_b"]
    g.a_w_in = ins["a_w_in"]
    g.a_b_gates = ins["a_b_gates"]
    g.a_norm_g = ins["a_norm_g"]
    g.a_w_out = ins["a_w_out"]
    g.state = ins["state"]
    g.state_mT = ins["state_mT"]
    g.w_kv_a = ins["w_kv_a"]
    g.kv_norm_g = ins["kv_norm_g"]
    g.q_norm_g = ins["q_norm_g"]
    g.w_dq = ins["w_dq"]
    g.w_uq = ins["w_uq"]
    g.w_uk = ins["w_uk"]
    g.w_ukT = ins["w_ukT"]
    g.w_uv = ins["w_uv"]
    g.w_o = ins["w_o"]
    g.router_w = ins["router_w"]
    g.router_b = ins["router_b"]
    g.e_gate = ins["e_gate"]
    g.e_up = ins["e_up"]
    g.e_down = ins["e_down"]
    g.cache = ins["cache"]
    g.page_table = ins["page_table"]
    g.y_prompt = outs["y_prompt"]
    g.y_sample = outs["y_sample"]
    g.C_p = outs["C_p"]
    g.C_s = outs["C_s"]
    g.m_out = outs["m_out"]
    g.lat = outs["lat"]
    g.krope = outs["krope"]
    g.const = const
    ctx = ExitStack()
    with ctx:
        def dram(n, s, d=F32):
            return nc.dram_tensor(n, s, d, kind="Internal").ap()

        def sb(n, s, d=F32):
            return ctx.enter_context(nc.sbuf_tensor(n, s, d))

        g.mods = dram("mods", [9, 12 * D])
        g.qkvo = dram("qkvo", [N, A_IN])
        g.h2 = dram("h2", [N + 1, D])
        g.yrows = dram("yrows", [SLOTS * P, D])
        g.slot_token = dram("slot_token", [(SLOTS + 1) * P, 1], I32)
        g.x = sb("x", [P, TILES, D])
        g.ones = sb("ones", [P, P])
        g.resident = {}
        for k in RESIDENT:
            shape, _ = CONST_SHAPES[k]
            g.resident[k] = sb(f"c_{k}", list(shape))
        g.ident = g.resident["ident"]
        g.tri = g.resident["tri"]
        g.lmask = g.resident["lmask"]
        g.qmask = g.resident["qmask"]
        g.smask = g.resident["smask"]
        g.bmask = g.resident["bmask"]
        g.count_down = g.resident["count_down"]
        g.count_up = g.resident["count_up"]
        g.steps = g.resident["steps"]
        g.s_w_in = ctx.enter_context(nc.semaphore("w_in_loaded"))
        g.s_x = ctx.enter_context(nc.semaphore("x_loaded"))
        stage_constants(nc, g)
        g.logits = sb("logits", [P, TILES, E])
        g.weight = sb("weight", [P, 2, TILES])
        g.dest = sb("dest", [P, 2, TILES], I32)
        g.slot_expert = sb("slot_expert", [P, SLOTS + 1], I32)
        g.slot_fresh = sb("slot_fresh", [P, SLOTS + 1], I32)
        g.slots_used = sb("slots_used", [P, 1], I32)
        with nc.sbuf_tensor("gates", [P, TILES, GATES], F32) as g.gates:
            with nc.sbuf_tensor("w_in", [P, KD, A_IN + GATES], F32) as g.w_in:
                if stages >= 1:
                    stage_ada(nc, g)
                if stages >= 2:
                    stage_in_proj(nc, g)
            with nc.sbuf_tensor("mixT0", [P, KD, N], F32) as g.mixT:
                with ExitStack() as gated:
                    def gsb(n, s):
                        return gated.enter_context(nc.sbuf_tensor(n, s, F32))

                    g.u = gsb("u", [P, TILES, H])
                    g.factors = gsb("factors", [P, 3, TILES, H])
                    g.decay = gsb("decay", [P, H, 2 * BATCHES])
                    g.M = gsb("M", [H, N])
                    if stages >= 3:
                        stage_gates(nc, g)
                    if stages >= 4:
                        stage_mlstm(nc, g)
                if stages >= 5:
                    stage_out_proj(nc, g, 0, g.a_w_out)
        if stages >= 6:
            stage_route(nc, g, 0)
        if stages >= 7:
            stage_experts(nc, g, 0)
        if stages >= 8:
            stage_combine(nc, g, 0, stages == 8)
        with nc.sbuf_tensor("mixT1", [P, KD, N], F32) as g.mixT:
            with ExitStack() as attending:
                def asb(n, s):
                    return attending.enter_context(nc.sbuf_tensor(n, s, F32))

                g.qS = asb("qS", [P, 3, BATCHES, H, STEPS])
                g.latT = asb("latT", [P, 2, N])
                g.krT = asb("krT", [P, N])
                with nc.sbuf_tensor("cqT", [P, 4, N], F32) as g.cqT:
                    if stages >= 9:
                        stage_latents(nc, g)
                    if stages >= 10:
                        stage_heads(nc, g)
                if stages >= 11:
                    stage_sample(nc, g)
            if stages >= 12:
                stage_out_proj(nc, g, 1, g.w_o)
        if stages >= 13:
            stage_route(nc, g, 1)
            stage_experts(nc, g, 1)
            stage_combine(nc, g, 1, True)
    return g


def kernel(**inputs):
    from concourse import bacc
    from concourse.bass_utils import run_bass_kernel_spmd

    nc = bacc.Bacc("TRN2", target_bir_lowering=False, num_devices=1)
    arrays = laid_out(inputs)
    ins = {k: nc.dram_tensor(f"in_{k}", v.shape, mybir.dt.from_np(v.dtype), kind="ExternalInput").ap()
           for k, v in arrays.items()}
    table = constants()
    const = {k: nc.dram_tensor(f"const_{k}", v.shape, mybir.dt.from_np(v.dtype), kind="ExternalInput").ap()
             for k, v in table.items()}
    outs = {k: nc.dram_tensor(f"out_{k}", list(s), F32, kind="ExternalOutput").ap() for k, s in OUTPUTS.items()}
    build(nc, ins, const, outs)
    fed = {f"in_{k}": v for k, v in arrays.items()} | {f"const_{k}": v for k, v in table.items()}
    r = run_bass_kernel_spmd(nc, [fed], core_ids=[0]).results[0]
    o = {k: r[f"out_{k}"] for k in OUTPUTS}

    def state(c):
        c = c.reshape(2, DK, -1, PAIRS, AUG).transpose(2, 3, 0, 1, 4).reshape(-1, H, DK, AUG)
        return c[None, ..., :DV], c[None, ..., DV]

    Cp, np_ = state(o["C_p"])
    Cs, ns = state(o["C_s"])
    m = o["m_out"].T
    return (o["y_prompt"].reshape(1, SEQ, D), o["y_sample"].reshape(BATCHES, STEPS, D),
            Cp, np_, m[None, 0:1], o["lat"][:SEQ][None], o["krope"][:SEQ][None],
            Cs, ns, m[None, 1:], o["lat"][SEQ:].reshape(BATCHES, STEPS, KVR),
            o["krope"][SEQ:].reshape(BATCHES, STEPS, ROPE))
```

```python
from contextlib import ExitStack

import numpy as np

import concourse.bass as bass
from concourse import mybir

F32 = mybir.dt.float32
F32R = mybir.dt.float32r
I32 = mybir.dt.int32
ALU = mybir.AluOpType
ACT = mybir.ActivationFunctionType
AX = mybir.AxisListType.X

P = 128
D = 1024
KD = D // P
HALF = 512
SEQ = 1024
BATCHES, STEPS = 8, 8
NSAMP = BATCHES * STEPS
N = SEQ + NSAMP
PT = SEQ // P
TILES = PT + 1
H = 8
DK = 64
DV = 128
AUG = DV + 1
PAIRS = H // 2
A_IN = 3072
GATES = 2 * H
KVR, ROPE, QR = 256, 64, 512
NOPE = 128
PAST, PAGE = 2048, 128
PAGES = PAST // PAGE
CTX = PAST + STEPS
KVW = 2 * PAGE + PAGE + KVR
E, GROUPS, PER = 16, 4, 4
FE = 512
FT = FE // P
SLOTS = (2 * N + E * (P - 1)) // P
ALPHA = 4.0 ** 0.25
EPS = 1e-6
SCALE = float(NOPE + ROPE) ** -0.5
NEG = -1.0e30
SHIFT1, SCALE1, GATE1, SHIFT2, SCALE2, GATE2 = range(6)


class Shared:
    pass


def rows_of(t):
    return NSAMP if t is TILES - 1 else P


def load_mods(eng, g, dst, layer, which, sample, sem):
    at = (layer * 6 + which) * D
    if not sample:
        eng.dma_start(dst[:, :], g.mods[0:1, at:at + D].broadcast_to([P, D])).then_inc(sem, 16)
    else:
        for b in range(BATCHES):
            src = g.mods[1 + b:2 + b, at:at + D].broadcast_to([STEPS, D])
            eng.dma_start(dst[b * STEPS:(b + 1) * STEPS, :], src).then_inc(sem, 16)


def stage_ada(nc, g):
    CH = 2 * 6 * D // HALF
    RING = 3
    with nc.cleanup_on_exit(), ExitStack() as ctx:
        def sb(n, s, d=F32):
            return ctx.enter_context(nc.sbuf_tensor(n, s, d))

        def sem(n):
            return nc.alloc_semaphore(f"ada_{n}")

        w = sb("ada_w_ring", [P, RING, KD * HALF])
        bias = sb("ada_bias_ring", [9, RING, HALF])
        out = sb("ada_out", [9, RING, HALF])
        c = sb("ada_c", [P, KD * 9])
        ex = sb("ada_exp", [P, KD * 9])
        sc = sb("ada_silu", [P, KD * 9])
        ps = ctx.enter_context(nc.psum_tensor("ada_ps", [P, RING, HALF], F32))
        s_c, s_exp, s_silu = sem("c_loaded"), sem("c_exp"), sem("silu_ready")
        s_w = [sem(f"w_loaded{i}") for i in range(RING)]
        s_mm, s_ev = sem("chunk_summed"), sem("chunk_out")
        s_st = [sem(f"mods_stored{i}") for i in range(RING)]
        block = ctx.enter_context(nc.Block())

        @block.sync
        def _(sp):
            sp.dma_start(c[:], g.cT).then_inc(s_c, 16)
            with sp.Fori(0, CH // RING) as i:
                for r in range(RING):
                    j = i * RING + r
                    sp.wait_ge(s_mm, j + 1)
                    sp.dma_start(w[:, r, :], g.ada_w[bass.ds(j, 1)].rearrange("o p n -> (o p) n")).then_inc(s_w[r], 16)
                    sp.wait_ge(s_ev, j + 1)
                    sp.dma_start(bias[:, r, :], g.ada_b[bass.ds(j, 1)].broadcast_to([9, HALF])).then_inc(s_w[r], 16)

        @block.scalar
        def _(act):
            act.dma_start(g.x[:, 0:PT, :], g.x_prompt.rearrange("(t p) d -> p t d", p=P)).then_inc(g.s_x, 16)
            act.dma_start(g.x[0:NSAMP, PT, :], g.x_sample).then_inc(g.s_x, 16)
            act.wait_ge(s_c, 16)
            nc.scalar.activation(ex[:], c[:], ACT.Exp, scale=-1.0).then_inc(s_exp, 1)
            with act.Fori(0, CH // RING) as i:
                for r in range(RING):
                    j = i * RING + r
                    act.wait_ge(s_ev, j + 1 + RING)
                    act.dma_start(g.mods[:, bass.ds(j * HALF, HALF)], out[:, r, :]).then_inc(s_st[r], 16)
            for r in range(RING):
                act.wait_ge(s_st[r], 16 * (CH // RING) + 16)

        @block.vector
        def _(v):
            v.wait_ge(s_exp, 1)
            nc.vector.tensor_scalar(ex[:], ex[:], 1.0, None, ALU.add)
            v.drain()
            nc.vector.reciprocal(ex[:], ex[:])
            v.drain()
            nc.vector.tensor_tensor(sc[:], c[:], ex[:], ALU.mult).then_inc(s_silu, 1)
            v.sem_inc(s_ev, RING)
            for r in range(RING):
                v.sem_inc(s_st[r], 16)
            with v.Fori(0, CH // RING) as i:
                for r in range(RING):
                    j = i * RING + r
                    v.wait_ge(s_mm, j + 1 + RING)
                    v.wait_ge(s_w[r], 32 * i + 32)
                    v.wait_ge(s_st[r], 16 * i + 16)
                    nc.vector.tensor_tensor(out[:, r, :], ps[0:9, r, :], bias[:, r, :], ALU.add).then_inc(s_ev, 1)

        @block.tensor
        def _(pe):
            pe.sem_inc(s_mm, RING)
            pe.wait_ge(s_silu, 1)
            with pe.Fori(0, CH // RING) as i:
                for r in range(RING):
                    j = i * RING + r
                    pe.wait_ge(s_w[r], 32 * i + 32)
                    pe.wait_ge(s_ev, j + 1)
                    for k in range(KD):
                        mm = nc.tensor.matmul(ps[0:9, r, :], sc[:, k * 9:(k + 1) * 9],
                                              w[:, r, k * HALF:(k + 1) * HALF], start=(k == 0), stop=(k == KD - 1))
                    mm.then_inc(s_mm, 1)


def stage_in_proj(nc, g):
    CHUNKS = A_IN // HALF
    with nc.cleanup_on_exit(), ExitStack() as ctx:
        def sb(n, s, d=F32):
            return ctx.enter_context(nc.sbuf_tensor(f"in_{n}", s, d))

        def sem(n):
            return nc.alloc_semaphore(f"in_{n}")

        shift, scale, h = sb("shift", [P, 2, D]), sb("scale", [P, 2, D]), sb("h", [P, D])
        hh, hl = sb("h_upper", [P, KD, N], F32R), sb("h_lower", [P, KD, N], F32R)
        raw = sb("w_raw", [P, 2, HALF])
        wh, wl = sb("w_upper", [P, 2, KD, HALF], F32R), sb("w_lower", [P, 2, KD, HALF], F32R)
        graw = sb("gate_raw", [P, KD, GATES])
        gh, gl = sb("gate_upper", [P, KD, GATES], F32R), sb("gate_lower", [P, KD, GATES], F32R)
        out = sb("out", [P, 3, HALF])
        psT = ctx.enter_context(nc.psum_tensor("in_psT", [P, KD, P], F32))
        ps = ctx.enter_context(nc.psum_tensor("in_ps", [P, 3, HALF], F32))
        psG = ctx.enter_context(nc.psum_tensor("in_psG", [P, 2, HALF], F32))
        s_mods, s_gw, s_gh, s_gl, s_h, s_T, s_hh, s_hl, s_hi, s_lo, s_mm, s_ev, s_gm, s_ge = (sem(x) for x in (
            "mods_loaded", "gate_weights_loaded", "gate_upper", "gate_lower", "h_ready", "h_turned",
            "hT_upper", "hT_lower", "w_upper", "w_lower", "tile_summed", "tile_out", "gates_summed", "gates_out"))
        s_turning = sem("turning")
        s_raw = [sem("w_loaded0"), sem("w_loaded1")]
        s_st = [sem("stored_even"), sem("stored_odd"), sem("stored_sample")]
        block = ctx.enter_context(nc.Block())

        def tiles(eng, body):
            with eng.Fori(0, PT // 2) as i:
                for par in range(2):
                    body(i * 2 + par, i, par, P)
            body(PT, 0, 2, NSAMP)

        @block.sync
        def _(sp):
            for z in range(2):
                load_mods(sp, g, shift[:, z, :], 0, SHIFT1, bool(z), s_mods)
                load_mods(sp, g, scale[:, z, :], 0, SCALE1, bool(z), s_mods)
            for c in range(CHUNKS):
                def store(t, i, slot, n):
                    sp.wait_ge(s_ev, TILES * c + t + 2)
                    sp.dma_start(g.qkvo[bass.ds(t * P, n), c * HALF:(c + 1) * HALF], out[0:n, slot, :]
                                 ).then_inc(s_st[slot], 16)

                tiles(sp, store)
            for slot in range(2):
                sp.wait_ge(s_st[slot], 16 * (PT // 2) * CHUNKS + 16)
            sp.wait_ge(s_st[2], 16 * CHUNKS + 16)

        @block.gpsimd
        def _(po):
            po.dma_start(graw[:], g.a_w_in[:, A_IN:A_IN + GATES].rearrange("(k p) n -> p k n", p=P)).then_inc(s_gw, 16)
            for c in range(CHUNKS):
                with po.Fori(0, KD // 2) as i:
                    for par in range(2):
                        k = i * 2 + par
                        po.wait_ge(s_lo, KD * c + k + 1)
                        po.dma_start(raw[:, par, :], g.a_w_in[bass.ds(k * P, P), c * HALF:(c + 1) * HALF]
                                     ).then_inc(s_raw[par], 16)

        def upper(act, c, i, par):
            act.wait_ge(s_raw[par], 16 * (KD // 2) * c + 16 * i + 16)
            nc.scalar.copy(wh[:, c % 2, bass.ds(i * 2 + par, 1), :].rearrange("p o n -> p (o n)"), raw[:, par, :]
                           ).then_inc(s_hi, 1)

        def lower(v, c, i, par):
            v.wait_ge(s_hi, KD * c + i * 2 + par + 1)
            at = (slice(None), c % 2, bass.ds(i * 2 + par, 1), slice(None))
            nc.vector.tensor_tensor(wl[at].rearrange("p o n -> p (o n)"), raw[:, par, :],
                                    wh[at].rearrange("p o n -> p (o n)").bitcast(F32), ALU.subtract).then_inc(s_lo, 1)

        @block.vector
        def _(v):
            nc.vector.memset(g.gates[:], 0.0)
            v.sem_inc(s_lo, 2)
            v.wait_ge(g.s_x, 32)
            v.wait_ge(s_mods, 32 + 32 * BATCHES)

            def modulate(t, n, z):
                v.wait_ge(s_T, t + 1)
                x = g.x[0:n, bass.ds(t, 1), :].rearrange("p o d -> p (o d)")
                nc.vector.scalar_tensor_tensor(out=h[0:n, :], in0=scale[0:n, z, :], scalar=1.0, in1=x,
                                               op0=ALU.add, op1=ALU.mult)
                v.drain()
                nc.vector.tensor_tensor(h[0:n, :], h[0:n, :], shift[0:n, z, :], ALU.add)
                v.drain()
                v.sem_inc(s_h, 1)

            def lower_h(t, n):
                v.wait_ge(s_hh, t + 1)
                at = (slice(None), slice(None), bass.ds(t * P, n))
                nc.vector.tensor_tensor(hl[at], psT[:, :, 0:n], hh[at].bitcast(F32), ALU.subtract).then_inc(s_hl, 1)

            modulate(0, P, 0)
            with v.Fori(0, KD // 2) as i:
                for par in range(2):
                    lower(v, 0, i, par)
            v.wait_ge(s_gh, 1)
            nc.vector.tensor_tensor(gl[:], graw[:], gh[:].bitcast(F32), ALU.subtract).then_inc(s_gl, 1)
            with v.Fori(0, PT // 2 - 1) as i:
                for par in range(2):
                    t = i * 2 + par
                    lower_h(t, P)
                    modulate(t + 1, P, 0)
                    lower(v, 1, i, par)
            lower_h(PT - 2, P)
            modulate(PT - 1, P, 0)
            lower(v, 1, PT // 2 - 1, 0)
            lower_h(PT - 1, P)
            modulate(PT, NSAMP, 1)
            lower(v, 1, PT // 2 - 1, 1)
            lower_h(PT, NSAMP)
            for c in range(2, CHUNKS):
                with v.Fori(0, KD // 2) as i:
                    for par in range(2):
                        lower(v, c, i, par)

        @block.tensor
        def _(pe):
            T = nc.tensor
            pe.sem_inc(s_T, 1)

            def turn(t, n):
                pe.wait_ge(s_h, t + 1)
                if not (isinstance(t, int) and t == 0):
                    pe.wait_ge(s_hl, t)
                    pe.sem_inc(s_turning, 1)
                for k in range(KD):
                    mm = T.transpose(psT[:, k, 0:n], h[0:n, k * P:(k + 1) * P], g.ident[0:n, 0:n])
                mm.then_inc(s_T, 1)

            def product(dst, t, n, high, low):
                for k in range(KD):
                    up, lw = hh[:, k, t * P:t * P + n], hl[:, k, t * P:t * P + n]
                    T.matmul(dst, up, high[:, k, :], start=(k == 0), stop=False)
                    T.matmul(dst, up, low[:, k, :], start=False, stop=False)
                    mm = T.matmul(dst, lw, high[:, k, :], start=False, stop=(k == KD - 1))
                return mm

            def job(c, odd, t):
                n, slot = rows_of(t), t % 2 if t < PT else 2
                pe.wait_ge(s_ev, c * TILES + t)
                product(ps[0:n, slot, :], t, n, wh[:, odd], wl[:, odd]).then_inc(s_mm, 1)

            turn(0, P)
            pe.wait_ge(s_gl, 1)
            pe.wait_ge(s_lo, KD + 2)
            for t in range(TILES):
                if t + 1 < TILES:
                    turn(t + 1, rows_of(t + 1))
                pe.wait_ge(s_hl, t + 1)
                job(0, 0, t)
                pe.wait_ge(s_ge, t + 1)
                product(psG[0:rows_of(t), t % 2, 0:GATES], t, rows_of(t), gh, gl).then_inc(s_gm, 1)

            def chunk(c, odd):
                pe.wait_ge(s_lo, c * KD + KD + 2)
                for t in range(TILES):
                    job(c, odd, t)

            with pe.Fori(0, CHUNKS // 2 - 1) as m:
                chunk(m * 2 + 1, 1)
                chunk(m * 2 + 2, 0)
            chunk(CHUNKS - 1, 1)

        @block.scalar
        def _(act):
            act.sem_inc(s_ev, 1)
            act.sem_inc(s_ge, 2)
            for slot in range(3):
                act.sem_inc(s_st[slot], 16)
            act.wait_ge(s_gw, 16)
            nc.scalar.copy(gh[:], graw[:]).then_inc(s_gh, 1)
            with act.Fori(0, KD // 2) as i:
                for par in range(2):
                    upper(act, 0, i, par)

            def leave(c, t, i, slot, n):
                act.wait_ge(s_mm, TILES * c + t + 1)
                act.wait_ge(s_st[slot], (c if slot == 2 else (PT // 2) * c + i) * 16 + 16)
                nc.scalar.activation(out[0:n, slot, :], ps[0:n, slot, :],
                                     ACT.Sigmoid if c >= 4 else ACT.Copy).then_inc(s_ev, 1)

            def first(t, i, slot, n):
                act.wait_ge(s_T, t + 2)
                for z in range(2):
                    nc.scalar.copy(hh[:, z * 4:z * 4 + 4, bass.ds(t * P, n)], psT[:, z * 4:z * 4 + 4, 0:n])
                act.drain()
                act.sem_inc(s_hh, 1)

            def second(t, i, slot, n):
                leave(0, t, i, slot, n)
                act.wait_ge(s_gm, t + 1)
                nc.scalar.copy(g.gates[0:n, bass.ds(t, 1), :].rearrange("p o d -> p (o d)"),
                               psG[0:n, slot % 2, 0:GATES]).then_inc(s_ge, 1)

            first(0, 0, 0, P)
            with act.Fori(0, PT // 2 - 1) as i:
                for par in range(2):
                    t = i * 2 + par
                    upper(act, 1, i, par)
                    first(t + 1, i, par, P)
                    second(t, i, par, P)
            upper(act, 1, PT // 2 - 1, 0)
            first(PT - 1, 0, 0, P)
            second(PT - 2, PT // 2 - 1, 0, P)
            upper(act, 1, PT // 2 - 1, 1)
            first(PT, 0, 0, NSAMP)
            second(PT - 1, PT // 2 - 1, 1, P)
            second(PT, 0, 2, NSAMP)
            for c in range(1, CHUNKS):
                def rest(t, i, slot, n):
                    leave(c, t, i, slot, n)
                    if slot < 2 and c + 1 < CHUNKS:
                        upper(act, c + 1, i, slot)

                tiles(act, rest)


def stage_gates(nc, g):
    with nc.cleanup_on_exit(), ExitStack() as ctx:
        def sb(n, s, d=F32):
            return ctx.enter_context(nc.sbuf_tensor(n, s, d))

        def sem(n):
            return nc.alloc_semaphore(f"g_{n}")

        bg = sb("g_bias", [P, GATES])
        mn = sb("g_min", [P, TILES, H])
        ab = sb("g_abs", [P, TILES, H])
        lf = sb("g_logf", [P, TILES, H])
        btok = sb("g_btok", [P, TILES, H])
        bh = sb("g_bh", [H, N])
        uh = sb("g_uh", [H, N])
        ca = sb("g_ca", [H, N])
        cb = sb("g_cb", [H, N])
        e3 = sb("g_e3", [H, 3, N])
        mend = sb("g_mend", [H, 2 * BATCHES])
        bend = sb("g_bend", [H, 2 * BATCHES])
        dec = sb("g_dec", [H, 2 * BATCHES])
        decd = sb("g_decd", [H, H, 2 * BATCHES])
        mprev = sb("g_mprev", [H, 2 * BATCHES])
        mout = sb("g_mout", [H, 1 + BATCHES])
        psb = ctx.enter_context(nc.psum_tensor("g_psb", [P, HALF], F32))
        psh = ctx.enter_context(nc.psum_tensor("g_psh", [P, 6, HALF], F32))
        s_ld, s_ab, s_e, s_ln, s_lf, s_b, s_u, s_t = (sem(x) for x in (
            "loaded", "abs_ready", "exp_ready", "ln_ready", "logf_ready", "b_summed", "u_ready", "turned_in"))
        s_args, s_exps, s_dd, s_back, s_st, s_gates = (sem(x) for x in (
            "exp_args", "exps_ready", "decay_diag", "turned_back", "m_stored", "gates_out"))
        block = ctx.enter_context(nc.Block())
        CP, CS = P, STEPS
        NC = PT + BATCHES

        def chunks(a):
            return (a[:, 0:SEQ].rearrange("h (c t) -> h c t", t=CP), a[:, SEQ:N].rearrange("h (c t) -> h c t", t=CS))

        @block.sync
        def _(sp):
            sp.dma_start(bg[:], g.a_b_gates.broadcast_to([P, GATES])).then_inc(s_ld, 16)
            sp.dma_start(mprev[:, PT:NC], g.state_mT).then_inc(s_ld, 16)
            sp.wait_ge(s_args, 1)
            sp.dma_start(g.m_out, mout[:]).then_inc(s_st, 16)
            sp.wait_ge(s_st, 16)

        @block.vector
        def _(v):
            V = nc.vector
            v.wait_ge(s_ld, 32)
            V.tensor_tensor(g.gates[:], g.gates[:], bg[:].unsqueeze(1).broadcast_to([P, TILES, GATES]), ALU.add)
            v.drain()
            xf = g.gates[:, :, H:GATES]
            V.tensor_scalar(mn[:], xf, 0.0, None, ALU.min)
            V.tensor_scalar(ab[:], xf, 0.0, None, ALU.max)
            v.drain()
            V.tensor_tensor(ab[:], mn[:], ab[:], ALU.subtract)
            v.drain()
            v.sem_inc(s_ab, 1)
            v.wait_ge(s_e, 1)
            V.tensor_scalar(ab[:], ab[:], 1.0, None, ALU.add)
            v.drain()
            v.sem_inc(s_ab, 1)
            v.wait_ge(s_ln, 1)
            V.tensor_tensor(lf[:], mn[:], ab[:], ALU.subtract)
            v.drain()
            v.sem_inc(s_lf, 1)
            v.wait_ge(s_b, 1)
            V.tensor_copy(btok[:, 0:PT, :], psb[:, 0:PT * H].rearrange("p (t h) -> p t h", h=H))
            V.memset(btok[:, PT, :], 0.0)
            v.drain()
            V.tensor_copy(btok[0:NSAMP, PT, :], psb[0:NSAMP, 128:128 + H])
            v.drain()
            V.tensor_tensor(g.u[:], g.gates[:, :, 0:H], btok[:], ALU.subtract)
            v.drain()
            v.sem_inc(s_u, 1)
            v.wait_ge(s_t, 1)
            V.tensor_copy(uh[:, 0:SEQ], psh[0:H, 0:2, :])
            V.tensor_copy(uh[:, SEQ:N], psh[0:H, 4, 0:NSAMP])
            V.tensor_copy(bh[:, 0:SEQ], psh[0:H, 2:4, :])
            V.tensor_copy(bh[:, SEQ:N], psh[0:H, 4, NSAMP:2 * NSAMP])
            v.drain()
            V.tensor_copy(ca[:], uh[:])
            v.drain()
            src, dst = ca, cb
            k = 1
            while k < CP:
                for part, n in zip(range(2), (CP, CS)):
                    s, d = chunks(src)[part], chunks(dst)[part]
                    if k < n:
                        V.tensor_tensor(d[:, :, k:n], s[:, :, k:n], s[:, :, 0:n - k], ALU.max)
                        V.tensor_copy(d[:, :, 0:k], s[:, :, 0:k])
                    else:
                        V.tensor_copy(d, s)
                v.drain()
                src, dst = dst, src
                k *= 2
            cm, tmp = src, dst
            for part, (lo, n) in enumerate(((0, CP), (PT, CS))):
                V.tensor_copy(mend[:, lo:lo + PT], chunks(cm)[part][:, :, n - 1])
                V.tensor_copy(bend[:, lo:lo + PT], chunks(bh)[part][:, :, n - 1])
            V.memset(mprev[:, 0:1], 0.0)
            v.drain()
            for c in range(PT):
                V.tensor_tensor(mend[:, c:c + 1], mend[:, c:c + 1], mprev[:, c:c + 1], ALU.max)
                v.drain()
                nxt = mprev[:, c + 1:c + 2] if c + 1 < PT else mout[:, 0:1]
                V.tensor_tensor(nxt, mend[:, c:c + 1], bend[:, c:c + 1], ALU.add)
                v.drain()
            V.tensor_tensor(mend[:, PT:NC], mend[:, PT:NC], mprev[:, PT:NC], ALU.max)
            v.drain()
            V.tensor_tensor(mout[:, 1:1 + BATCHES], mend[:, PT:NC], bend[:, PT:NC], ALU.add)
            for part, (lo, n) in enumerate(((0, CP), (PT, CS))):
                mp = mprev[:, lo:lo + PT].unsqueeze(2).broadcast_to([H, PT, n])
                me = mend[:, lo:lo + PT].unsqueeze(2).broadcast_to([H, PT, n])
                M = chunks(g.M)[part]
                V.tensor_tensor(M, chunks(cm)[part], mp, ALU.max)
                v.drain()
                V.tensor_tensor(chunks(e3[:, 0, :])[part], mp, M, ALU.subtract)
                V.tensor_tensor(chunks(tmp)[part], chunks(bh)[part], M, ALU.add)
                V.tensor_tensor(chunks(e3[:, 2, :])[part], chunks(uh)[part], me, ALU.subtract)
            v.drain()
            V.tensor_scalar(e3[:, 1, :], tmp[:], -1.0, None, ALU.mult)
            V.tensor_tensor(dec[:], mprev[:], mend[:], ALU.subtract)
            v.drain()
            v.sem_inc(s_args, 1)
            v.wait_ge(s_exps, 1)
            V.tensor_tensor(decd[:], g.ident[0:H, 0:H].unsqueeze(2).broadcast_to([H, H, NC]),
                            dec[:].unsqueeze(1).broadcast_to([H, H, NC]), ALU.mult)
            v.drain()
            v.sem_inc(s_dd, 1)
            v.wait_ge(s_back, 1)
            V.memset(g.factors[:], 0.0)
            v.drain()
            for x in range(3):
                V.tensor_copy(g.factors[:, x, 0:PT, :], psh[:, x, 0:PT * H].rearrange("p (t h) -> p t h", h=H))
                V.tensor_copy(g.factors[0:NSAMP, x, PT, :], psh[0:NSAMP, x, PT * H:TILES * H])
            V.tensor_copy(g.decay[:], psh[:, 3, 0:H * NC].rearrange("p (h c) -> p h c", h=H))

        @block.scalar
        def _(act):
            act.wait_ge(s_ab, 1)
            nc.scalar.activation(ab[:], ab[:], ACT.Exp)
            act.drain()
            act.sem_inc(s_e, 1)
            act.wait_ge(s_ab, 2)
            nc.scalar.activation(ab[:], ab[:], ACT.Ln)
            act.drain()
            act.sem_inc(s_ln, 1)
            act.wait_ge(s_args, 1)
            nc.scalar.activation(e3[:], e3[:], ACT.Exp)
            nc.scalar.activation(dec[:], dec[:], ACT.Exp)
            act.drain()
            act.sem_inc(s_exps, 1)

        @block.tensor
        def _(pe):
            T = nc.tensor
            pe.wait_ge(s_lf, 1)
            T.matmul(psb[:, 0:PT * H], g.tri[:, 0, :], lf[:, 0:PT, :], start=True, stop=True)
            T.matmul(psb[0:NSAMP, 128:128 + H], g.tri[0:NSAMP, 1, 0:NSAMP], lf[0:NSAMP, PT, :],
                     start=True, stop=True)
            pe.drain()
            pe.sem_inc(s_b, 1)
            pe.wait_ge(s_u, 1)
            for bank, src in ((0, g.u), (2, btok)):
                for t in range(PT):
                    T.transpose(psh[0:H, bank + t // 4, (t % 4) * P:(t % 4 + 1) * P], src[:, t, :], g.ident[:])
                o = 0 if bank == 0 else NSAMP
                T.transpose(psh[0:H, 4, o:o + NSAMP], src[0:NSAMP, PT, :], g.ident[0:NSAMP, 0:NSAMP])
            pe.drain()
            pe.sem_inc(s_t, 1)
            pe.wait_ge(s_dd, 1)
            for x in range(3):
                for t in range(TILES):
                    n = rows_of(t)
                    T.transpose(psh[0:n, x, t * H:(t + 1) * H], e3[:, x, t * P:t * P + n], g.ident[0:H, 0:H])
            T.matmul(psh[:, 3, 0:H * NC], g.ones[0:H, :], decd[:], start=True, stop=True)
            pe.drain()
            pe.sem_inc(s_back, 1)


def stage_mlstm(nc, g):
    with nc.cleanup_on_exit(), ExitStack() as ctx:
        def sb(n, s, d=F32):
            return ctx.enter_context(nc.sbuf_tensor(n, s, d))

        def sem(n):
            return nc.alloc_semaphore(f"m_{n}")

        qkvo = sb("m_qkvo", [P, 2, A_IN])
        qT = sb("m_qT", [P, PAIRS, P])
        kT = sb("m_kT", [P, PAIRS, P])
        negid = sb("m_negid", [H, H])
        kfac = sb("m_kfac", [P, TILES, H])
        Md = sb("m_Md", [H, H, P])
        mask = [sb("m_mask_prompt", [P, 4, P]), sb("m_mask_sample", [P, 4, NSAMP])]
        ex = sb("m_ex", [P, H, P])
        va = sb("m_va", [P, H, AUG])
        kw = sb("m_kw", [P, H, DK])
        kwb = sb("m_kwb", [NSAMP, BATCHES, H * DK])
        qb = sb("m_qb", [P, BATCHES, PAIRS, NSAMP])
        C = sb("m_C", [P, PAIRS, AUG])
        Cs = sb("m_Cs", [P, BATCHES, PAIRS, AUG])
        hh = sb("m_hh", [P, H, AUG])
        sg = sb("m_sg", [P, D])
        y = sb("m_y", [P, D])
        ng = sb("m_ng", [P, D])
        dn = sb("m_dn", [P, 2, H])
        st = sb("m_st", [P, H, 6])
        mv = sb("m_mv", [P, H, 2])
        rs = sb("m_rs", [P, H])
        bmT = sb("m_bmT", [P, BATCHES, NSAMP])
        ps = ctx.enter_context(nc.psum_tensor("m_ps", [P, 8, HALF], F32))
        TS, AA, NN, QQ = 0, 2, 4, 6
        OWN, CARRIED = (NN, TS), (QQ, AA)
        ADDED = (NN, NN + 1, QQ, QQ + 1)
        s_ld = [sem("qkvo_loaded0"), sem("qkvo_loaded1")]
        s_c, s_T, s_qk, s_Md, s_A, s_E, s_S, s_P, s_kv = (sem(x) for x in (
            "side_loaded", "qk_turned", "qkT_ready", "M_diag", "exponents", "exp_ready", "scores", "weighted", "keys_values_ready"))
        s_N, s_comb, s_U, s_C, s_free, s_var, s_sd, s_gate, s_y, s_yT, s_out, s_set, s_qb, s_st, s_turning = (sem(x) for x in (
            "heads_summed", "heads_combined", "state_added", "state_ready", "slot_read", "variance",
            "deviation", "gate_ready", "y_ready", "y_turned", "y_out", "tables_set", "by_batch", "states_stored", "turning"))
        block = ctx.enter_context(nc.Block())

        @block.sync
        def _(sp):
            sp.dma_start(ng[:], g.a_norm_g.broadcast_to([P, D])).then_inc(s_c, 16)
            sp.dma_start(Cs[:], g.state).then_inc(s_c, 16)
            sp.dma_start(bmT[:], g.const["bmaskT"]).then_inc(s_c, 16)
            with sp.Fori(0, PT // 2) as i:
                for par in range(2):
                    t = i * 2 + par
                    sp.wait_ge(s_free, t + 1)
                    sp.dma_start(qkvo[:, par, :], g.qkvo[bass.ds(t * P, P), :]).then_inc(s_ld[par], 16)
            sp.wait_ge(s_free, PT + 1)
            sp.dma_start(qkvo[0:NSAMP, 0, :], g.qkvo[SEQ:N, :]).then_inc(s_ld[0], 16)
            sp.wait_ge(s_C, PT)
            sp.dma_start(g.C_p, C[:]).then_inc(s_st, 16)
            sp.wait_ge(s_C, PT + BATCHES)
            sp.dma_start(g.C_s, Cs[:]).then_inc(s_st, 16)
            sp.wait_ge(s_st, 32)

        def half(h):
            return slice(DK * (h % 2), DK * (h % 2) + DK)

        @block.tensor
        def _(pe):
            T = nc.tensor

            def front(t, par, i, n, sample):
                pe.wait_ge(s_ld[par], 16 * i + 16)
                if not (isinstance(t, int) and t == 0):
                    pe.wait_ge(s_comb, 2 * t)
                    pe.sem_inc(s_turning, 1)
                for z in range(2):
                    for p in range(PAIRS):
                        mm = T.transpose(ps[:, TS + z, p * P:p * P + n],
                                         qkvo[0:n, par, z * 512 + p * P:z * 512 + (p + 1) * P], g.ident[0:n, 0:n])
                mm.then_inc(s_T, 1)
                pe.wait_ge(s_Md, t + 1)
                for a in range(2):
                    T.matmul(ps[0:n, AA + a, 0:4 * n], g.ident[0:n, 0:n], mask[sample][0:n, :, 0:n],
                             start=True, stop=False)
                    mm = T.matmul(ps[0:n, AA + a, 0:4 * n], g.ones[0:H, 0:n], Md[:, a * 4:a * 4 + 4, 0:n],
                                  start=False, stop=True)
                mm.then_inc(s_A, 1)

            def scores(t, n):
                pe.wait_ge(s_qk, t + 1)
                for h in range(H):
                    T.matmul(ps[0:n, TS + h % 2, (h // 2) * n:(h // 2 + 1) * n], kT[half(h), h // 2, 0:n],
                             qT[half(h), h // 2, 0:n], start=True, stop=True, skip_group_check=True)
                pe.drain()
                pe.sem_inc(s_S, 1)

            def products(t, n, sample, a):
                if sample and a == 1:
                    pe.wait_ge(s_qb, 1)
                if a == 1:
                    pe.wait_ge(s_P, 2 * t + 2)
                else:
                    pe.wait_ge(s_out, t + 1)
                for h in range(4 * a, 4 * a + 4):
                    b, o = h % 2, (h // 2 % 2) * AUG
                    T.matmul(ps[0:n, OWN[a] + b, o:o + AUG], ex[0:n, h, 0:n], va[0:n, h, :],
                             start=True, stop=True, skip_group_check=True)
                    if not sample:
                        T.matmul(ps[0:n, CARRIED[a] + b, o:o + AUG], qT[half(h), h // 2, 0:n], C[half(h), h // 2, :],
                                 start=True, stop=True, skip_group_check=True)
                    else:
                        for z in range(BATCHES):
                            T.matmul(ps[0:n, CARRIED[a] + b, o:o + AUG], qb[half(h), z, h // 2, :],
                                     Cs[half(h), z, h // 2, :], start=(z == 0), stop=(z == BATCHES - 1),
                                     skip_group_check=True)
                pe.drain()
                pe.sem_inc(s_N, 1)

            def add(t, n, sample):
                pe.wait_ge(s_comb, 2 * t + 3)
                if not sample:
                    for p in range(PAIRS):
                        mm = T.matmul(ps[:, ADDED[p], 0:2 * AUG],
                                      kw[:, 2 * p:2 * p + 2, :], va[:, 2 * p:2 * p + 2, :], start=True, stop=True)
                    mm.then_inc(s_U, 1)
                else:
                    for z in range(BATCHES):
                        if z >= 1:
                            pe.wait_ge(s_C, PT + z)
                        for p in range(PAIRS):
                            mm = T.matmul(ps[:, ADDED[p], 0:2 * AUG],
                                          kwb[:, z, p * P:(p + 1) * P], va[0:n, 2 * p:2 * p + 2, :],
                                          start=True, stop=True)
                        mm.then_inc(s_U, 1)

            def turn_y(t, n):
                pe.wait_ge(s_C, t + (BATCHES if n == NSAMP else 1))
                pe.wait_ge(s_y, t + 2)
                pe.sem_inc(s_turning, 1)
                for k in range(KD):
                    mm = T.transpose(ps[:, NN + k // 4, (k % 4) * P:(k % 4) * P + n], y[0:n, k * P:(k + 1) * P],
                                     g.ident[0:n, 0:n])
                mm.then_inc(s_yT, 1)

            pe.sem_inc(s_A, 1)
            pe.sem_inc(s_U, 1)
            pe.sem_inc(s_yT, 1)
            pe.wait_ge(s_set, 1)
            front(0, 0, 0, P, 0)
            scores(0, P)
            products(0, P, False, 1)
            products(0, P, False, 0)
            add(0, P, False)

            def step(t, par, i, n, last):
                front(t, par, i, n, int(last))
                scores(t, n)
                products(t, n, last, 1)
                turn_y(t - 1, P)
                products(t, n, last, 0)
                add(t, n, last)

            with pe.Fori(0, PT // 2 - 1) as i:
                for par in range(2):
                    step(i * 2 + par + 1, 1 - par, i + par, P, False)
            step(PT - 1, 1, PT // 2 - 1, P, False)
            step(PT, 0, PT // 2, NSAMP, True)
            turn_y(PT, NSAMP)

        @block.gpsimd
        def _(po):
            G = nc.gpsimd
            G.memset(va[:, :, DV:AUG], 1.0)
            po.sem_inc(s_free, 2)
            po.wait_ge(s_c, 48)
            po.wait_ge(s_set, 1)

            def chunk(t, par, i, n):
                po.wait_ge(s_A, t + 1)
                G.tensor_tensor(Md[:, :, 0:n], g.M[:, bass.ds(t * P, n)].unsqueeze(1).broadcast_to([H, H, n]),
                                negid[:].unsqueeze(2).broadcast_to([H, H, n]), ALU.mult)
                po.drain()
                po.sem_inc(s_Md, 1)
                po.wait_ge(s_ld[par], 16 * i + 16)
                po.wait_ge(s_U, t + 1)
                L = qkvo[0:n, par, :]
                f = kfac[0:n, bass.ds(t, 1), :].rearrange("p o h -> p (o h)")
                G.tensor_tensor(kw[0:n, :, :], L[:, 512:D].rearrange("p (h k) -> p h k", h=H),
                                f.unsqueeze(2).broadcast_to([n, H, DK]), ALU.mult)
                G.tensor_copy(va[0:n, :, 0:DV], L[:, D:2 * D].rearrange("p (h v) -> p h v", h=H))
                po.drain()
                po.sem_inc(s_kv, 1)
                po.wait_ge(s_y, t + 1)
                G.tensor_tensor(sg[0:n, :], L[:, 2 * D:3 * D], ng[0:n, :], ALU.mult)
                po.drain()
                po.sem_inc(s_gate, 1)
                po.wait_ge(s_T, t + 1)
                po.sem_inc(s_free, 1)

            with po.Fori(0, PT // 2) as i:
                for par in range(2):
                    chunk(i * 2 + par, par, i, P)
            chunk(PT, 0, PT // 2, NSAMP)

        @block.scalar
        def _(act):
            S = nc.scalar
            act.sem_inc(s_out, 1)

            def queries_keys(t, n):
                act.wait_ge(s_T, t + 1)
                S.copy(qT[:, :, 0:n], ps[:, TS, :].rearrange("p (a s) -> p a s", a=PAIRS)[:, :, 0:n])
                S.mul(kT[:, :, 0:n], ps[:, TS + 1, :].rearrange("p (a s) -> p a s", a=PAIRS)[:, :, 0:n], DK ** -0.5)
                act.drain()
                act.sem_inc(s_qk, 1)

            def exponentials(t, n):
                act.wait_ge(s_A, t + 2)
                act.wait_ge(s_N, 2 * t + 2)
                for h in range(H):
                    a = ps[0:n, AA + h // 4, (h % 4) * n:(h % 4 + 1) * n]
                    S.activation(ex[0:n, h, 0:n], a, ACT.Exp,
                                 bias=g.u[0:n, bass.ds(t, 1), h:h + 1].rearrange("p o h -> p (o h)"))
                act.drain()
                act.sem_inc(s_E, 1)

            def root(t, n):
                act.wait_ge(s_var, t + 1)
                S.activation(rs[0:n, :], rs[0:n, :], ACT.Sqrt)
                act.drain()
                act.sem_inc(s_sd, 1)

            def keep(t, n):
                act.wait_ge(s_yT, t + 2)
                for z in range(2):
                    S.copy(g.mixT[:, z * 4:z * 4 + 4, bass.ds(t * P, n)],
                           ps[:, NN + z, :].rearrange("p (k s) -> p k s", k=4)[:, :, 0:n])
                act.drain()
                act.sem_inc(s_out, 1)

            queries_keys(0, P)
            exponentials(0, P)
            with act.Fori(0, PT - 1) as t:
                queries_keys(t + 1, P)
                exponentials(t + 1, P)
                root(t, P)
                keep(t, P)
            queries_keys(PT, NSAMP)
            exponentials(PT, NSAMP)
            root(PT - 1, P)
            keep(PT - 1, P)
            root(PT, NSAMP)
            keep(PT, NSAMP)

        @block.vector
        def _(v):
            V = nc.vector
            v.sem_inc(s_comb, 1)
            v.sem_inc(s_y, 1)
            V.memset(C[:], 0.0)
            V.tensor_scalar(negid[:], g.ident[0:H, 0:H], -1.0, None, ALU.mult)
            V.tensor_scalar(kfac[:], g.factors[:, 2, :, :], DK ** -0.5, None, ALU.mult)
            for z, n in enumerate((P, NSAMP)):
                V.tensor_copy(mask[z][:], g.lmask[:, z, 0:n].unsqueeze(1).broadcast_to([P, 4, n]))
            v.drain()
            v.sem_inc(s_set, 1)
            v.sem_inc(s_N, 2)
            v.wait_ge(s_c, 48)

            def weigh(t, n, sample):
                if sample:
                    v.wait_ge(s_qk, t + 1)
                    v.wait_ge(s_kv, t + 1)
                    for z in range(BATCHES):
                        V.tensor_scalar(kwb[:, z, :], kw[0:n, :, :].rearrange("p h k -> p (h k)"),
                                        g.bmask[0:n, z:z + 1], None, ALU.mult)
                        V.tensor_tensor(qb[:, z, :, :], qT[:, :, 0:n],
                                        bmT[:, z, :].unsqueeze(1).broadcast_to([P, PAIRS, n]), ALU.mult)
                    v.drain()
                    v.sem_inc(s_qb, 1)
                v.wait_ge(s_E, t + 1)
                v.wait_ge(s_kv, t + 1)
                v.wait_ge(s_S, t + 1)
                for a in range(2):
                    V.tensor_tensor(ex[0:n, a:H:2, 0:n], ex[0:n, a:H:2, 0:n],
                                    ps[0:n, TS + a, 0:4 * n].rearrange("p (h s) -> p h s", h=4), ALU.mult)
                    v.drain()
                    v.sem_inc(s_P, 1)

            def chunk(t, n, sample, last=False):
                f = g.factors[0:n, :, bass.ds(t, 1), :].rearrange("p x o h -> p x (o h)")
                for a in (1, 0):
                    v.wait_ge(s_N, 2 * t + 4 - a)
                    for b in range(2):
                        hs = slice(4 * a + b, 4 * a + 4, 2)
                        two = ps[0:n, CARRIED[a] + b, 0:2 * AUG].rearrange("p (h v) -> p h v", h=2)
                        V.tensor_tensor(hh[0:n, hs, :], two,
                                        f[:, 0, hs].unsqueeze(2).broadcast_to([n, 2, AUG]), ALU.mult)
                        v.drain()
                        V.tensor_tensor(hh[0:n, hs, :], hh[0:n, hs, :],
                                        ps[0:n, OWN[a] + b, 0:2 * AUG].rearrange("p (h v) -> p h v", h=2), ALU.add)
                    v.drain()
                    v.sem_inc(s_comb, 1)
                for z in range(BATCHES if sample else 1):
                    v.wait_ge(s_U, t + z + 2)
                    for h in range(H):
                        U = ps[half(h), ADDED[h // 2], (h % 2) * AUG:(h % 2 + 1) * AUG]
                        old = Cs[half(h), z, h // 2, :] if sample else C[half(h), h // 2, :]
                        V.scalar_tensor_tensor(out=old, in0=old, scalar=g.decay[half(h), h, bass.ds(t + z, 1)], in1=U,
                                               op0=ALU.mult, op1=ALU.add)
                    v.drain()
                    v.sem_inc(s_C, 1)
                den = hh[0:n, :, DV]
                V.tensor_scalar(dn[0:n, 0, :], den, -1.0, None, ALU.mult)
                v.drain()
                V.tensor_tensor(dn[0:n, 0, :], dn[0:n, 0, :], den, ALU.max)
                v.drain()
                V.tensor_tensor(dn[0:n, 0, :], dn[0:n, 0, :], f[:, 1, :], ALU.max)
                v.drain()
                V.reciprocal(dn[0:n, 1, :], dn[0:n, 0, :])
                v.drain()
                v.wait_ge(s_yT, t + 1)
                yh = y[0:n, :].rearrange("p (h v) -> p h v", h=H)
                V.tensor_tensor(yh, hh[0:n, :, 0:DV], dn[0:n, 1, :].unsqueeze(2).broadcast_to([n, H, DV]), ALU.mult)
                v.drain()
                for h in range(H):
                    V.bn_stats(st[0:n, h, :], yh[:, h, :])
                v.drain()
                for h in range(H):
                    V.bn_aggr(mv[0:n, h, :], st[0:n, h, :])
                v.drain()
                V.tensor_scalar(rs[0:n, :], mv[0:n, :, 1], EPS, None, ALU.add)
                v.drain()
                v.sem_inc(s_var, 1)
                if not sample:
                    weigh(t + 1, NSAMP if last else P, last)
                V.tensor_tensor(yh, yh, mv[0:n, :, 0].unsqueeze(2).broadcast_to([n, H, DV]), ALU.subtract)
                v.drain()
                v.wait_ge(s_gate, t + 1)
                V.tensor_tensor(y[0:n, :], y[0:n, :], sg[0:n, :], ALU.mult)
                v.wait_ge(s_sd, t + 1)
                V.reciprocal(rs[0:n, :], rs[0:n, :])
                v.drain()
                V.tensor_tensor(yh, yh, rs[0:n, :].unsqueeze(2).broadcast_to([n, H, DV]), ALU.mult)
                v.drain()
                v.sem_inc(s_y, 1)

            weigh(0, P, False)
            with v.Fori(0, PT - 1) as t:
                chunk(t, P, False)
            chunk(PT - 1, P, False, True)
            chunk(PT, NSAMP, True)


def norm_steps(nc, v, w, n, ask, answer, have):
    V = nc.vector
    z = w.z[0:n, :]
    for a in range(2):
        V.bn_stats(w.stats[0:n, a, :], z[:, a * HALF:(a + 1) * HALF])
    v.drain()
    V.bn_aggr(w.mv[0:n, :], w.stats[0:n, :, :].rearrange("p a s -> p (a s)"))
    v.drain()
    V.tensor_scalar(w.sd[0:n, :], w.mv[0:n, 1:2], EPS, None, ALU.add)
    v.drain()
    v.sem_inc(ask, 1)
    v.wait_ge(answer, have)
    V.reciprocal(w.sd[0:n, :], w.sd[0:n, :])
    v.drain()
    V.tensor_scalar(z, z, w.mv[0:n, 0:1], w.sd[0:n, 0:1], ALU.subtract, ALU.mult)
    v.drain()
    V.tensor_tensor(z, z, w.g[0:n, :], ALU.mult)
    v.drain()


def stage_out_proj(nc, g, layer, weight):
    with nc.cleanup_on_exit(), ExitStack() as ctx:
        def sb(n, s, d=F32):
            return ctx.enter_context(nc.sbuf_tensor(f"o{layer}_{n}", s, d))

        def sem(n):
            return nc.alloc_semaphore(f"o{layer}_{n}")

        w = Shared()
        raw = sb("w_raw", [P, 2, D])
        wh, wl = sb("w_upper", [P, KD, D], F32R), sb("w_lower", [P, KD, D], F32R)
        rw = sb("rw", [P, KD, E])
        mh, ml = sb("mix_upper", [P, 2, KD, P], F32R), sb("mix_lower", [P, 2, KD, P], F32R)
        w.z, w.stats, w.mv, w.sd = sb("z", [P, D]), sb("stats", [P, 2, 6]), sb("mv", [P, 2]), sb("sd", [P, 1])
        w.g, lb = sb("lg", [P, D]), sb("lb", [P, D])
        gate, scale, shift = sb("gate", [P, D]), sb("scale", [P, D]), sb("shift", [P, D])
        h2 = sb("h2", [P, 2, D])
        hT = sb("hT", [P, KD, P])
        ps = ctx.enter_context(nc.psum_tensor(f"o{layer}_ps", [P, 2, D], F32))
        psT = ctx.enter_context(nc.psum_tensor(f"o{layer}_psT", [P, KD, P], F32))
        psR = ctx.enter_context(nc.psum_tensor(f"o{layer}_psR", [P, HALF], F32))
        s_hi, s_lo, s_ld, s_mods, s_mh, s_ml, s_Y, s_read, s_var, s_sd, s_h2, s_T, s_hT, s_R, s_done, s_z = (sem(x) for x in (
            "w_upper", "w_lower", "side_loaded", "mods_loaded", "mix_upper", "mix_lower", "y_summed", "y_read", "variance", "deviation",
            "h2_ready", "h2_turned", "h2T_ready", "logits_summed", "logits_out", "zero_row"))
        s_raw = [sem("w_loaded0"), sem("w_loaded1")]
        s_st = [sem("h2_stored0"), sem("h2_stored1")]
        block = ctx.enter_context(nc.Block())

        @block.sync
        def _(sp):
            for k in range(2):
                sp.dma_start(raw[:, k, :], weight[k * P:(k + 1) * P, :]).then_inc(s_raw[k], 16)
            sp.dma_start(w.g[:], g.ln_g[2 * layer:2 * layer + 1, :].broadcast_to([P, D])).then_inc(s_ld, 16)
            sp.dma_start(lb[:], g.ln_b[2 * layer:2 * layer + 1, :].broadcast_to([P, D])).then_inc(s_ld, 16)
            sp.dma_start(rw[:], g.router_w.rearrange("(k p) e -> p k e", p=P)).then_inc(s_ld, 16)
            for which, dst in ((GATE1, gate), (SHIFT2, shift), (SCALE2, scale)):
                load_mods(sp, g, dst, layer, which, False, s_mods)
            for k in range(2, KD):
                sp.wait_ge(s_lo, k - 1)
                sp.dma_start(raw[:, k % 2, :], weight[k * P:(k + 1) * P, :]).then_inc(s_raw[k % 2], 16)

            def store(t, par, n):
                sp.wait_ge(s_h2, t + 2)
                sp.dma_start(g.h2[bass.ds(t * P, n), :], h2[0:n, par, :]).then_inc(s_st[par], 16)

            with sp.Fori(0, PT // 2) as i:
                for par in range(2):
                    store(i * 2 + par, par, P)
            for which, dst in ((GATE1, gate), (SHIFT2, shift), (SCALE2, scale)):
                load_mods(sp, g, dst, layer, which, True, s_mods)
            store(PT, 0, NSAMP)
            sp.wait_ge(s_z, 1)
            sp.wait_ge(s_st[1], 16 * (PT // 2) + 16)
            sp.dma_start(g.h2[N:N + 1, :], h2[0:1, 1, :]).then_inc(s_st[1], 16)
            sp.wait_ge(s_st[0], 16 * (PT // 2 + 1) + 16)
            sp.wait_ge(s_st[1], 16 * (PT // 2 + 1) + 16)

        @block.tensor
        def _(pe):
            T = nc.tensor
            pe.sem_inc(s_Y, 2)

            def route(t, n):
                pe.wait_ge(s_h2, t + 2)
                pe.wait_ge(s_hT, t + 1)
                for k in range(KD):
                    mm = T.transpose(psT[:, k, 0:n], hcur(t)[0:n, k * P:(k + 1) * P], g.ident[0:n, 0:n])
                mm.then_inc(s_T, 1)
                pe.wait_ge(s_hT, t + 2)
                pe.wait_ge(s_ld, 48)
                pe.wait_ge(s_done, t + 1)
                for k in range(KD):
                    mm = T.matmul(psR[0:n, 0:E], hT[:, k, 0:n], rw[:, k, :], start=(k == 0), stop=(k == KD - 1))
                mm.then_inc(s_R, 1)

            def project(t, par, n):
                pe.wait_ge(s_ml, t + 1)
                pe.wait_ge(s_read, t + 1)
                for k in range(KD):
                    if isinstance(t, int) and t == 0:
                        pe.wait_ge(s_lo, k + 1)
                    up, lw = mh[:, par, k, 0:n], ml[:, par, k, 0:n]
                    for c in range(2):
                        dst, cols = ps[0:n, par, c * HALF:(c + 1) * HALF], slice(c * HALF, (c + 1) * HALF)
                        T.matmul(dst, up, wh[:, k, cols], start=(k == 0), stop=False)
                        T.matmul(dst, up, wl[:, k, cols], start=False, stop=False)
                        mm = T.matmul(dst, lw, wh[:, k, cols], start=False, stop=(k == KD - 1))
                mm.then_inc(s_Y, 1)

            slot = [0]

            def hcur(t):
                return h2[:, slot[0], :]

            project(0, 0, P)
            with pe.Fori(0, PT // 2 - 1) as i:
                for par in range(2):
                    t = i * 2 + par
                    project(t + 1, 1 - par, P)
                    slot[0] = par
                    route(t, P)
            project(PT - 1, 1, P)
            slot[0] = 0
            route(PT - 2, P)
            project(PT, 0, NSAMP)
            slot[0] = 1
            route(PT - 1, P)
            slot[0] = 0
            route(PT, NSAMP)

        @block.scalar
        def _(act):
            act.sem_inc(s_hT, 1)
            act.sem_inc(s_done, 1)

            def upper(t, par, n):
                if not isinstance(t, int) or t >= 2:
                    act.wait_ge(s_Y, t + 1)
                nc.scalar.copy(mh[:, par, :, 0:n], g.mixT[:, :, bass.ds(t * P, n)]).then_inc(s_mh, 1)

            upper(0, 0, P)
            for k in range(KD):
                act.wait_ge(s_raw[k % 2], 16 * (k // 2) + 16)
                nc.scalar.copy(wh[:, k, :], raw[:, k % 2, :]).then_inc(s_hi, 1)
            upper(1, 1, P)

            def tile(t, n):
                act.wait_ge(s_var, t + 1)
                nc.scalar.activation(w.sd[0:n, :], w.sd[0:n, :], ACT.Sqrt)
                act.drain()
                act.sem_inc(s_sd, 1)
                act.wait_ge(s_T, t + 1)
                act.wait_ge(s_R, t + 1)
                for z in range(2):
                    nc.scalar.copy(hT[:, z * 4:z * 4 + 4, 0:n], psT[:, z * 4:z * 4 + 4, 0:n])
                act.drain()
                act.sem_inc(s_hT, 1)
                act.wait_ge(s_R, t + 2)
                nc.scalar.copy(g.logits[0:n, bass.ds(t, 1), :].rearrange("p o e -> p (o e)"), psR[0:n, 0:E])
                act.drain()
                act.sem_inc(s_done, 1)

            with act.Fori(0, PT // 2 - 1) as i:
                for par in range(2):
                    upper(i * 2 + par + 2, par, P)
                    tile(i * 2 + par, P)
            upper(PT, 0, NSAMP)
            tile(PT - 2, P)
            tile(PT - 1, P)
            tile(PT, NSAMP)

        @block.vector
        def _(v):
            V = nc.vector
            v.sem_inc(s_read, 2)
            v.sem_inc(s_h2, 1)
            v.sem_inc(s_R, 1)
            v.sem_inc(s_st[0], 16)
            v.sem_inc(s_st[1], 16)
            V.memset(g.logits[:], 0.0)

            def lower(t, par, n):
                v.wait_ge(s_mh, t + 1)
                V.tensor_tensor(ml[:, par, :, 0:n], g.mixT[:, :, bass.ds(t * P, n)], mh[:, par, :, 0:n].bitcast(F32),
                                ALU.subtract).then_inc(s_ml, 1)

            lower(0, 0, P)
            for k in range(KD):
                v.wait_ge(s_hi, k + 1)
                V.tensor_tensor(wl[:, k, :], raw[:, k % 2, :], wh[:, k, :].bitcast(F32), ALU.subtract
                                ).then_inc(s_lo, 1)
            lower(1, 1, P)
            v.wait_ge(s_ld, 48)

            def tile(t, par, i, n, mods, ahead=None):
                x = g.x[0:n, bass.ds(t, 1), :].rearrange("p o d -> p (o d)")
                z = w.z[0:n, :]
                v.wait_ge(s_mods, mods)
                v.wait_ge(s_Y, t + 3)
                V.tensor_tensor(z, ps[0:n, par, :], gate[0:n, :], ALU.mult)
                v.drain()
                v.sem_inc(s_read, 1)
                if ahead:
                    lower(t + 2, par, ahead)
                V.scalar_tensor_tensor(out=z, in0=x, scalar=ALPHA, in1=z, op0=ALU.mult, op1=ALU.add)
                v.drain()
                norm_steps(nc, v, w, n, s_var, s_sd, t + 1)
                V.tensor_tensor(x, z, lb[0:n, :], ALU.add)
                v.drain()
                v.wait_ge(s_st[par], 16 * i + 16)
                o = h2[0:n, par, :]
                V.scalar_tensor_tensor(out=o, in0=scale[0:n, :], scalar=1.0, in1=x, op0=ALU.add, op1=ALU.mult)
                v.drain()
                V.tensor_tensor(o, o, shift[0:n, :], ALU.add)
                v.drain()
                v.sem_inc(s_h2, 1)

            with v.Fori(0, PT // 2 - 1) as i:
                for par in range(2):
                    tile(i * 2 + par, par, i, P, 48, P)
            tile(PT - 2, 0, PT // 2 - 1, P, 48, NSAMP)
            tile(PT - 1, 1, PT // 2 - 1, P, 48)
            tile(PT, 0, PT // 2, NSAMP, 48 + 3 * 16 * BATCHES)
            v.wait_ge(s_st[1], 16 * (PT // 2) + 16)
            v.wait_ge(s_R, PT + 1)
            V.memset(h2[0:1, 1, :], 0.0)
            v.drain()
            v.sem_inc(s_z, 1)


def stage_route(nc, g, layer):
    with nc.cleanup_on_exit(), ExitStack() as ctx:
        def sb(n, s, d=F32):
            return ctx.enter_context(nc.sbuf_tensor(f"r{layer}_{n}", s, d))

        def sem(n):
            return nc.alloc_semaphore(f"r{layer}_{n}")

        sh3 = [P, TILES, E]
        rb = sb("bias", [P, E])
        sc, sel, work = sb("scores", sh3), sb("sel", sh3), sb("work", sh3)
        oh = [sb("first", sh3), sb("second", sh3)]
        gs, gm, gi = sb("gs", [P, TILES, GROUPS]), sb("gm", [P, TILES, GROUPS]), sb("gi", [P, TILES, GROUPS])
        pr = sb("pairs", [P, TILES, GROUPS, 3])
        mx = sb("mx", [P, TILES])
        ws = sb("ws", [P, TILES])
        both = sb("both", sh3)
        tot = sb("tot", sh3)
        carry = sb("carry", [P, TILES + 1, E])
        place = sb("place", sh3)
        more = sb("more", [P, E, TILES])
        blocks, ends, tmp = sb("blocks", [P, E]), sb("ends", [P, 2, E]), sb("start", [P, E])
        destf = sb("destf", [P, 2, TILES])
        full = sb("full", [P, SLOTS + 1, E])
        slotf = sb("slotf", [P, SLOTS + 1])
        fresh = sb("fresh", [P, SLOTS + 1])
        taken = sb("taken", [P, SLOTS + 1])
        ids = sb("ids", [P, TILES], I32)
        ps = ctx.enter_context(nc.psum_tensor(f"r{layer}_ps", [P, 2, HALF], F32))
        s_ld, s_e, s_oh, s_cnt, s_dest, s_sc = (sem(x) for x in (
            "loaded", "exp_ready", "choices", "counted", "dest_ready", "scattered"))
        block = ctx.enter_context(nc.Block())

        @block.sync
        def _(sp):
            sp.dma_start(rb[:], g.router_b.broadcast_to([P, E])).then_inc(s_ld, 16)
            sp.dma_start(ids[:], g.const["token_ids"]).then_inc(s_ld, 16)
            sp.dma_start(g.slot_token, g.const["no_token"].rearrange("s (p o) -> (s p) o", o=1)).then_inc(s_ld, 16)

        @block.scalar
        def _(act):
            nc.scalar.activation(sc[:], g.logits[:], ACT.Exp, scale=-1.0)
            act.drain()
            act.sem_inc(s_e, 1)

        @block.tensor
        def _(pe):
            pe.wait_ge(s_oh, 1)
            b2 = both[:].rearrange("p t e -> p (t e)")
            nc.tensor.matmul(ps[:, 0, 0:TILES * E], g.tri[:, 2, :], b2, start=True, stop=True)
            nc.tensor.matmul(ps[:, 1, 0:TILES * E], g.ones[:], b2, start=True, stop=True)
            pe.drain()
            pe.sem_inc(s_cnt, 1)

        @block.gpsimd
        def _(po):
            po.wait_ge(s_ld, 48)
            po.wait_ge(s_dest, 1)
            n = 0
            for k in range(2):
                for t in range(TILES):
                    r = rows_of(t)
                    nc.gpsimd.indirect_dma_start(
                        g.slot_token, bass.IndirectOffsetOnAxis(g.dest[0:r, k, t:t + 1], axis=0),
                        ids[0:r, t:t + 1], None).then_inc(s_sc, 16)
                    n += 16
            po.wait_ge(s_sc, n)

        @block.vector
        def _(v):
            V = nc.vector

            def wide(a, n=E):
                return a.unsqueeze(2).broadcast_to([P, TILES, n])

            v.wait_ge(s_ld, 48)
            v.wait_ge(s_e, 1)
            V.tensor_scalar(sc[:], sc[:], 1.0, None, ALU.add)
            v.drain()
            V.reciprocal(sc[:], sc[:])
            v.drain()
            V.tensor_tensor(sel[:], sc[:], rb[:].unsqueeze(1).broadcast_to(sh3), ALU.add)
            v.drain()
            s4 = sel[:].rearrange("p t (g x) -> p t g x", g=GROUPS)
            V.tensor_tensor(pr[:], s4[:, :, :, 0:3], s4[:, :, :, 1:4], ALU.add)
            V.tensor_tensor(gs[:], s4[:, :, :, 0], s4[:, :, :, 3], ALU.add)
            v.drain()
            V.tensor_reduce(gm[:], pr[:], AX, ALU.max)
            v.drain()
            V.tensor_tensor(pr[:, :, :, 0:2], s4[:, :, :, 0:2], s4[:, :, :, 2:4], ALU.add)
            V.tensor_tensor(gs[:], gs[:], gm[:], ALU.max)
            v.drain()
            V.tensor_tensor(gs[:], gs[:], pr[:, :, :, 0], ALU.max)
            v.drain()
            V.tensor_tensor(gs[:], gs[:], pr[:, :, :, 1], ALU.max)
            v.drain()

            def first_largest(values, hot, n):
                down = g.count_down[:, E - n:E].unsqueeze(1).broadcast_to([P, TILES, n])
                V.tensor_reduce(mx[:], values, AX, ALU.max)
                v.drain()
                V.tensor_tensor(hot, values, wide(mx[:], n), ALU.is_equal)
                v.drain()
                V.tensor_tensor(hot, hot, down, ALU.mult)
                v.drain()
                V.tensor_reduce(mx[:], hot, AX, ALU.max)
                v.drain()
                V.tensor_tensor(hot, down, wide(mx[:], n), ALU.is_equal)
                v.drain()

            first_largest(gs[:], gi[:], GROUPS)
            V.tensor_scalar(gm[:], gi[:], -1.0, -NEG, ALU.add, ALU.mult)
            V.tensor_tensor(work[:].rearrange("p t (g x) -> p t g x", g=GROUPS), s4,
                            gi[:].unsqueeze(3).broadcast_to([P, TILES, GROUPS, PER]), ALU.mult)
            v.drain()
            V.tensor_tensor(work[:].rearrange("p t (g x) -> p t g x", g=GROUPS),
                            work[:].rearrange("p t (g x) -> p t g x", g=GROUPS),
                            gm[:].unsqueeze(3).broadcast_to([P, TILES, GROUPS, PER]), ALU.add)
            v.drain()
            first_largest(work[:], oh[0][:], E)
            V.scalar_tensor_tensor(out=work[:], in0=oh[0][:], scalar=4 * NEG, in1=work[:], op0=ALU.mult, op1=ALU.add)
            v.drain()
            first_largest(work[:], oh[1][:], E)
            for k in range(2):
                V.tensor_tensor(work[:], sc[:], oh[k][:], ALU.mult)
                v.drain()
                V.tensor_reduce(g.weight[:, k, :], work[:], AX, ALU.add)
                v.drain()
            V.tensor_tensor(ws[:], g.weight[:, 0, :], g.weight[:, 1, :], ALU.add)
            v.drain()
            V.reciprocal(ws[:], ws[:])
            V.tensor_tensor(both[:], oh[0][:], oh[1][:], ALU.add)
            v.drain()
            for k in range(2):
                V.tensor_tensor(g.weight[:, k, :], g.weight[:, k, :], ws[:], ALU.mult)
            V.memset(both[NSAMP:P, TILES - 1, :], 0.0)
            V.memset(carry[:, 0, :], 0.0)
            v.drain()
            v.sem_inc(s_oh, 1)
            v.wait_ge(s_cnt, 1)
            V.tensor_copy(tot[:].rearrange("p t e -> p (t e)"), ps[:, 1, 0:TILES * E])
            v.drain()
            for t in range(TILES):
                V.tensor_tensor(carry[:, t + 1, :], carry[:, t, :], tot[:, t, :], ALU.add)
                v.drain()
            V.tensor_tensor(more[:], carry[:, TILES, :].unsqueeze(2).broadcast_to([P, E, TILES]),
                            g.steps[:].unsqueeze(1).broadcast_to([P, E, TILES]), ALU.is_gt)
            v.drain()
            V.tensor_reduce(blocks[:], more[:], AX, ALU.add)
            v.drain()
            V.tensor_copy(ends[:, 0, :], blocks[:])
            v.drain()
            a, k = 0, 1
            while k < E:
                V.tensor_tensor(ends[:, 1 - a, k:E], ends[:, a, k:E], ends[:, a, 0:E - k], ALU.add)
                V.tensor_copy(ends[:, 1 - a, 0:k], ends[:, a, 0:k])
                v.drain()
                a, k = 1 - a, 2 * k
            V.tensor_tensor(tmp[:], ends[:, a, :], blocks[:], ALU.subtract)
            V.tensor_tensor(full[:], ends[:, a, :].unsqueeze(1).broadcast_to([P, SLOTS + 1, E]),
                            g.count_up[:].unsqueeze(2).broadcast_to([P, SLOTS + 1, E]), ALU.is_le)
            v.drain()
            V.tensor_reduce(slotf[:], full[:], AX, ALU.add)
            V.tensor_scalar(tmp[:], tmp[:], float(P), None, ALU.mult)
            v.drain()
            V.tensor_scalar(slotf[:], slotf[:], float(E - 1), None, ALU.min)
            V.tensor_tensor(place[:], carry[:, 0:TILES, :], tmp[:].unsqueeze(1).broadcast_to(sh3), ALU.add)
            v.drain()
            V.tensor_copy(g.slot_expert[:], slotf[:])
            V.memset(fresh[:, 0:1], 1.0)
            V.tensor_tensor(fresh[:, 1:], slotf[:, 1:], slotf[:, 0:SLOTS], ALU.is_gt)
            V.tensor_tensor(taken[:], ends[:, a, E - 1:E].broadcast_to([P, SLOTS + 1]), g.count_up[:], ALU.is_gt)
            V.tensor_copy(g.slots_used[:], ends[:, a, E - 1:E])
            v.drain()
            V.tensor_tensor(fresh[:], fresh[:], taken[:], ALU.mult)
            v.drain()
            V.tensor_copy(g.slot_fresh[:], fresh[:])
            V.tensor_tensor(place[:], place[:], ps[:, 0, 0:TILES * E].rearrange("p (t e) -> p t e", e=E), ALU.add)
            v.drain()
            for k in range(2):
                V.tensor_tensor(work[:], place[:], oh[k][:], ALU.mult)
                v.drain()
                V.tensor_reduce(destf[:, k, :], work[:], AX, ALU.add)
                v.drain()
            V.tensor_copy(g.dest[:], destf[:])
            v.drain()
            v.sem_inc(s_dest, 1)


def stage_experts(nc, g, layer):
    with nc.cleanup_on_exit(), ExitStack() as ctx:
        def sb(n, s, d=F32):
            return ctx.enter_context(nc.sbuf_tensor(f"e{layer}_{n}", s, d))

        def sem(n):
            return nc.alloc_semaphore(f"e{layer}_{n}")

        UNIT = KD * FE
        PIECES = 4
        PC = UNIT // PIECES
        raw = sb("raw", [P, 3, UNIT])
        wh, wl = sb("wh", [P, 3, UNIT], F32R), sb("wl", [P, 3, UNIT], F32R)
        tok = sb("tok", [P, 1], I32)
        xg = sb("xg", [P, D])
        xh, xl = sb("xh", [P, KD, P], F32R), sb("xl", [P, KD, P], F32R)
        hid = sb("hid", [P, FE])
        hh, hl = sb("hh", [P, FT, P], F32R), sb("hl", [P, FT, P], F32R)
        y = sb("y", [P, D])
        psX = ctx.enter_context(nc.psum_tensor(f"e{layer}_psX", [P, KD, P], F32))
        psG = ctx.enter_context(nc.psum_tensor(f"e{layer}_psG", [P, 2, FE], F32))
        psH = ctx.enter_context(nc.psum_tensor(f"e{layer}_psH", [P, FT, P], F32))
        psY = ctx.enter_context(nc.psum_tensor(f"e{layer}_psY", [P, 2, HALF], F32))
        s_raw = [sem(f"weights_loaded{z}") for z in range(3)]
        s_hi = [sem(f"upper_parts{z}") for z in range(3)]
        s_lo = [sem(f"lower_parts{z}") for z in range(3)]
        s_used = [sem(f"weights_used{z}") for z in range(3)]
        s_tok, s_ask, s_x, s_xt, s_xh, s_xl = (sem(n) for n in (
            "tokens_loaded", "tokens_known", "rows_gathered", "rows_turned", "xT_upper", "xT_lower"))
        s_silu, s_hid, s_ht, s_hh, s_hl, s_out, s_st, s_fill, s_end = (sem(n) for n in (
            "silu_ready", "hidden_ready", "hidden_turned", "hT_upper", "hT_lower", "y_out", "y_stored", "unused_filled", "passed"))
        block = ctx.enter_context(nc.Block())

        def table(eng, t, at):
            most = E - 1 if t is g.slot_expert else SLOTS
            return eng.value_load(t[0:1, bass.ds(at, 1)], min_val=0, max_val=most)

        def slots(eng, body):
            used = table(eng, g.slots_used, 0)
            with eng.Fori(0, SLOTS) as b:
                with eng.If(used > b):
                    body(b)
                with eng.Else():
                    eng.sem_inc(s_end, 1)

        @block.sync
        def _(sp):
            def load(e):
                for z, src in enumerate((g.e_gate, g.e_up, g.e_down)):
                    sp.dma_start(raw[:, z, :].rearrange("p (k f) -> p k f", k=KD if z < 2 else FT),
                                 src[bass.ds(e, 1)].rearrange("o (k p) f -> p (o k) f", p=P)).then_inc(s_raw[z], 16)

            load(table(sp, g.slot_expert, 0) + layer * E)

            def slot(b):
                with sp.If(table(sp, g.slot_fresh, b + 1) > 0):
                    e = table(sp, g.slot_expert, b + 1) + layer * E
                    for z, src in enumerate((g.e_gate, g.e_up, g.e_down)):
                        sp.wait_ge(s_lo[z], b * PIECES + PIECES)
                        sp.dma_start(raw[:, z, :].rearrange("p (k f) -> p k f", k=KD if z < 2 else FT),
                                     src[bass.ds(e, 1)].rearrange("o (k p) f -> p (o k) f", p=P)
                                     ).then_inc(s_raw[z], 16)
                with sp.Else():
                    for z in range(3):
                        sp.wait_ge(s_raw[z], b * 16 + 16)
                        sp.sem_inc(s_raw[z], 16)
                sp.drain()

            if layer == 0:
                used = table(sp, g.slots_used, 0)
                with sp.Fori(0, SLOTS) as b:
                    with sp.If(used > b):
                        sp.sem_inc(s_fill, 16)
                    with sp.Else():
                        sp.dma_start(g.yrows[bass.ds(b * P, P), :], g.h2[0:P, :]).then_inc(s_fill, 16)
                    sp.drain()
            slots(sp, slot)
            if layer == 0:
                sp.wait_ge(s_fill, 16 * SLOTS)

        @block.gpsimd
        def _(po):
            def gather(b):
                po.dma_start(tok[:], g.slot_token[bass.ds(b * P, P), :]).then_inc(s_tok, 16)
                po.wait_ge(s_tok, 16 * b + 16)
                po.sem_inc(s_ask, 1)
                nc.gpsimd.indirect_dma_start(xg[:], None, g.h2, bass.IndirectOffsetOnAxis(tok[:], axis=0)
                                             ).then_inc(s_x, 16)

            gather(0)

            def slot(b):
                po.wait_ge(s_xt, b + 1)
                po.wait_ge(s_x, 16 * b + 16)
                gather(b + 1)

            slots(po, slot)

        @block.tensor
        def _(pe):
            T = nc.tensor

            def turn(b, ks=range(KD)):
                if ks[0] == 0:
                    pe.wait_ge(s_x, 16 * b + 16)
                    pe.sem_inc(s_end, 1)
                for k in ks:
                    mm = T.transpose(psX[:, k, :], xg[:, k * P:(k + 1) * P], g.ident[:])
                if ks[-1] == KD - 1:
                    mm.then_inc(s_xt, 1)

            def product(out, upper, lower, z, piece, n, w, first, last):
                for i in range(n):
                    k = piece * n + i
                    cols = w(k)
                    T.matmul(out, upper[:, k, :], wh[:, z, cols], start=first and i == 0, stop=False)
                    T.matmul(out, upper[:, k, :], wl[:, z, cols], start=False, stop=False)
                    mm = T.matmul(out, lower[:, k, :], wh[:, z, cols], start=False, stop=last and i == n - 1)
                return mm

            def slot(b):
                pe.wait_ge(s_xl, b + 1)
                pe.wait_ge(s_hid, b + 1)
                for z in range(2):
                    for c in range(PIECES):
                        pe.wait_ge(s_lo[z], b * PIECES + c + 1)
                        mm = product(psG[:, z, :], xh, xl, z, c, KD // PIECES, lambda k: slice(k * FE, (k + 1) * FE),
                                     c == 0, c == PIECES - 1)
                    mm.then_inc(s_used[z], 1)
                turn(b + 1, range(3))
                pe.wait_ge(s_hid, b + 2)
                pe.sem_inc(s_end, 1)
                for f in range(FT):
                    mm = T.transpose(psH[:, f, :], hid[:, f * P:(f + 1) * P], g.ident[:])
                mm.then_inc(s_ht, 1)
                turn(b + 1, range(3, KD))
                pe.wait_ge(s_hl, b + 1)
                pe.wait_ge(s_out, b + 1)
                for c in range(PIECES):
                    pe.wait_ge(s_lo[2], b * PIECES + c + 1)
                    for y2 in range(2):
                        mm = product(psY[:, y2, :], hh, hl, 2, c, 1,
                                     lambda k: slice(k * D + y2 * HALF, k * D + (y2 + 1) * HALF),
                                     c == 0, c == PIECES - 1)
                mm.then_inc(s_used[2], 1)

            turn(0)
            slots(pe, slot)

        @block.scalar
        def _(act):
            S = nc.scalar

            def upper(z, b):
                act.wait_ge(s_raw[z], b * 16 + 16)
                for c in range(PIECES):
                    S.copy(wh[:, z, c * PC:(c + 1) * PC], raw[:, z, c * PC:(c + 1) * PC]).then_inc(s_hi[z], 1)

            def next_upper(z, b, fresh):
                with act.If(fresh > 0):
                    act.wait_ge(s_used[z], b + 1)
                    upper(z, b + 1)
                with act.Else():
                    act.sem_inc(s_hi[z], PIECES)
                act.drain()

            def copy_x(b):
                act.wait_ge(s_xt, b + 1)
                for z in range(2):
                    S.copy(xh[:, z * 4:z * 4 + 4, :], psX[:, z * 4:z * 4 + 4, :])
                act.drain()
                act.sem_inc(s_xh, 1)

            def slot(b):
                fresh = table(act, g.slot_fresh, b + 1)
                act.wait_ge(s_used[0], b + 1)
                S.activation(hid[:], psG[:, 0, :], ACT.Silu).then_inc(s_silu, 1)
                next_upper(0, b, fresh)
                act.wait_ge(s_ht, b + 1)
                S.copy(hh[:], psH[:]).then_inc(s_hh, 1)
                copy_x(b + 1)
                next_upper(1, b, fresh)
                act.wait_ge(s_used[2], b + 1)
                act.wait_ge(s_st, 16 * b + 16)
                for z in range(2):
                    S.copy(y[:, z * HALF:(z + 1) * HALF], psY[:, z, :])
                act.drain()
                act.sem_inc(s_out, 1)
                act.dma_start(g.yrows[bass.ds(b * P, P), :], y[:]).then_inc(s_st, 16)
                next_upper(2, b, fresh)

            act.sem_inc(s_st, 16)
            act.sem_inc(s_out, 1)
            for z in range(3):
                upper(z, 0)
            copy_x(0)
            slots(act, slot)
            act.wait_ge(s_st, table(act, g.slots_used, 0) * 16 + 16)
            act.sem_inc(s_end, 1)

        @block.vector
        def _(v):
            V = nc.vector

            def lower(z, b, pieces=range(PIECES)):
                for c in pieces:
                    v.wait_ge(s_hi[z], b * PIECES + c + 1)
                    at = slice(c * PC, (c + 1) * PC)
                    V.tensor_tensor(wl[:, z, at], raw[:, z, at], wh[:, z, at].bitcast(F32), ALU.subtract
                                    ).then_inc(s_lo[z], 1)

            def next_lower(z, b, fresh, pieces=range(PIECES)):
                with v.If(fresh > 0):
                    lower(z, b + 1, pieces)
                with v.Else():
                    v.wait_ge(s_hi[z], b * PIECES + 2 * PIECES)
                    v.sem_inc(s_lo[z], len(pieces))
                v.drain()

            def lower_x(b):
                v.wait_ge(s_xh, b + 1)
                V.tensor_tensor(xl[:], psX[:], xh[:].bitcast(F32), ALU.subtract).then_inc(s_xl, 1)

            def slot(b):
                fresh = table(v, g.slot_fresh, b + 1)
                next_lower(0, b, fresh, range(2))
                v.wait_ge(s_silu, b + 1)
                v.wait_ge(s_used[1], b + 1)
                V.tensor_tensor(hid[:], hid[:], psG[:, 1, :], ALU.mult).then_inc(s_hid, 1)
                v.wait_ge(s_hh, b + 1)
                V.tensor_tensor(hl[:], psH[:], hh[:].bitcast(F32), ALU.subtract).then_inc(s_hl, 1)
                lower_x(b + 1)
                next_lower(0, b, fresh, range(2, PIECES))
                next_lower(1, b, fresh)
                next_lower(2, b, fresh)

            v.sem_inc(s_hid, 1)
            for z in range(3):
                lower(z, 0)
            lower_x(0)
            slots(v, slot)


def stage_combine(nc, g, layer, last):
    with nc.cleanup_on_exit(), ExitStack() as ctx:
        def sb(n, s, d=F32):
            return ctx.enter_context(nc.sbuf_tensor(f"c{layer}_{n}", s, d))

        def sem(n):
            return nc.alloc_semaphore(f"c{layer}_{n}")

        RING = 4
        zr, stats = sb("z", [P, RING, D]), sb("stats", [P, 2, 6])
        mv, sd, off = sb("mv", [P, 2]), sb("sd", [P, 2]), sb("off", [P, 2])
        lg, lb, gate = sb("lg", [P, D]), sb("lb", [P, D]), sb("gate", [P, 2, D])
        ya, yb = sb("ya", [P, 2, D]), sb("yb", [P, 2, D])
        s_ld, s_mods, s_first, s_both, s_gated, s_var, s_sd, s_off, s_norm, s_x, s_st = (sem(x) for x in (
            "side_loaded", "mods_loaded", "first_weighted", "both_summed", "gated", "variance", "deviation",
            "offset_ready", "normalised", "x_ready", "y_stored"))
        s_g = [sem("rows_gathered0"), sem("rows_gathered1")]
        block = ctx.enter_context(nc.Block())

        @block.sync
        def _(sp):
            r = 2 * layer + 1
            sp.dma_start(lg[:], g.ln_g[r:r + 1, :].broadcast_to([P, D])).then_inc(s_ld, 16)
            sp.dma_start(lb[:], g.ln_b[r:r + 1, :].broadcast_to([P, D])).then_inc(s_ld, 16)
            load_mods(sp, g, gate[:, 0, :], layer, GATE2, False, s_mods)
            load_mods(sp, g, gate[:, 1, :], layer, GATE2, True, s_mods)
            if last:
                with sp.Fori(0, PT) as t:
                    sp.wait_ge(s_x, t + 1)
                    sp.dma_start(g.y_prompt[bass.ds(t * P, P), :],
                                 g.x[:, bass.ds(t, 1), :].rearrange("p o d -> p (o d)")).then_inc(s_st, 16)
                sp.wait_ge(s_x, TILES)
                sp.dma_start(g.y_sample, g.x[0:NSAMP, PT, :]).then_inc(s_st, 16)
                sp.wait_ge(s_st, 16 * TILES)

        @block.gpsimd
        def _(po):
            def gather(t):
                n, par = rows_of(t), t % 2
                for k, y in enumerate((ya, yb)):
                    nc.gpsimd.indirect_dma_start(y[0:n, par, :], None, g.yrows,
                                                 bass.IndirectOffsetOnAxis(g.dest[0:n, k, t:t + 1], axis=0)
                                                 ).then_inc(s_g[par], 16)

            gather(0)
            gather(1)
            po.wait_ge(s_mods, 16 + 16 * BATCHES)
            for t in range(TILES):
                n = rows_of(t)
                po.wait_ge(s_both, t + 1)
                z = zr[0:n, t % RING, :]
                nc.gpsimd.tensor_tensor(z, z, gate[0:n, t // PT, :], ALU.mult).then_inc(s_gated, 1)
                if t + 2 < TILES:
                    gather(t + 2)

        @block.scalar
        def _(act):
            def first(t):
                n, par = rows_of(t), t % 2
                act.wait_ge(s_g[par], 32 * (t // 2) + 32)
                if t >= RING:
                    act.wait_ge(s_x, t - RING + 1)
                nc.scalar.activation(zr[0:n, t % RING, :], ya[0:n, par, :], ACT.Copy,
                                     scale=g.weight[0:n, 0, t:t + 1]).then_inc(s_first, 1)

            first(0)
            first(1)
            for t in range(TILES):
                n, par = rows_of(t), t % 2
                if t + 2 < TILES:
                    first(t + 2)
                act.wait_ge(s_var, t + 1)
                nc.scalar.activation(sd[0:n, par:par + 1], sd[0:n, par:par + 1], ACT.Sqrt).then_inc(s_sd, 1)
                act.wait_ge(s_off, t + 1)
                z = zr[0:n, t % RING, :]
                nc.scalar.activation(z, z, ACT.Identity, bias=off[0:n, par:par + 1], scale=sd[0:n, par:par + 1]
                                     ).then_inc(s_norm, 1)

        @block.vector
        def _(v):
            V = nc.vector
            v.wait_ge(s_ld, 32)

            def both(t):
                n, z = rows_of(t), zr[0:rows_of(t), t % RING, :]
                v.wait_ge(s_first, t + 1)
                V.scalar_tensor_tensor(out=z, in0=yb[0:n, t % 2, :], scalar=g.weight[0:n, 1, t:t + 1], in1=z,
                                       op0=ALU.mult, op1=ALU.add).then_inc(s_both, 1)

            def finish(t):
                n, z = rows_of(t), zr[0:rows_of(t), t % RING, :]
                v.wait_ge(s_norm, t + 1)
                V.tensor_tensor(z, z, lg[0:n, :], ALU.mult)
                v.drain()
                V.tensor_tensor(g.x[0:n, t, :], z, lb[0:n, :], ALU.add).then_inc(s_x, 1)

            both(0)
            for t in range(TILES):
                n, par, z = rows_of(t), t % 2, zr[0:rows_of(t), t % RING, :]
                if t + 1 < TILES:
                    both(t + 1)
                v.wait_ge(s_gated, t + 1)
                V.scalar_tensor_tensor(out=z, in0=g.x[0:n, t, :], scalar=ALPHA, in1=z, op0=ALU.mult, op1=ALU.add)
                v.drain()
                for a in range(2):
                    V.bn_stats(stats[0:n, a, :], z[:, a * HALF:(a + 1) * HALF])
                v.drain()
                V.bn_aggr(mv[0:n, :], stats[0:n, :, :].rearrange("p a s -> p (a s)"))
                v.drain()
                s = sd[0:n, par:par + 1]
                V.tensor_scalar(s, mv[0:n, 1:2], EPS, None, ALU.add).then_inc(s_var, 1)
                if t >= 1:
                    finish(t - 1)
                v.wait_ge(s_sd, t + 1)
                V.reciprocal(s, s)
                v.drain()
                V.tensor_scalar(off[0:n, par:par + 1], mv[0:n, 0:1], s, -1.0, ALU.mult, ALU.mult).then_inc(s_off, 1)
            finish(TILES - 1)


def stage_combine_latents(nc, g):
    with nc.cleanup_on_exit(), ExitStack() as ctx:
        def sb(n, s, d=F32):
            return ctx.enter_context(nc.sbuf_tensor(f"l_{n}", s, d))

        def sem(n):
            return nc.alloc_semaphore(f"l_{n}")

        KVA = KVR + ROPE
        half = ROPE // 2
        RING = 3
        zr, stats = sb("z", [P, RING, D]), sb("stats", [P, 2, 6])
        mv, sd, off = sb("mv", [P, 2]), sb("sd", [P, 2]), sb("off", [P, 2])
        lg, lb, gate = sb("lg", [P, D]), sb("lb", [P, D]), sb("gate", [P, D])
        ya, yb = sb("ya", [P, 2, D]), sb("yb", [P, 2, D])
        wkv, wdq = sb("wkv", [P, KD, KVA]), sb("wdq", [P, KD, QR])
        scale, shift = sb("scale", [P, D]), sb("shift", [P, D])
        trig = sb("trig", [P, TILES, 2, half])
        gkv, gq = sb("gkv", [P, KVR]), sb("gq", [P, QR])
        h = sb("h", [P, D])
        xT, hT = sb("xT", [P, KD, P]), sb("hT", [P, KD, P])
        junk = hT[:].rearrange("p k t -> p (k t)")
        ss, rs = sb("ss", [P, 2]), sb("rs", [P, 2])
        lat, kr, cq = sb("lat", [P, 2, KVR]), sb("kr", [P, 2, 2, ROPE]), sb("cq", [P, QR])
        r4 = cq[:, 0:4 * half].rearrange("p (a r) -> p a r", a=4)
        psT = ctx.enter_context(nc.psum_tensor("l_psT", [P, 2 * KD, P], F32))
        psK = ctx.enter_context(nc.psum_tensor("l_psK", [P, HALF], F32))
        psQ = ctx.enter_context(nc.psum_tensor("l_psQ", [P, HALF], F32))
        psC = ctx.enter_context(nc.psum_tensor("l_psC", [P, 4, P], F32))
        psL = ctx.enter_context(nc.psum_tensor("l_psL", [P, 4, P], F32))
        s_ln, s_gate, s_first, s_both, s_gated, s_var, s_dev, s_off, s_norm, s_x = (sem(x) for x in (
            "norm_loaded", "gate_loaded", "first_weighted", "both_summed", "gated", "variance", "deviation",
            "offset_ready", "normalised_x", "x_ready"))
        s_g = [sem("rows_gathered0"), sem("rows_gathered1")]
        s_ld, s_mods, s_h, s_T, s_xT, s_mm, s_ss, s_ms, s_root, s_nrm, s_post, s_out = (sem(x) for x in (
            "side_loaded", "mods_loaded", "h_ready", "turned", "xT_ready", "projected", "squares_summed",
            "mean_squares", "roots", "normalised", "latents_turned", "latents_out"))
        s_st = [sem("rows_stored0"), sem("rows_stored1")]
        block = ctx.enter_context(nc.Block())

        @block.sync
        def _(sp):
            sp.dma_start(lg[:], g.ln_g[1:2, :].broadcast_to([P, D])).then_inc(s_ln, 16)
            sp.dma_start(lb[:], g.ln_b[1:2, :].broadcast_to([P, D])).then_inc(s_ln, 16)
            load_mods(sp, g, gate, 0, GATE2, False, s_gate)
            load_mods(sp, g, shift, 1, SHIFT1, False, s_mods)
            load_mods(sp, g, scale, 1, SCALE1, False, s_mods)
            sp.dma_start(wkv[:], g.w_kv_a.rearrange("(k p) n -> p k n", p=P)).then_inc(s_ld, 16)
            sp.dma_start(wdq[:], g.w_dq.rearrange("(k p) n -> p k n", p=P)).then_inc(s_ld, 16)
            sp.dma_start(gkv[:], g.kv_norm_g.broadcast_to([P, KVR])).then_inc(s_ld, 16)
            sp.dma_start(gq[:], g.q_norm_g.broadcast_to([P, QR])).then_inc(s_ld, 16)
            sp.dma_start(trig[:], g.const["trig_tok"]).then_inc(s_ld, 16)
            for t in range(TILES):
                n, par = rows_of(t), t % 2
                if t == PT - 2:
                    sp.wait_ge(s_gated, PT)
                    load_mods(sp, g, gate, 0, GATE2, True, s_gate)
                    sp.wait_ge(s_h, PT)
                    load_mods(sp, g, shift, 1, SHIFT1, True, s_mods)
                    load_mods(sp, g, scale, 1, SCALE1, True, s_mods)
                sp.wait_ge(s_nrm, t + 1)
                sp.dma_start(g.lat[t * P:t * P + n, :], lat[0:n, par, :]).then_inc(s_st[par], 16)
                sp.dma_start(g.krope[t * P:t * P + n, :], kr[0:n, par, 0, :]).then_inc(s_st[par], 16)
            sp.wait_ge(s_st[0], 32 * (PT // 2 + 1))
            sp.wait_ge(s_st[1], 32 * (PT // 2))

        @block.gpsimd
        def _(po):
            def gather(t):
                n, par = rows_of(t), t % 2
                for k, y in enumerate((ya, yb)):
                    nc.gpsimd.indirect_dma_start(y[0:n, par, :], None, g.yrows,
                                                 bass.IndirectOffsetOnAxis(g.dest[0:n, k, t:t + 1], axis=0)
                                                 ).then_inc(s_g[par], 16)

            gather(0)
            gather(1)
            for t in range(TILES):
                n = rows_of(t)
                po.wait_ge(s_gate, 16 if t < PT else 16 + 16 * BATCHES)
                po.wait_ge(s_both, t + 1)
                z = zr[0:n, t % RING, :]
                nc.gpsimd.tensor_tensor(z, z, gate[0:n, :], ALU.mult).then_inc(s_gated, 1)
                if t + 2 < TILES:
                    gather(t + 2)

        @block.tensor
        def _(pe):
            T = nc.tensor

            def project(t):
                n = rows_of(t)
                pe.wait_ge(s_x, t + 1)
                pe.wait_ge(s_h, t + 1)
                if t >= 1:
                    pe.wait_ge(s_xT, t)
                for k in range(KD):
                    T.transpose(psT[:, k, 0:n], g.x[0:n, t, k * P:(k + 1) * P], g.ident[0:n, 0:n])
                for k in range(KD):
                    mm = T.transpose(psT[:, KD + k, 0:n], h[0:n, k * P:(k + 1) * P], g.ident[0:n, 0:n])
                mm.then_inc(s_T, 1)
                pe.wait_ge(s_ld, 80)
                pe.wait_ge(s_xT, t + 1)
                if t >= 1:
                    pe.wait_ge(s_nrm, t)
                for k in range(KD):
                    T.matmul(psK[0:n, 0:KVA], xT[:, k, 0:n], wkv[:, k, :], start=(k == 0), stop=(k == KD - 1))
                for k in range(KD):
                    mm = T.matmul(psQ[0:n, :], hT[:, k, 0:n], wdq[:, k, :], start=(k == 0), stop=(k == KD - 1))
                mm.then_inc(s_mm, 1)

            def turn_latents(t):
                n, par = rows_of(t), t % 2
                pe.wait_ge(s_nrm, t + 1)
                if t >= 1:
                    pe.wait_ge(s_out, t)
                for k in range(4):
                    T.transpose(psC[:, k, 0:n], cq[0:n, k * P:(k + 1) * P], g.ident[0:n, 0:n])
                for k in range(2):
                    T.transpose(psL[:, k, 0:n], lat[0:n, par, k * P:(k + 1) * P], g.ident[0:n, 0:n])
                T.transpose(psL[:, 2, 0:n], kr[0:n, par, :, :].rearrange("p a r -> p (a r)"),
                            g.ident[0:n, 0:n]).then_inc(s_post, 1)

            project(0)
            for t in range(1, TILES):
                project(t)
                turn_latents(t - 1)
            turn_latents(TILES - 1)

        @block.scalar
        def _(act):
            S = nc.scalar

            def first(t):
                n, par = rows_of(t), t % 2
                act.wait_ge(s_g[par], 32 * (t // 2) + 32)
                if t >= RING:
                    act.wait_ge(s_x, t - RING + 1)
                S.activation(zr[0:n, t % RING, :], ya[0:n, par, :], ACT.Copy,
                             scale=g.weight[0:n, 0, t:t + 1]).then_inc(s_first, 1)

            def normalise_x(t):
                n, par, z = rows_of(t), t % 2, zr[0:rows_of(t), t % RING, :]
                act.wait_ge(s_var, t + 1)
                S.activation(sd[0:n, par:par + 1], sd[0:n, par:par + 1], ACT.Sqrt).then_inc(s_dev, 1)
                act.wait_ge(s_off, t + 1)
                S.activation(z, z, ACT.Identity, bias=off[0:n, par:par + 1], scale=sd[0:n, par:par + 1]
                             ).then_inc(s_norm, 1)

            def copy_turned(t):
                n = rows_of(t)
                act.wait_ge(s_T, t + 1)
                if t >= 1:
                    act.wait_ge(s_mm, t)
                for z in range(2):
                    S.copy(xT[:, z * 4:z * 4 + 4, 0:n], psT[:, z * 4:z * 4 + 4, 0:n])
                    S.copy(hT[:, z * 4:z * 4 + 4, 0:n], psT[:, KD + z * 4:KD + z * 4 + 4, 0:n])
                act.drain()
                act.sem_inc(s_xT, 1)

            def squares(t):
                n = rows_of(t)
                act.wait_ge(s_mm, t + 1)
                S.activation(junk[0:n, 0:KVR], psK[0:n, 0:KVR], ACT.Square, accum_out=ss[0:n, 0:1])
                act.drain()
                S.activation(junk[0:n, KVR:KVR + QR], psQ[0:n, :], ACT.Square, accum_out=ss[0:n, 1:2])
                act.drain()
                act.sem_inc(s_ss, 1)
                act.wait_ge(s_ms, t + 1)
                S.activation(rs[0:n, :], rs[0:n, :], ACT.Sqrt)
                act.drain()
                act.sem_inc(s_root, 1)

            def back(t):
                n = rows_of(t)
                act.wait_ge(s_post, t + 1)
                S.copy(g.cqT[:, :, t * P:t * P + n], psC[:, :, 0:n])
                S.copy(g.latT[:, :, t * P:t * P + n], psL[:, 0:2, 0:n])
                S.copy(g.krT[:, t * P:t * P + n], psL[:, 2, 0:n])
                act.drain()
                act.sem_inc(s_out, 1)

            first(0)
            first(1)
            normalise_x(0)
            for t in range(TILES):
                copy_turned(t)
                if t + 2 < TILES:
                    first(t + 2)
                if t + 1 < TILES:
                    normalise_x(t + 1)
                squares(t)
                if t >= 1:
                    back(t - 1)
            back(TILES - 1)

        @block.vector
        def _(v):
            V = nc.vector

            def both(t):
                n, z = rows_of(t), zr[0:rows_of(t), t % RING, :]
                v.wait_ge(s_first, t + 1)
                V.scalar_tensor_tensor(out=z, in0=yb[0:n, t % 2, :], scalar=g.weight[0:n, 1, t:t + 1], in1=z,
                                       op0=ALU.mult, op1=ALU.add).then_inc(s_both, 1)

            def middle(t):
                n, par, z = rows_of(t), t % 2, zr[0:rows_of(t), t % RING, :]
                v.wait_ge(s_gated, t + 1)
                V.scalar_tensor_tensor(out=z, in0=g.x[0:n, t, :], scalar=ALPHA, in1=z, op0=ALU.mult, op1=ALU.add)
                v.drain()
                for a in range(2):
                    V.bn_stats(stats[0:n, a, :], z[:, a * HALF:(a + 1) * HALF])
                v.drain()
                V.bn_aggr(mv[0:n, :], stats[0:n, :, :].rearrange("p a s -> p (a s)"))
                v.drain()
                s = sd[0:n, par:par + 1]
                V.tensor_scalar(s, mv[0:n, 1:2], EPS, None, ALU.add).then_inc(s_var, 1)
                v.wait_ge(s_dev, t + 1)
                V.reciprocal(s, s)
                v.drain()
                V.tensor_scalar(off[0:n, par:par + 1], mv[0:n, 0:1], s, -1.0, ALU.mult, ALU.mult).then_inc(s_off, 1)

            def finish(t):
                n, z = rows_of(t), zr[0:rows_of(t), t % RING, :]
                v.wait_ge(s_norm, t + 1)
                V.tensor_tensor(z, z, lg[0:n, :], ALU.mult)
                v.drain()
                V.tensor_tensor(g.x[0:n, t, :], z, lb[0:n, :], ALU.add).then_inc(s_x, 1)
                v.drain()

            def modulate(t):
                n = rows_of(t)
                v.wait_ge(s_mods, 32 if t < PT else 32 + 32 * BATCHES)
                if t >= 1:
                    v.wait_ge(s_T, t)
                V.scalar_tensor_tensor(out=h[0:n, :], in0=scale[0:n, :], scalar=1.0, in1=g.x[0:n, t, :],
                                       op0=ALU.add, op1=ALU.mult)
                v.drain()
                V.tensor_tensor(h[0:n, :], h[0:n, :], shift[0:n, :], ALU.add).then_inc(s_h, 1)

            def normalise(t):
                n, par = rows_of(t), t % 2
                v.wait_ge(s_ss, t + 1)
                V.tensor_scalar(rs[0:n, 0:1], ss[0:n, 0:1], 1.0 / KVR, EPS, ALU.mult, ALU.add)
                V.tensor_scalar(rs[0:n, 1:2], ss[0:n, 1:2], 1.0 / QR, EPS, ALU.mult, ALU.add)
                v.drain()
                v.sem_inc(s_ms, 1)
                if t >= 2:
                    v.wait_ge(s_st[par], 32 * (t // 2))
                if t >= 1:
                    v.wait_ge(s_post, t)
                c, s = trig[0:n, t, 0, :], trig[0:n, t, 1, :]
                a, b = psK[0:n, KVR:KVR + half], psK[0:n, KVR + half:KVA]
                V.tensor_tensor(r4[0:n, 0, :], a, c, ALU.mult)
                V.tensor_tensor(r4[0:n, 1, :], b, s, ALU.mult)
                V.tensor_tensor(r4[0:n, 2, :], a, s, ALU.mult)
                V.tensor_tensor(r4[0:n, 3, :], b, c, ALU.mult)
                v.drain()
                for z in range(2):
                    V.tensor_tensor(kr[0:n, par, z, 0:half], r4[0:n, 0, :], r4[0:n, 1, :], ALU.subtract)
                    V.tensor_tensor(kr[0:n, par, z, half:ROPE], r4[0:n, 2, :], r4[0:n, 3, :], ALU.add)
                v.wait_ge(s_root, t + 1)
                V.reciprocal(rs[0:n, :], rs[0:n, :])
                v.drain()
                V.scalar_tensor_tensor(out=lat[0:n, par, :], in0=psK[0:n, 0:KVR], scalar=rs[0:n, 0:1],
                                       in1=gkv[0:n, :], op0=ALU.mult, op1=ALU.mult)
                V.scalar_tensor_tensor(out=cq[0:n, :], in0=psQ[0:n, :], scalar=rs[0:n, 1:2], in1=gq[0:n, :],
                                       op0=ALU.mult, op1=ALU.mult)
                v.drain()
                v.sem_inc(s_nrm, 1)

            v.wait_ge(s_ln, 32)
            both(0)
            middle(0)
            both(1)
            finish(0)
            modulate(0)
            v.wait_ge(s_ld, 80)
            for t in range(TILES):
                if t + 1 < TILES:
                    middle(t + 1)
                if t + 2 < TILES:
                    both(t + 2)
                if t + 1 < TILES:
                    finish(t + 1)
                    modulate(t + 1)
                normalise(t)


def stage_heads(nc, g):
    with nc.cleanup_on_exit(), ExitStack() as ctx:
        def sb(n, s, d=F32):
            return ctx.enter_context(nc.sbuf_tensor(f"a_{n}", s, d))

        def sem(n):
            return nc.alloc_semaphore(f"a_{n}")

        wq, wk = sb("wq", [P, 4, 2 * P]), sb("wk", [P, 2, NOPE])
        wkT, wv = sb("wkT", [P, KVR]), sb("wv", [P, 2, DV])
        trig = sb("trig", [P, N])
        qn, qr, kT = sb("qn", [P, N]), sb("qr", [P, N]), sb("kT", [P, SEQ])
        vv = sb("v", [P, PT, DV])
        pb = sb("p", [P, 2, SEQ])
        pT = sb("pT", [P, 2, PT, P])
        nm, rsum, rinv = sb("nm", [P, 2]), sb("rsum", [P, 2]), sb("rinv", [P, 2])
        psS = ctx.enter_context(nc.psum_tensor("a_psS", [P, 2, SEQ], F32))
        psP = ctx.enter_context(nc.psum_tensor("a_psP", [P, PT, P], F32))
        psJ = ctx.enter_context(nc.psum_tensor("a_psJ", [P, 2, HALF], F32))
        s_c, s_w, s_job, s_ja, s_jv, s_S, s_max, s_exp, s_nrm, s_T, s_pT, s_o = (sem(x) for x in (
            "trig_loaded", "weights_loaded", "job_summed", "jobs_out_act", "jobs_out_dve", "scores", "maxima",
            "exp_ready", "weights_ready", "weights_turned", "pT_ready", "outputs_summed"))
        block = ctx.enter_context(nc.Block())

        RUNS = ((0, HALF), (HALF, HALF), (SEQ, NSAMP))
        JOBS = 11
        ACT_JOBS = 8 + PT

        @block.sync
        def _(sp):
            sp.dma_start(trig[:], g.const["trig_feat"]).then_inc(s_c, 16)
            with sp.Fori(0, H) as h:
                sp.wait_ge(s_job, JOBS * h + JOBS)
                for dst, src in ((wq[:].rearrange("p k n -> p (k n)"), g.w_uq), (wk[:].rearrange("p k n -> p (k n)"), g.w_uk),
                                 (wkT[:], g.w_ukT), (wv[:].rearrange("p k n -> p (k n)"), g.w_uv)):
                    sp.dma_start(dst, src[bass.ds(h, 1)].rearrange("o p n -> (o p) n")).then_inc(s_w, 16)

        @block.tensor
        def _(pe):
            T = nc.tensor
            pe.sem_inc(s_job, JOBS)
            pe.wait_ge(s_c, 16)
            with pe.Fori(0, H) as h:
                A = h * ACT_JOBS + ACT_JOBS
                pe.wait_ge(s_w, 64 * h + 64)
                for r, (lo, n) in enumerate(RUNS):
                    for z in range(2):
                        if z == 0:
                            pe.wait_ge(s_ja, A + r)
                        elif r == 0:
                            pe.wait_ge(s_ja, A - 1)
                        else:
                            pe.wait_ge(s_jv, 3 * h + r)
                        for k in range(4):
                            mm = T.matmul(psJ[:, z, 0:n], wq[:, k, z * P:(z + 1) * P], g.cqT[:, k, lo:lo + n],
                                          start=(k == 0), stop=(k == 3))
                        mm.then_inc(s_job, 1)
                for c in range(2):
                    if c == 0:
                        pe.wait_ge(s_ja, A + 3)
                    else:
                        pe.wait_ge(s_jv, 3 * h + 3)
                    for k in range(2):
                        mm = T.matmul(psJ[:, c, :], wk[:, k, :], g.latT[:, k, c * HALF:(c + 1) * HALF],
                                      start=(k == 0), stop=(k == 1))
                    mm.then_inc(s_job, 1)
                for c in range(2):
                    pe.wait_ge(s_ja, A + 4 + c)
                    for j in range(4):
                        for k in range(2):
                            mm = T.matmul(psJ[:, c, j * DV:(j + 1) * DV],
                                          g.latT[:, k, (c * 4 + j) * P:(c * 4 + j + 1) * P], wv[:, k, :],
                                          start=(k == 0), stop=(k == 1))
                    mm.then_inc(s_job, 1)
                pe.wait_ge(s_ja, A + 6)
                for c in range(2):
                    mm = T.matmul(psJ[:, 0, c * NSAMP:(c + 1) * NSAMP], wkT[:, c * P:(c + 1) * P], qn[:, SEQ:N],
                                  start=True, stop=True)
                mm.then_inc(s_job, 1)

                def scores(i):
                    par, width = i % 2, (i + 1) * P
                    pe.wait_ge(s_exp, h * PT + i + 1)
                    q = slice(i * P, (i + 1) * P)
                    for lo in range(0, width, HALF):
                        hi = min(width, lo + HALF)
                        T.matmul(psS[:, par, lo:hi], qn[:, q], kT[:, lo:hi], start=True, stop=False)
                        last = hi == width
                        mm = T.matmul(psS[:, par, lo:hi], qr[:, q], g.krT[:, lo:hi], start=False, stop=not last)
                        if last:
                            mm = T.matmul(psS[:, par, i * P:width], g.ident[:], g.qmask[:], start=False, stop=True)
                    mm.then_inc(s_S, 1)

                def outputs(i):
                    pe.wait_ge(s_pT, h * PT + i + 2)
                    pe.wait_ge(s_ja, A + 7 + i)
                    for j in range(i + 1):
                        mm = T.matmul(psJ[:, (i + 1) % 2, 0:P], vv[:, j, :], pT[:, i % 2, j, :],
                                      start=(j == 0), stop=(j == i))
                    mm.then_inc(s_o, 1)

                pe.wait_ge(s_ja, A + 7)
                pe.wait_ge(s_jv, 3 * h + 3)
                scores(0)
                for i in range(PT):
                    if i + 1 < PT:
                        scores(i + 1)
                    pe.wait_ge(s_nrm, h * PT + i + 1)
                    pe.wait_ge(s_pT, h * PT + i + 1)
                    for j in range(i + 1):
                        mm = T.transpose(psP[:, j, :], pb[:, i % 2, j * P:(j + 1) * P], g.ident[:])
                    mm.then_inc(s_T, 1)
                    if i >= 1:
                        outputs(i - 1)
                outputs(PT - 1)

        @block.scalar
        def _(act):
            S = nc.scalar
            act.sem_inc(s_ja, ACT_JOBS)
            act.sem_inc(s_exp, 2)
            act.sem_inc(s_pT, 1)
            with act.Fori(0, H) as h:
                J = JOBS * h + JOBS
                for r, (lo, n) in enumerate(RUNS):
                    act.wait_ge(s_job, J + 2 * r + 1)
                    S.copy(qn[:, lo:lo + n], psJ[:, 0, 0:n]).then_inc(s_ja, 1)
                for c in range(2):
                    act.wait_ge(s_job, J + 7 + c)
                    S.copy(kT[:, c * HALF:(c + 1) * HALF], psJ[:, c, :]).then_inc(s_ja, 1)
                for c in range(2):
                    act.wait_ge(s_job, J + 9 + c)
                    S.copy(vv[:, c * 4:c * 4 + 4, :], psJ[:, c, :].rearrange("p (j v) -> p j v", j=4)).then_inc(s_ja, 1)
                act.wait_ge(s_job, J + 11)
                act.wait_ge(s_jv, 3 * h + 3)
                for z in range(3):
                    src = psJ[:, 0, z * NSAMP:(z + 1) * NSAMP] if z < 2 else qr[:, SEQ:N]
                    S.copy(g.qS[:, z, :, bass.ds(h, 1), :].rearrange("p b o t -> p b (o t)"),
                           src.rearrange("p (b t) -> p b t", b=BATCHES))
                act.drain()
                act.sem_inc(s_ja, 1)

                def exp(i):
                    par, width = i % 2, (i + 1) * P
                    act.wait_ge(s_max, h * PT + i + 1)
                    act.wait_ge(s_T, h * PT + i + 1)
                    S.activation(pb[:, par, 0:width], psS[:, par, 0:width], ACT.Exp, bias=nm[:, par:par + 1],
                                 scale=SCALE, accum_out=rsum[:, par:par + 1])
                    act.drain()
                    act.sem_inc(s_exp, 1)

                def output(i):
                    act.wait_ge(s_o, h * PT + i + 3)
                    S.copy(g.mixT[:, bass.ds(h, 1), i * P:(i + 1) * P].rearrange("p o t -> p (o t)"),
                           psJ[:, (i + 1) % 2, 0:P]).then_inc(s_ja, 1)

                exp(0)
                for i in range(PT):
                    if i + 1 < PT:
                        exp(i + 1)
                    act.wait_ge(s_T, h * PT + i + 3)
                    act.wait_ge(s_o, h * PT + i + 1)
                    for lo in range(0, i + 1, 4):
                        hi = min(i + 1, lo + 4)
                        S.copy(pT[:, i % 2, lo:hi, :], psP[:, lo:hi, :])
                    act.drain()
                    act.sem_inc(s_pT, 1)
                    if i >= 1:
                        output(i - 1)
                output(PT - 1)

        @block.vector
        def _(v):
            V = nc.vector
            v.sem_inc(s_T, 2)
            v.sem_inc(s_o, 2)
            v.wait_ge(s_c, 16)
            with v.Fori(0, H) as h:
                for r, (lo, n) in enumerate(RUNS):
                    v.wait_ge(s_job, JOBS * h + JOBS + 2 * r + 2)
                    V.tensor_tensor(qr[:, lo:lo + n], psJ[:, 1, 0:n], trig[:, lo:lo + n], ALU.mult).then_inc(s_jv, 1)

                def maximum(i):
                    par, width = i % 2, (i + 1) * P
                    v.wait_ge(s_S, h * PT + i + 1)
                    V.tensor_reduce(nm[:, par:par + 1], psS[:, par, 0:width], AX, ALU.max)
                    v.drain()
                    V.tensor_scalar(nm[:, par:par + 1], nm[:, par:par + 1], -SCALE, None, ALU.mult)
                    v.drain()
                    v.sem_inc(s_max, 1)

                maximum(0)
                for i in range(PT):
                    par, width = i % 2, (i + 1) * P
                    v.wait_ge(s_exp, h * PT + i + 3)
                    V.reciprocal(rinv[:, par:par + 1], rsum[:, par:par + 1])
                    v.drain()
                    V.tensor_scalar(pb[:, par, 0:width], pb[:, par, 0:width], rinv[:, par:par + 1], None, ALU.mult)
                    v.drain()
                    v.sem_inc(s_nrm, 1)
                    if i + 1 < PT:
                        maximum(i + 1)


def stage_sample(nc, g):
    NQ = H * STEPS
    with nc.cleanup_on_exit(), ExitStack() as ctx:
        def sb(n, s, d=F32):
            return ctx.enter_context(nc.sbuf_tensor(f"s_{n}", s, d))

        def sem(n):
            return nc.alloc_semaphore(f"s_{n}")

        pt = sb("page_table", [1, BATCHES * PAGES], I32)
        KW = 3 * PAGE
        keys = sb("page_keys", [P, 2, PAGES, KW])
        vals = sb("page_values", [P, 2, PAGES, KVR])
        new = sb("new", [STEPS, 2, KVR])
        qB = sb("q", [P, 2, 3, NQ])
        pb = sb("p", [NQ, CTX])
        pT = sb("pT", [P, PAGES + 1, NQ])
        wv = sb("wv", [P, H, 2 * DV])
        oQ = sb("o_rows", [NQ, BATCHES, KVR])
        oS = pT[:, 0:2 * BATCHES, :].rearrange("p (c b) q -> p c b q", c=2)
        nm, rsum = sb("nm", [NQ, 1]), sb("rsum", [NQ, 2])
        psS = ctx.enter_context(nc.psum_tensor("s_psS", [P, 5 * HALF], F32))
        psP = ctx.enter_context(nc.psum_tensor("s_psP", [P, PAGES, NQ], F32))
        psO = ctx.enter_context(nc.psum_tensor("s_psO", [P, HALF], F32))
        s_pt, s_wv, s_q, s_S, s_max, s_exp, s_nrm, s_T, s_pT, s_o, s_oS, s_fin, s_new = (sem(x) for x in (
            "table_loaded", "wv_loaded", "queries_staged", "scores", "maximum", "exp_ready", "weights_ready",
            "weights_turned", "pT_ready", "outputs_summed", "outputs_kept", "values_summed", "new_loaded"))
        s_keys = [sem("keys_loaded0"), sem("keys_loaded1")]
        s_vals = [sem("values_loaded0"), sem("values_loaded1")]
        s_turning = sem("turning")
        block = ctx.enter_context(nc.Block())

        def load_pages(eng, b, par, dst, cols, done):
            for j in range(PAGES):
                page = eng.value_load(pt[0:1, bass.ds(b * PAGES + j, 1)], min_val=0, max_val=g.cache.shape[0] - 1)
                eng.dma_start(dst[:, par, j, :], g.cache[bass.ds(page, 1), :, cols].rearrange("o p n -> (o p) n")
                              ).then_inc(done[par], 16)

        @block.sync
        def _(sp):
            sp.dma_start(pt[:], g.page_table).then_inc(s_pt, 16)
            sp.dma_start(wv[:], g.w_uv.rearrange("h p n -> p h n")).then_inc(s_wv, 16)
            sp.wait_ge(s_pt, 16)
            with sp.Fori(0, BATCHES // 2) as i:
                for par in range(2):
                    b = i * 2 + par
                    sp.wait_ge(s_S, b + 1)
                    load_pages(sp, b, par, keys, slice(0, KW), s_keys)

        @block.gpsimd
        def _(po):
            def stage_queries(b, par):
                po.wait_ge(s_S, b + 1)
                nc.gpsimd.tensor_copy(qB[:, par, :, :].rearrange("p z (h t) -> p z h t", h=H),
                                      g.qS[:, :, bass.ds(b, 1), :, :].rearrange("p z o h t -> p z (o h) t"))
                po.drain()
                po.sem_inc(s_q, 1)

            def values(b, par):
                po.wait_ge(s_o, b + 1)
                load_pages(po, b, par, vals, slice(KW, KVW), s_vals)
                po.dma_start(new[:, par, :], g.lat[bass.ds(SEQ + b * STEPS, STEPS), :]).then_inc(s_vals[par], 16)

            po.wait_ge(s_pt, 16)
            po.sem_inc(s_turning, 1)
            stage_queries(0, 0)
            with po.Fori(0, BATCHES // 2 - 1) as i:
                for par in range(2):
                    stage_queries(i * 2 + par + 1, 1 - par)
                    values(i * 2 + par, par)
            stage_queries(BATCHES - 1, 1)
            values(BATCHES - 2, 0)
            values(BATCHES - 1, 1)

        @block.tensor
        def _(pe):
            T = nc.tensor

            def scores(b, par, i):
                pe.wait_ge(s_q, b + 1)
                pe.wait_ge(s_keys[par], 16 * PAGES * (i + 1))
                pe.wait_ge(s_exp, b + 1)
                for c in range(4):
                    for z in range(3):
                        T.matmul(psS[0:NQ, c * HALF:(c + 1) * HALF], qB[:, par, z, :],
                                 keys[:, par, c * 4:c * 4 + 4, z * PAGE:(z + 1) * PAGE],
                                 start=(z == 0), stop=(z == 2))
                cols = bass.ds(SEQ + b * STEPS, STEPS)
                for z in range(2):
                    T.matmul(psS[0:NQ, PAST:CTX], qB[:, par, z, :],
                             g.latT[:, z, cols], start=(z == 0), stop=False)
                T.matmul(psS[0:NQ, PAST:CTX], qB[:, par, 2, :], g.krT[:, cols], start=False, stop=False)
                T.matmul(psS[0:NQ, PAST:CTX], g.ident[0:NQ, 0:NQ], g.smask[0:NQ, :],
                         start=False, stop=True).then_inc(s_S, 1)

            def turn(b):
                pe.wait_ge(s_nrm, b + 1)
                pe.wait_ge(s_oS, b + 1)
                pe.sem_inc(s_turning, 1)
                for j in range(PAGES):
                    T.transpose(psP[:, j, :], pb[:, j * PAGE:(j + 1) * PAGE], g.ident[0:NQ, 0:NQ])
                T.transpose(psO[0:STEPS, KVR:KVR + NQ], pb[:, PAST:CTX], g.ident[0:NQ, 0:NQ]).then_inc(s_T, 1)

            def outputs(b, par, i):
                pe.wait_ge(s_vals[par], 16 * (PAGES + 1) * (i + 1))
                pe.wait_ge(s_pT, b + 1)
                for j in range(PAGES):
                    T.matmul(psO[0:NQ, 0:KVR], pT[:, j, :], vals[:, par, j, :],
                             start=(j == 0), stop=False)
                T.matmul(psO[0:NQ, 0:KVR], pT[0:STEPS, PAGES, :], new[:, par, :],
                         start=False, stop=True).then_inc(s_o, 1)

            pe.sem_inc(s_o, 2)
            pe.sem_inc(s_S, 2)
            scores(0, 0, 0)
            with pe.Fori(0, BATCHES // 2 - 1) as i:
                for par in range(2):
                    b = i * 2 + par
                    turn(b)
                    scores(b + 1, 1 - par, i + par)
                    outputs(b, par, i)
            turn(BATCHES - 2)
            scores(BATCHES - 1, 1, BATCHES // 2 - 1)
            outputs(BATCHES - 2, 0, BATCHES // 2 - 1)
            turn(BATCHES - 1)
            outputs(BATCHES - 1, 1, BATCHES // 2 - 1)
            pe.wait_ge(s_oS, BATCHES + 1)
            pe.sem_inc(s_turning, 1)
            for b in range(BATCHES):
                for c in range(2):
                    mm = T.transpose(psP[:, c * BATCHES + b, :], oQ[:, b, c * P:(c + 1) * P], g.ident[0:NQ, 0:NQ])
            mm.then_inc(s_T, 1)
            pe.wait_ge(s_oS, BATCHES + 2)
            pe.wait_ge(s_wv, 16)
            for h in range(H):
                for c in range(2):
                    mm = T.matmul(psO[:, h * NSAMP:(h + 1) * NSAMP], wv[:, h, c * DV:(c + 1) * DV],
                                  oS[:, c, :, h * STEPS:(h + 1) * STEPS], start=(c == 0), stop=(c == 1))
            mm.then_inc(s_fin, 1)

        @block.scalar
        def _(act):
            S = nc.scalar
            act.sem_inc(s_exp, 1)
            act.sem_inc(s_oS, 1)

            def exp(b):
                act.wait_ge(s_max, b + 1)
                act.wait_ge(s_T, b + 1)
                S.activation(pb[:], psS[0:NQ, 0:CTX], ACT.Exp, bias=nm[:], scale=SCALE, accum_out=rsum[:, 0:1])
                act.drain()
                act.sem_inc(s_exp, 1)

            def copy_turned(b):
                act.wait_ge(s_T, b + 2)
                act.wait_ge(s_o, b + 2)
                for z in range(2):
                    S.copy(pT[:, z * 8:z * 8 + 8, :], psP[:, z * 8:z * 8 + 8, :])
                S.copy(pT[0:STEPS, PAGES, :], psO[0:STEPS, KVR:KVR + NQ])
                act.drain()
                act.sem_inc(s_pT, 1)

            def keep(b):
                act.wait_ge(s_o, b + 3)
                S.copy(oQ[:, bass.ds(b, 1), :].rearrange("p o n -> p (o n)"), psO[0:NQ, 0:KVR])
                act.drain()
                act.sem_inc(s_oS, 1)

            exp(0)
            with act.Fori(0, BATCHES - 1) as b:
                copy_turned(b)
                exp(b + 1)
                keep(b)
            copy_turned(BATCHES - 1)
            keep(BATCHES - 1)
            act.wait_ge(s_T, BATCHES + 2)
            for c in range(2):
                S.copy(oS[:, c, :, :], psP[:, c * BATCHES:(c + 1) * BATCHES, :])
            act.drain()
            act.sem_inc(s_oS, 1)
            act.wait_ge(s_fin, 1)
            S.copy(g.mixT[:, :, SEQ:N], psO[:].rearrange("p (h t) -> p h t", h=H))

        @block.vector
        def _(v):
            V = nc.vector
            v.sem_inc(s_T, 1)
            with v.Fori(0, BATCHES) as b:
                v.wait_ge(s_S, b + 3)
                V.tensor_reduce(nm[:], psS[0:NQ, 0:CTX], AX, ALU.max)
                v.drain()
                V.tensor_scalar(nm[:], nm[:], -SCALE, None, ALU.mult)
                v.drain()
                v.sem_inc(s_max, 1)
                v.wait_ge(s_exp, b + 2)
                V.reciprocal(rsum[:, 1:2], rsum[:, 0:1])
                v.drain()
                V.tensor_scalar(pb[:], pb[:], rsum[:, 1:2], None, ALU.mult)
                v.drain()
                v.sem_inc(s_nrm, 1)


OUTPUTS = {
    "y_prompt": (SEQ, D), "y_sample": (NSAMP, D),
    "C_p": (P, PAIRS, AUG), "C_s": (P, BATCHES, PAIRS, AUG), "m_out": (H, 1 + BATCHES),
    "lat": (N, KVR), "krope": (N, ROPE),
}


def laid_out(inputs):
    a = {k: np.asarray(v) for k, v in inputs.items()}
    o = {}
    o["x_prompt"] = a["x_prompt"].reshape(SEQ, D)
    o["x_sample"] = a["x_sample"].reshape(NSAMP, D)
    c = np.concatenate([a["c_prompt"], a["c_sample"]], 0)
    o["cT"] = c.T.reshape(KD, P, 9).transpose(1, 0, 2).reshape(P, KD * 9)
    o["ada_w"] = a["ada_w"].reshape(2, KD, P, 12, HALF).transpose(0, 3, 2, 1, 4).reshape(24, P, KD * HALF)
    o["ada_b"] = a["ada_b"].reshape(24, HALF)
    o["ln_g"] = a["ln_g"].reshape(4, D)
    o["ln_b"] = a["ln_b"].reshape(4, D)
    o["a_w_in"] = a["a_w_in"][0]
    o["a_b_gates"] = a["a_b_gates"]
    o["a_norm_g"] = a["a_norm_g"]
    o["a_w_out"] = a["a_w_out"][0]
    st = np.concatenate([a["state_C"][0], a["state_n"][0][..., None]], -1)
    o["state"] = st.reshape(BATCHES, PAIRS, 2, DK, AUG).transpose(2, 3, 0, 1, 4).reshape(P, BATCHES, PAIRS, AUG)
    o["state_mT"] = a["state_m"][0].T
    o["w_kv_a"] = a["b_w_kv_a"]
    o["kv_norm_g"] = a["b_kv_norm_g"].reshape(1, KVR)
    o["q_norm_g"] = a["b_q_norm_g"]
    o["w_dq"] = a["b_w_dq"][0]
    uq = a["b_w_uq"][0].reshape(4, P, H, NOPE + ROPE)
    half = ROPE // 2
    uq = np.concatenate([uq, uq[..., NOPE + half:], uq[..., NOPE:NOPE + half]], -1)
    o["w_uq"] = uq.transpose(2, 1, 0, 3).reshape(H, P, 4 * 2 * P)
    uk, uv = a["b_w_uk"], a["b_w_uv"]
    o["w_uk"] = uk.reshape(2, P, H, NOPE).transpose(2, 1, 0, 3).reshape(H, P, 2 * NOPE)
    o["w_ukT"] = uk.transpose(1, 2, 0)
    o["w_uv"] = uv.reshape(2, P, H, DV).transpose(2, 1, 0, 3).reshape(H, P, 2 * DV)
    o["w_o"] = a["b_w_o"][0]
    o["router_w"] = a["router_w"]
    o["router_b"] = a["router_b"].reshape(1, E)
    for n in ("gate", "up", "down"):
        w = a[f"e_w_{n}"]
        o[f"e_{n}"] = w.reshape((2 * E,) + w.shape[2:])
    cl, ck = a["cache_latent"], a["cache_krope"]
    lt = cl.transpose(0, 2, 1).reshape(-1, 2, P, PAGE).transpose(0, 2, 1, 3).reshape(-1, P, 2 * PAGE)
    kt = ck.transpose(0, 2, 1)
    o["cache"] = np.concatenate([lt, np.concatenate([kt, kt], 1), cl], -1)
    o["page_table"] = a["page_table"].reshape(1, BATCHES * PAGES).astype(np.int32)
    return {k: np.ascontiguousarray(v) for k, v in o.items()}


def constants():
    o = {}
    s, t = np.arange(P)[:, None], np.arange(P)[None, :]
    same = (s // STEPS == t // STEPS) & (s < NSAMP) & (t < NSAMP)
    o["ident"] = np.eye(P)
    o["tri"] = np.stack([s <= t, (s <= t) & same, s < t], 1)
    o["lmask"] = np.stack([np.where(s <= t, 0.0, NEG), np.where((s <= t) & same, 0.0, NEG)], 1)
    o["qmask"] = np.where(t <= s, 0.0, NEG)
    o["smask"] = np.where(np.arange(STEPS)[None, :] <= np.arange(NSAMP)[:, None] % STEPS, 0.0, NEG)
    o["bmask"] = (np.arange(NSAMP)[:, None] // STEPS == np.arange(BATCHES)[None, :])
    o["bmaskT"] = np.broadcast_to(o["bmask"].T.reshape(1, BATCHES, NSAMP), (P, BATCHES, NSAMP))
    o["count_down"] = np.broadcast_to(E - np.arange(E)[None], (P, E))
    o["count_up"] = np.broadcast_to(np.arange(SLOTS + 1)[None], (P, SLOTS + 1))
    o["steps"] = np.broadcast_to(P * np.arange(TILES)[None], (P, TILES))
    pos = np.concatenate([np.arange(SEQ), PAST + np.arange(NSAMP) % STEPS]).astype(np.float32)
    half = ROPE // 2
    inv = (10000.0 ** (-np.arange(half) / half)).astype(np.float32)
    ang = pos[:, None] * inv[None]
    cos, sin = np.cos(ang).astype(np.float32), np.sin(ang).astype(np.float32)
    cs = np.zeros((TILES * P, 2, half), np.float32)
    cs[:N, 0], cs[:N, 1] = cos, sin
    o["trig_tok"] = cs.reshape(TILES, P, 2, half).transpose(1, 0, 2, 3)
    o["trig_feat"] = np.concatenate([cos, cos, -sin, sin], 1).T
    o = {k: np.ascontiguousarray(v, dtype=np.float32) for k, v in o.items()}
    ids = np.arange(TILES * P).reshape(TILES, P).T
    o["token_ids"] = np.ascontiguousarray(ids.astype(np.int32))
    o["no_token"] = np.full((SLOTS + 1, P), N, np.int32)
    return o


CONST_SHAPES = {k: (v.shape, v.dtype) for k, v in constants().items()}
RESIDENT = ("ident", "tri", "lmask", "qmask", "smask", "bmask", "count_down", "count_up", "steps")


def stage_constants(nc, g):
    with nc.cleanup_on_exit(), ExitStack() as ctx:
        s, s_one = nc.alloc_semaphore("constants"), nc.alloc_semaphore("ones")
        block = ctx.enter_context(nc.Block())

        @block.sync
        def _(sp):
            for k in RESIDENT:
                t = g.resident[k]
                sp.dma_start(t[:], g.const[k]).then_inc(s, 16)
            sp.wait_ge(s, 16 * len(RESIDENT))
            sp.wait_ge(s_one, 1)

        @block.vector
        def _(v):
            nc.vector.memset(g.ones[:], 1.0)
            v.drain()
            v.sem_inc(s_one, 1)


def build(nc, ins, const, outs, stages=99):
    g = Shared()
    g.x_prompt = ins["x_prompt"]
    g.x_sample = ins["x_sample"]
    g.cT = ins["cT"]
    g.ada_w = ins["ada_w"]
    g.ada_b = ins["ada_b"]
    g.ln_g = ins["ln_g"]
    g.ln_b = ins["ln_b"]
    g.a_w_in = ins["a_w_in"]
    g.a_b_gates = ins["a_b_gates"]
    g.a_norm_g = ins["a_norm_g"]
    g.a_w_out = ins["a_w_out"]
    g.state = ins["state"]
    g.state_mT = ins["state_mT"]
    g.w_kv_a = ins["w_kv_a"]
    g.kv_norm_g = ins["kv_norm_g"]
    g.q_norm_g = ins["q_norm_g"]
    g.w_dq = ins["w_dq"]
    g.w_uq = ins["w_uq"]
    g.w_uk = ins["w_uk"]
    g.w_ukT = ins["w_ukT"]
    g.w_uv = ins["w_uv"]
    g.w_o = ins["w_o"]
    g.router_w = ins["router_w"]
    g.router_b = ins["router_b"]
    g.e_gate = ins["e_gate"]
    g.e_up = ins["e_up"]
    g.e_down = ins["e_down"]
    g.cache = ins["cache"]
    g.page_table = ins["page_table"]
    g.y_prompt = outs["y_prompt"]
    g.y_sample = outs["y_sample"]
    g.C_p = outs["C_p"]
    g.C_s = outs["C_s"]
    g.m_out = outs["m_out"]
    g.lat = outs["lat"]
    g.krope = outs["krope"]
    g.const = const
    ctx = ExitStack()
    with ctx:
        def dram(n, s, d=F32):
            return nc.dram_tensor(n, s, d, kind="Internal").ap()

        def sb(n, s, d=F32):
            return ctx.enter_context(nc.sbuf_tensor(n, s, d))

        g.mods = dram("mods", [9, 12 * D])
        g.qkvo = dram("qkvo", [N, A_IN])
        g.h2 = dram("h2", [N + 1, D])
        g.yrows = dram("yrows", [SLOTS * P, D])
        g.slot_token = dram("slot_token", [(SLOTS + 1) * P, 1], I32)
        g.x = sb("x", [P, TILES, D])
        g.ones = sb("ones", [P, P])
        g.resident = {}
        for k in RESIDENT:
            shape, _ = CONST_SHAPES[k]
            g.resident[k] = sb(f"c_{k}", list(shape))
        g.ident = g.resident["ident"]
        g.tri = g.resident["tri"]
        g.lmask = g.resident["lmask"]
        g.qmask = g.resident["qmask"]
        g.smask = g.resident["smask"]
        g.bmask = g.resident["bmask"]
        g.count_down = g.resident["count_down"]
        g.count_up = g.resident["count_up"]
        g.steps = g.resident["steps"]
        g.s_x = ctx.enter_context(nc.semaphore("x_loaded"))
        stage_constants(nc, g)
        g.logits = sb("logits", [P, TILES, E])
        g.weight = sb("weight", [P, 2, TILES])
        g.dest = sb("dest", [P, 2, TILES], I32)
        g.slot_expert = sb("slot_expert", [P, SLOTS + 1], I32)
        g.slot_fresh = sb("slot_fresh", [P, SLOTS + 1], I32)
        g.slots_used = sb("slots_used", [P, 1], I32)
        with nc.sbuf_tensor("gates", [P, TILES, GATES], F32) as g.gates:
            if stages >= 1:
                stage_ada(nc, g)
            if stages >= 2:
                stage_in_proj(nc, g)
            with nc.sbuf_tensor("mixT0", [P, KD, N], F32) as g.mixT:
                with ExitStack() as gated:
                    def gsb(n, s):
                        return gated.enter_context(nc.sbuf_tensor(n, s, F32))

                    g.u = gsb("u", [P, TILES, H])
                    g.factors = gsb("factors", [P, 3, TILES, H])
                    g.decay = gsb("decay", [P, H, 2 * BATCHES])
                    g.M = gsb("M", [H, N])
                    if stages >= 3:
                        stage_gates(nc, g)
                    if stages >= 4:
                        stage_mlstm(nc, g)
                if stages >= 5:
                    stage_out_proj(nc, g, 0, g.a_w_out)
        if stages >= 6:
            stage_route(nc, g, 0)
        if stages >= 7:
            stage_experts(nc, g, 0)
        if stages == 8:
            stage_combine(nc, g, 0, True)
        with nc.sbuf_tensor("mixT1", [P, KD, N], F32) as g.mixT:
            with ExitStack() as attending:
                def asb(n, s):
                    return attending.enter_context(nc.sbuf_tensor(n, s, F32))

                g.qS = asb("qS", [P, 3, BATCHES, H, STEPS])
                g.latT = asb("latT", [P, 2, N])
                g.krT = asb("krT", [P, N])
                with nc.sbuf_tensor("cqT", [P, 4, N], F32) as g.cqT:
                    if stages >= 9:
                        stage_combine_latents(nc, g)
                    if stages >= 10:
                        stage_heads(nc, g)
                if stages >= 11:
                    stage_sample(nc, g)
            if stages >= 12:
                stage_out_proj(nc, g, 1, g.w_o)
        if stages >= 13:
            stage_route(nc, g, 1)
            stage_experts(nc, g, 1)
            stage_combine(nc, g, 1, True)
    return g


def kernel(**inputs):
    from concourse import bacc
    from concourse.bass_utils import run_bass_kernel_spmd

    nc = bacc.Bacc("TRN2", target_bir_lowering=False, num_devices=1)
    arrays = laid_out(inputs)
    ins = {k: nc.dram_tensor(f"in_{k}", v.shape, mybir.dt.from_np(v.dtype), kind="ExternalInput").ap()
           for k, v in arrays.items()}
    table = constants()
    const = {k: nc.dram_tensor(f"const_{k}", v.shape, mybir.dt.from_np(v.dtype), kind="ExternalInput").ap()
             for k, v in table.items()}
    outs = {k: nc.dram_tensor(f"out_{k}", list(s), F32, kind="ExternalOutput").ap() for k, s in OUTPUTS.items()}
    build(nc, ins, const, outs)
    fed = {f"in_{k}": v for k, v in arrays.items()} | {f"const_{k}": v for k, v in table.items()}
    r = run_bass_kernel_spmd(nc, [fed], core_ids=[0]).results[0]
    o = {k: r[f"out_{k}"] for k in OUTPUTS}

    def state(c):
        c = c.reshape(2, DK, -1, PAIRS, AUG).transpose(2, 3, 0, 1, 4).reshape(-1, H, DK, AUG)
        return c[None, ..., :DV], c[None, ..., DV]

    Cp, np_ = state(o["C_p"])
    Cs, ns = state(o["C_s"])
    m = o["m_out"].T
    return (o["y_prompt"].reshape(1, SEQ, D), o["y_sample"].reshape(BATCHES, STEPS, D),
            Cp, np_, m[None, 0:1], o["lat"][:SEQ][None], o["krope"][:SEQ][None],
            Cs, ns, m[None, 1:], o["lat"][SEQ:].reshape(BATCHES, STEPS, KVR),
            o["krope"][SEQ:].reshape(BATCHES, STEPS, ROPE))
```
